# Optimizing a Trainium2 kernel written in Bass

```python
import jax
import jax.numpy as jnp
from jax import lax
import numpy as np

D_MODEL = 2048
BATCH = 1
SEQ = 256
DEPTH = 2

MIX_WIDTH = D_MODEL
MLSTM_WIDTH = MIX_WIDTH // 2
MLSTM_HEADS = 4
MLSTM_DV = MLSTM_WIDTH // MLSTM_HEADS
MLSTM_DK = MLSTM_DV // 2
MLSTM_CHUNK = 64
POOL_WIDTH = MIX_WIDTH - MLSTM_WIDTH
POOL_WINDOWS = (2, 4, 8, 16)
POOL_GROUP = POOL_WIDTH // len(POOL_WINDOWS)
EVEN_SIZES = (MLSTM_HEADS * MLSTM_DK, MLSTM_HEADS * MLSTM_DK, MLSTM_WIDTH, MLSTM_WIDTH, MLSTM_HEADS, MLSTM_HEADS, POOL_WIDTH)
EVEN_IN = sum(EVEN_SIZES)

GLA_HEADS = 4
GLA_DK_TOTAL = D_MODEL // 2
GLA_DV_TOTAL = D_MODEL
GLA_DK = GLA_DK_TOTAL // GLA_HEADS
GLA_DV = GLA_DV_TOTAL // GLA_HEADS
GLA_GATE_RANK = 16
GLA_TAU = 16.0
GLA_CHUNK = 32
ODD_SIZES = (GLA_DK_TOTAL, GLA_DK_TOTAL, GLA_DV_TOTAL, GLA_DV_TOTAL, GLA_GATE_RANK)
ODD_IN = sum(ODD_SIZES)

PEER_KEYS = 128
PEER_EXPERTS = PEER_KEYS * PEER_KEYS
PEER_HEADS = 8
PEER_QDIM = 256
PEER_HALF = PEER_QDIM // 2
PEER_TOPK = 16
PEER_BLOCK = 128

N_EVEN = (DEPTH + 1) // 2
N_ODD = DEPTH // 2
EPS = 1e-6

kernel_name = 'hybrid_mlstm_pool_gla_peer'

def _split(z, sizes):
    return jnp.split(z, np.cumsum(sizes)[:-1].tolist(), axis=-1)

def rmsnorm(x, g):
    xf = x.astype(jnp.float32)
    y = xf * lax.rsqrt(jnp.mean(xf * xf, axis=-1, keepdims=True) + EPS)
    return (y * g.astype(jnp.float32)).astype(x.dtype)

def headnorm(x, g):
    H, d = x.shape[-2:]
    y = x * lax.rsqrt(jnp.mean(x * x, axis=-1, keepdims=True) + EPS)
    return y * g.astype(jnp.float32).reshape(H, d)

def _to_chunks(a, L):
    nc = a.shape[2] // L
    a = a.reshape(a.shape[:2] + (nc, L) + a.shape[3:])
    return jnp.moveaxis(a, 2, 0)

def _from_chunks(a):
    a = jnp.moveaxis(a, 0, 2)
    return a.reshape(a.shape[:2] + (a.shape[2] * a.shape[3],) + a.shape[4:])

def mlstm_chunkwise(q, k, v, i_pre, f_pre):
    f32 = jnp.float32
    B, H, S, DK = q.shape
    DV = v.shape[-1]
    L = MLSTM_CHUNK
    q = q.astype(f32)
    k = k.astype(f32) * (DK ** -0.5)
    v = v.astype(f32)
    ig = i_pre.astype(f32)
    lf = jax.nn.log_sigmoid(f_pre.astype(f32))
    causal = jnp.tril(jnp.ones((L, L), dtype=bool))

    def step(carry, inp):
        C, n, m = carry
        q_, k_, v_, i_, f_ = inp
        b = jnp.cumsum(f_, axis=-1)
        dmat = jnp.where(causal, b[..., :, None] - b[..., None, :] + i_[..., None, :], -jnp.inf)
        inter = b + m[..., None]
        m_t = jnp.maximum(jnp.max(dmat, axis=-1), inter)
        a_inter = jnp.exp(inter - m_t)
        s = jnp.einsum('bhtd,bhsd->bhts', q_, k_) * jnp.exp(dmat - m_t[..., None])
        num = jnp.einsum('bhts,bhsv->bhtv', s, v_) + a_inter[..., None] * jnp.einsum('bhvd,bhtd->bhtv', C, q_)
        den = jnp.sum(s, axis=-1) + a_inter * jnp.einsum('bhd,bhtd->bht', n, q_)
        h = num / jnp.maximum(jnp.abs(den), jnp.exp(-m_t))[..., None]
        bL = b[..., -1]
        dec = bL[..., None] - b + i_
        m_new = jnp.maximum(bL + m, jnp.max(dec, axis=-1))
        wk = jnp.exp(dec - m_new[..., None])
        sc = jnp.exp(bL + m - m_new)
        C_new = sc[..., None, None] * C + jnp.einsum('bhs,bhsv,bhsd->bhvd', wk, v_, k_)
        n_new = sc[..., None] * n + jnp.einsum('bhs,bhsd->bhd', wk, k_)
        return (C_new, n_new, m_new), h

    init = (jnp.zeros((B, H, DV, DK), f32), jnp.zeros((B, H, DK), f32), jnp.zeros((B, H), f32))
    xs = (_to_chunks(q, L), _to_chunks(k, L), _to_chunks(v, L), _to_chunks(ig, L), _to_chunks(lf, L))
    _, h = lax.scan(step, init, xs)
    return _from_chunks(h)

def multiscale_pool(p, w_pool, pool_scale):
    f32 = jnp.float32
    S = p.shape[1]
    pf = p.astype(f32)
    cs = jnp.pad(jnp.cumsum(pf, axis=1), ((0, 0), (1, 0), (0, 0)))
    t = jnp.arange(S)
    outs = []
    for g, w in enumerate(POOL_WINDOWS):
        sl = slice(g * POOL_GROUP, (g + 1) * POOL_GROUP)
        c = cs[..., sl]
        lo = jnp.maximum(t + 1 - w, 0)
        cnt = jnp.minimum(t + 1, w).astype(f32)
        mixed = (c[:, 1:] - c[:, lo]) / cnt[:, None] - pf[..., sl]
        outs.append(jnp.einsum('bsc,cd->bsd', mixed, w_pool[g].astype(f32)))
    y = jnp.concatenate(outs, axis=-1) * pool_scale.astype(f32)
    return y.astype(p.dtype)

def gla_chunkwise(q, k, v, log_a):
    f32 = jnp.float32
    B, H, S, DK = q.shape
    DV = v.shape[-1]
    L = GLA_CHUNK
    q = q.astype(f32) * (DK ** -0.5)
    k = k.astype(f32)
    v = v.astype(f32)
    la = log_a.astype(f32)
    causal = jnp.tril(jnp.ones((L, L), dtype=bool))

    def step(St, inp):
        q_, k_, v_, a_ = inp
        b = jnp.cumsum(a_, axis=-2)
        rel = jnp.where(causal[..., None], b[..., :, None, :] - b[..., None, :, :], -jnp.inf)
        att = jnp.einsum('bhtd,bhsd,bhtsd->bhts', q_, k_, jnp.exp(rel))
        o = jnp.einsum('bhts,bhsv->bhtv', att, v_) + jnp.einsum('bhtd,bhdv->bhtv', q_ * jnp.exp(b), St)
        bL = b[..., -1:, :]
        S_new = jnp.exp(bL[..., 0, :])[..., None] * St + jnp.einsum('bhsd,bhsv->bhdv', k_ * jnp.exp(bL - b), v_)
        return S_new, o

    xs = (_to_chunks(q, L), _to_chunks(k, L), _to_chunks(v, L), _to_chunks(la, L))
    _, o = lax.scan(step, jnp.zeros((B, H, DK, DV), f32), xs)
    return _from_chunks(o)

def even_mixer(h, w_in, b_igate, b_fgate, head_gain, w_pool, pool_scale, w_out):
    B, S, _ = h.shape
    H = MLSTM_HEADS
    z = h @ w_in
    q, k, v, o, ig, fg, p = _split(z, EVEN_SIZES)

    def heads(a, d):
        return a.reshape(B, S, H, d).transpose(0, 2, 1, 3)

    hm = mlstm_chunkwise(heads(q, MLSTM_DK), heads(k, MLSTM_DK), heads(v, MLSTM_DV),
                         (ig + b_igate).transpose(0, 2, 1), (fg + b_fgate).transpose(0, 2, 1))
    hm = headnorm(hm.transpose(0, 2, 1, 3), head_gain).reshape(B, S, MLSTM_WIDTH)
    hm = hm * jax.nn.sigmoid(o.astype(jnp.float32))
    hp = multiscale_pool(p, w_pool, pool_scale)
    y = jnp.concatenate([hm.astype(h.dtype), hp], axis=-1)
    return y @ w_out

def odd_mixer(h, w_in, w_gate, b_gate, head_gain, w_out):
    B, S, _ = h.shape
    H = GLA_HEADS
    z = h @ w_in
    q, k, v, r, gl = _split(z, ODD_SIZES)
    log_a = jax.nn.log_sigmoid((gl @ w_gate + b_gate).astype(jnp.float32)) / GLA_TAU

    def heads(a, d):
        return a.reshape(B, S, H, d).transpose(0, 2, 1, 3)

    o = gla_chunkwise(heads(q, GLA_DK), heads(k, GLA_DK), heads(v, GLA_DV), heads(log_a, GLA_DK))
    o = headnorm(o.transpose(0, 2, 1, 3), head_gain).reshape(B, S, GLA_DV_TOTAL)
    y = (o * jax.nn.silu(r.astype(jnp.float32))).astype(h.dtype)
    return y @ w_out

def peer_ffn(h, w_q, sub_keys, u_tab, v_tab):
    f32 = jnp.float32
    B, S, D = h.shape
    hb = h.reshape((B * S) // PEER_BLOCK, PEER_BLOCK, D)
    keys = sub_keys.astype(f32)

    def block(xb):
        T = xb.shape[0]
        q = (xb @ w_q).reshape(T, PEER_HEADS, 2, PEER_HALF).astype(f32)
        s = jnp.einsum('thpc,hpnc->thpn', q, keys)
        sv, si = lax.top_k(s, PEER_TOPK)
        cand = (sv[:, :, 0, :, None] + sv[:, :, 1, None, :]).reshape(T, PEER_HEADS, PEER_TOPK * PEER_TOPK)
        cv, ci = lax.top_k(cand, PEER_TOPK)
        e1 = jnp.take_along_axis(si[:, :, 0], ci // PEER_TOPK, axis=-1)
        e2 = jnp.take_along_axis(si[:, :, 1], ci % PEER_TOPK, axis=-1)
        eid = e1 * PEER_KEYS + e2
        g = jax.nn.softmax(cv, axis=-1)
        u = jnp.take(u_tab, eid, axis=0)
        a = jnp.einsum('td,thkd->thk', xb, u).astype(f32)
        coef = (g * jax.nn.gelu(a, approximate=False)).astype(xb.dtype)
        vv = jnp.take(v_tab, eid, axis=0)
        return jnp.einsum('thk,thkd->td', coef, vv)

    y = lax.map(block, hb)
    return y.reshape(B, S, D)

def setup_inputs(seed: int = 0) -> dict:
    key = jax.random.key(seed)
    ks = jax.random.split(key, 21)
    f32 = jnp.float32

    def nrm(k, shape, std):
        return jax.random.normal(k, shape, f32) * std

    def gain(k, shape):
        return 1.0 + 0.02 * jax.random.normal(k, shape, f32)

    return {
        'x': jax.random.normal(ks[0], (BATCH, SEQ, D_MODEL), f32),
        'e_norm': gain(ks[1], (N_EVEN, D_MODEL)),
        'e_w_in': nrm(ks[2], (N_EVEN, D_MODEL, EVEN_IN), D_MODEL ** -0.5),
        'e_b_igate': nrm(ks[3], (N_EVEN, MLSTM_HEADS), 0.1),
        'e_b_fgate': 3.0 + nrm(ks[4], (N_EVEN, MLSTM_HEADS), 0.5),
        'e_head_gain': gain(ks[5], (N_EVEN, MLSTM_WIDTH)),
        'e_w_pool': nrm(ks[6], (N_EVEN, len(POOL_WINDOWS), POOL_GROUP, POOL_GROUP), POOL_GROUP ** -0.5),
        'e_pool_scale': gain(ks[7], (N_EVEN, POOL_WIDTH)),
        'e_w_out': nrm(ks[8], (N_EVEN, MIX_WIDTH, D_MODEL), MIX_WIDTH ** -0.5),
        'o_norm': gain(ks[9], (N_ODD, D_MODEL)),
        'o_w_in': nrm(ks[10], (N_ODD, D_MODEL, ODD_IN), D_MODEL ** -0.5),
        'o_w_gate': nrm(ks[11], (N_ODD, GLA_GATE_RANK, GLA_DK_TOTAL), GLA_GATE_RANK ** -0.5),
        'o_b_gate': nrm(ks[12], (N_ODD, GLA_DK_TOTAL), 0.1),
        'o_head_gain': gain(ks[13], (N_ODD, GLA_DV_TOTAL)),
        'o_w_out': nrm(ks[14], (N_ODD, GLA_DV_TOTAL, D_MODEL), GLA_DV_TOTAL ** -0.5),
        'f_norm': gain(ks[15], (DEPTH, D_MODEL)),
        'f_w_q': nrm(ks[16], (DEPTH, D_MODEL, PEER_HEADS * PEER_QDIM), D_MODEL ** -0.5),
        'f_sub_keys': nrm(ks[17], (DEPTH, PEER_HEADS, 2, PEER_KEYS, PEER_HALF), PEER_HALF ** -0.5),
        'f_u': nrm(ks[18], (DEPTH, PEER_EXPERTS, D_MODEL), D_MODEL ** -0.5),
        'f_v': nrm(ks[19], (DEPTH, PEER_EXPERTS, D_MODEL), PEER_HEADS ** -0.5),
        'final_norm': gain(ks[20], (D_MODEL,)),
    }

def reference(x, e_norm, e_w_in, e_b_igate, e_b_fgate, e_head_gain, e_w_pool, e_pool_scale, e_w_out,
              o_norm, o_w_in, o_w_gate, o_b_gate, o_head_gain, o_w_out,
              f_norm, f_w_q, f_sub_keys, f_u, f_v, final_norm):
    for layer in range(DEPTH):
        j = layer // 2
        if layer % 2 == 0:
            x = x + even_mixer(rmsnorm(x, e_norm[j]), e_w_in[j], e_b_igate[j], e_b_fgate[j], e_head_gain[j],
                               e_w_pool[j], e_pool_scale[j], e_w_out[j])
        else:
            x = x + odd_mixer(rmsnorm(x, o_norm[j]), o_w_in[j], o_w_gate[j], o_b_gate[j], o_head_gain[j], o_w_out[j])
        x = x + peer_ffn(rmsnorm(x, f_norm[layer]), f_w_q[layer], f_sub_keys[layer], f_u[layer], f_v[layer])
    return rmsnorm(x, final_norm)


_drawn_inputs = setup_inputs


def setup_inputs(seed=0):
    import zlib

    import numpy as np

    out = dict(_drawn_inputs(seed))
    spreads = {}
    factors = {'e_b_igate': 200.0, 'o_head_gain': 28.488, 'final_norm': 23.652}
    for name, (base, spread) in spreads.items():
        noise = np.random.default_rng([zlib.crc32(name.encode()), seed]).standard_normal(out[name].shape)
        drawn = base * np.exp(spread * noise) if base else spread * noise
        out[name] = jnp.asarray(drawn.astype(out[name].dtype))
    for name, factor in factors.items():
        out[name] = (out[name] * factor).astype(out[name].dtype)
    return out
```

```python
from contextlib import ExitStack

import concourse.bass as bass
import numpy as np
from concourse import mybir

F32 = mybir.dt.float32
F32R = mybir.dt.float32r
U32 = mybir.dt.uint32
ALU = mybir.AluOpType
ACT = mybir.ActivationFunctionType
AX = mybir.AxisListType

P = 128
D = 2048
T = 256
TB = T // P
KB = D // P
EPS = 1e-6

M_HEADS, M_DK, M_DV = 4, 128, 256
M_WIDTH = M_HEADS * M_DV
POOL_WINDOWS = (2, 4, 8, 16)
POOL_GROUP = 256
G_HEADS, G_DK, G_DV = 4, 256, 512
G_RANK = 16
G_TAU = 16.0
G_SUB = 16

N_KEYS = 128
HEADS = 8
TOPK = 16
ITEMS = TB * HEADS
SLOTS = HEADS * TOPK

SLAB = 1024
RING = 4
NEG = -1e30

PHASES = [("qk", 0, 16), ("v", 0, 16), ("o", 0, 16), ("p", 0, 16), ("out", 0, 32), ("wq", 0, 32),
          ("u", 0, 256), ("vt", 0, 256),
          ("qk", 1, 32), ("v", 1, 32), ("r", 1, 32), ("out", 1, 32), ("wq", 1, 32),
          ("u", 1, 256), ("vt", 1, 256)]
SLAB0, _n = {}, 0
for _name, _layer, _k in PHASES:
    SLAB0[_name, _layer] = _n
    _n += _k
BLOCK0, _n = {}, 0
for _name, _layer, _k in PHASES:
    BLOCK0[_name, _layer] = _n
    if _name not in ("v", "vt"):
        _n += _k // 2
DENSE = [sum(k for n, l, k in PHASES if l == layer and n not in ("u", "vt")) for layer in range(2)]

XT, HT = 0, 4096
E_Q, E_K, E_V, E_SO = 8192, 9216, 10240, 12288
E_PAD, E_PW = 16, 16 + T
E_PT, E_S2, E_S4 = 14336, 16512, 18688
E_PE, E_MASK, E_WPOOL, E_ICNT, E_WG = 20864, 22400, 22912, 24960, 25984
E_ROWS, E_SEL = 26560, 28352
O_Q, O_K, O_V, O_R, O_B, O_KE, O_QE, O_ATT = 8192, 10240, 12288, 16384, 20480, 22528, 26624, 28672
O_WGATE, O_WGL, O_GLT = 26624, 27648, 27904
K_QS, K_TK, K_SC, K_KEYS = 20480, 20992, 24576, 30720


def decoder_kernel(nc, xT, dense0, dense1, u0, u1, v_tab, keys, gains, gates_in, w_pool, inv_count,
                   w_glow, w_gate, out):
    ctx = ExitStack()
    with ctx:
        def sb(name, shape, dt=F32):
            return ctx.enter_context(nc.sbuf_tensor(name, shape, dt))

        def S(name):
            return ctx.enter_context(nc.semaphore(name))

        spill = nc.dram_tensor("x_spill", (P, KB * T), F32).ap()

        big = sb("big", [P, 32768])
        act_hi_t = sb("act_hi_t", [P, KB, T], F32R)
        lo_base = nc.sbuf_base
        act_lo_t = sb("act_lo_t", [P, KB, T], F32R)
        onehot = nc.alloc_sbuf_tensor_at("onehot", [P, 2, 8, P], F32, offset=lo_base + 8 * 1024)
        ring_base = nc.sbuf_base
        w_raw = sb("w_raw", [P, RING, SLAB])
        w_lo = nc.alloc_sbuf_tensor_at("w_lo", [P, RING, SLAB], F32R, offset=ring_base)
        w_hi = sb("w_hi", [P, RING, SLAB], F32R)
        gain = sb("gain", [P, 128])
        gbias = sb("gbias", [P, 2])
        ones = sb("ones", [P, P])
        iota = sb("iota", [P, P])
        ident = sb("ident", [P, P])
        zrow = sb("zrow", [1, P])
        epst = sb("epst", [P, 1])
        credit = sb("credit", [1, 2])
        tri01 = sb("tri01", [P, T])
        stdv = sb("stdv", [P, T])
        rstd = sb("rstd", [P, T])
        e12 = sb("e12", [P, 2, ITEMS, TOPK])
        cv = sb("cv", [P, ITEMS, TOPK])
        csum = sb("csum", [P, ITEMS])
        jt = sb("jt", [P, 3, T])
        js = sb("js", [P, 3, 16])
        ps = ctx.enter_context(nc.psum_tensor("ps", [P, 8, 512], F32))

        s_x = [S(f"s_x{c}") for c in range(4)]
        s_landed = [S(f"s_landed{s}") for s in range(RING)]
        s_consts = S("s_consts")
        s_spill = S("s_spill")
        s_reload = S("s_reload")
        s_keys = S("s_keys")
        s_out = S("s_out")
        s_hi = S("s_hi")
        s_lo = S("s_lo")
        s_used = S("s_used")
        s_evac = S("s_evac")
        s_vevac = S("s_vevac")
        s_sq = S("s_sq")
        s_sum = S("s_sum")
        s_std = S("s_std")
        s_rstd = S("s_rstd")
        s_h = S("s_h")
        s_ahi = S("s_ahi")
        s_alo = S("s_alo")
        s_yadd = S("s_yadd")
        s_vec = S("s_vec")
        s_tk = S("s_tk")
        s_act = S("s_act")
        s_pool = S("s_pool")
        s_pool_turn = S("s_pool_turn")
        s_gates_ps = S("s_gates_ps")
        s_grow = S("s_grow")
        s_grow_act = S("s_grow_act")
        s_rows = S("s_rows")
        s_floor = S("s_floor")
        s_d_ps = S("s_d_ps")
        s_dm = S("s_dm")
        s_p = S("s_p")
        s_s_ps = S("s_s_ps")
        s_s = S("s_s")
        s_num_ps = S("s_num_ps")
        s_hn = S("s_hn")
        s_hsq = S("s_hsq")
        s_ssq_ps = S("s_ssq_ps")
        s_hstd = S("s_hstd")
        s_mixed = S("s_mixed")
        s_pool_ps = S("s_pool_ps")
        s_pool_out = S("s_pool_out")
        s_y = S("s_y")
        s_gl_ps = S("s_gl_ps")
        s_gl = S("s_gl")
        s_pre_ps = S("s_pre_ps")
        s_la = S("s_la")
        s_bias = S("s_bias")
        s_la_act = S("s_la_act")
        s_karg = S("s_karg")
        s_kexp = S("s_kexp")
        s_ke = S("s_ke")
        s_att_ps = S("s_att_ps")
        s_att = S("s_att")
        s_o_ps = S("s_o_ps")
        s_o = S("s_o")
        s_osq = S("s_osq")
        s_sc_ps = S("s_sc_ps")
        s_sc = S("s_sc")
        s_cvs = S("s_cvs")
        s_cexp = S("s_cexp")
        s_slots = S("s_slots")
        s_jt_ps = S("s_jt_ps")
        s_jt = S("s_jt")
        s_js = S("s_js")
        s_oh1 = S("s_oh1")
        s_oh2 = S("s_oh2")
        s_oh_free = S("s_oh_free")
        s_g = S("s_g")
        s_chi = S("s_chi")
        s_clo = S("s_clo")

        def at(o, n, k=None):
            a = big[:, o:o + n]
            return a if k is None else a.rearrange("p (k t) -> p k t", k=k)

        def bank(b, n=512, k=None):
            a = ps[:, b, 0:n]
            return a if k is None else a.rearrange("p (k t) -> p k t", k=k)

        def banks(b, nb):
            return ps[:, b:b + nb, :].rearrange("p b n -> p (b n)")

        G_NORM = [0, 16, 32, 48, 64]
        G_EH, G_PS, G_OH, G_BG = 80, 88, 96, 112
        N_CONSTS = 6
        POOL_CONSTS = 17
        WG_W = 36

        FILL = {("h", 0): 0, ("y", 0): 1, ("k", 0): 2, ("h", 1): 3, ("y", 1): 4, ("k", 1): 5}

        block = ctx.enter_context(nc.Block())

        @block.sync
        def _(sp):
            for c in range(4):
                sp.dma_start(at(XT + 1024 * c, 1024, 4), xT[:, 4 * c:4 * c + 4, :]).then_inc(s_x[c], 16)

            def load(slot, n, src, wait=True):
                if wait:
                    sp.wait_ge(s_used, n - (RING - 1))
                sp.dma_start(w_raw[:, slot, :], src).then_inc(s_landed[slot], 16)

            for layer, (dense, u) in enumerate(((dense0, u0), (dense1, u1))):
                n0 = SLAB0["qk", layer]
                if layer == 0:
                    for s in range(RING):
                        load(s, s, dense[s], wait=False)
                with sp.Fori(1 if layer == 0 else 0, DENSE[layer] // RING) as i:
                    for s in range(RING):
                        load(s, i * RING + (n0 + s), dense[bass.ds(i * RING + s, 1)].rearrange("a p n -> (a p) n"))
                n0 = SLAB0["u", layer]
                with sp.Fori(0, 2 * N_KEYS // RING) as i:
                    for s in range(RING):
                        load(s, i * RING + (n0 + s), u[bass.ds(i * RING + s, 1)].rearrange("a p n -> (a p) n"))
                n0 = SLAB0["vt", layer]
                vrows = v_tab[layer].rearrange("(e p) (h n) -> e p h n", p=P, h=2)
                with sp.Fori(0, 2 * N_KEYS // RING) as i:
                    for s in range(RING):
                        load(s, i * RING + (n0 + s),
                             vrows[bass.ds(i * 2 + s // 2, 1), :, s % 2, :].rearrange("a p n -> (a p) n"))
            for c in range(4):
                sp.wait_ge(s_h, 16 + c + 1)
                sp.dma_start(out[:, 4 * c:4 * c + 4, :], at(HT + 1024 * c, 1024, 4)).then_inc(s_out, 16)
            sp.wait_ge(s_out, 64)

        @block.gpsimd
        def _(pool):
            count = [0]

            def step(ins):
                ins.then_inc(s_pool, 1)
                count[0] += 1
                pool.wait_ge(s_pool, count[0])

            step(pool.memset(at(E_WG, 16 * WG_W), 0.0))
            pool.dma_start(gain[:, :], gains).then_inc(s_consts, 16)
            wg = at(E_WG, 16 * WG_W, 16)
            pool.dma_start(wg[:, :, 0:4], gates_in[:, 0:KB, 0:4]).then_inc(s_consts, 16)
            pool.dma_start(wg[:, :, 32:36], gates_in[:, 0:KB, 4:8]).then_inc(s_consts, 16)
            pool.dma_start(gbias[0:4, :], gates_in[0:4, KB, 0:2]).then_inc(s_consts, 16)
            pool.dma_start(at(E_WPOOL, 2048), w_pool).then_inc(s_consts, 16)
            pool.dma_start(at(E_ICNT, 1024), inv_count).then_inc(s_consts, 16)
            pool.dma_start(at(K_KEYS, 2048), keys[0]).then_inc(s_keys, 16)
            step(pool.memset(ones[:, :], 1.0))
            step(pool.memset(epst[:, :], EPS))
            step(pool.memset(zrow[:, :], 0.0))
            step(pool.memset(ident[:, :], 0.0))
            step(pool.affine_select(out=ident[:, :], in_=ident[:, :], compare_op=ALU.not_equal, fill=1.0,
                                    base=0, pattern=[[-1, P]], channel_multiplier=1))
            step(pool.iota(iota[:, :], pattern=[[1, P]], base=0, channel_multiplier=0,
                           allow_small_or_imprecise_dtypes=True))
            step(pool.memset(tri01[:, :], 1.0))
            step(pool.affine_select(out=tri01[:, 0:P], in_=tri01[:, 0:P], compare_op=ALU.is_ge, fill=0.0,
                                    base=0, pattern=[[1, P]], channel_multiplier=-1))
            step(pool.memset(at(E_MASK, 384), 0.0))
            for b in (0, 2):
                m = at(E_MASK + P * b, P)
                step(pool.affine_select(out=m, in_=m, compare_op=ALU.is_ge, fill=NEG, base=0,
                                        pattern=[[1, P]], channel_multiplier=-1))
            sel = big[0:4, E_SEL:E_SEL + 1024].rearrange("p (h t) -> p h t", h=4)
            step(pool.memset(sel, 0.0))
            step(pool.affine_select(out=sel, in_=sel, compare_op=ALU.not_equal, fill=1.0, base=0,
                                    pattern=[[-1, 4], [0, T]], channel_multiplier=1))
            for o in (E_PT, E_S2, E_S4):
                step(pool.memset(at(o, 8 * E_PW, 8)[:, :, 0:E_PAD], 0.0))
            assert count[0] == POOL_CONSTS, count[0]
            pool.memset(credit[:, :], 0.0).then_inc(s_oh_free, 8)
            pool.wait_ge(s_oh_free, 8)
            pool.memset(credit[:, :], 0.0).then_inc(s_g, 4)
            pool.wait_ge(s_g, 4)
            pool.memset(credit[:, :], 0.0).then_inc(s_sc, 1)
            pool.wait_ge(s_sc, 1)
            pool.memset(credit[:, :], 0.0).then_inc(s_sc_ps, 1)
            pool.wait_ge(s_sc_ps, 1)
            pool.memset(credit[:, :], 0.0).then_inc(s_oh2, 16)

            def tiles(o, j0, shift=0):
                return at(o, 8 * E_PW, 8)[:, j0:8, E_PAD - shift:E_PAD - shift + T]

            pool.wait_ge(s_evac, BLOCK0["out", 0])
            step(pool.tensor_tensor(tiles(E_S2, 0), tiles(E_PT, 0), tiles(E_PT, 0, 1), ALU.add))
            step(pool.tensor_tensor(tiles(E_S4, 2), tiles(E_S2, 2), tiles(E_S2, 2, 2), ALU.add))
            step(pool.tensor_tensor(tiles(E_S2, 4), tiles(E_S4, 4), tiles(E_S4, 4, 4), ALU.add))
            step(pool.tensor_tensor(tiles(E_S4, 6), tiles(E_S2, 6), tiles(E_S2, 6, 8), ALU.add))
            pool.wait_ge(s_consts, 16 * N_CONSTS)
            for g in range(4):
                src = at(E_S2 if g % 2 == 0 else E_S4, 8 * E_PW, 8)[:, 2 * g:2 * g + 2, E_PAD:E_PW]
                pt = at(E_PT, 8 * E_PW, 8)[:, 2 * g:2 * g + 2, E_PAD:E_PW]
                inv = at(E_ICNT + T * g, T).unsqueeze(1).broadcast_to([P, 2, T])
                step(pool.tensor_tensor(src, src, inv, ALU.mult))
                pool.tensor_tensor(pt, src, pt, ALU.subtract).then_inc(s_mixed, 1)

            for layer in range(2):
                pool.wait_ge(s_evac, BLOCK0["wq", layer])
                pool.dma_start(spill, at(XT, 4096)).then_inc(s_spill, 16)
                with pool.Fori(0, T // 16) as i:
                    pool.wait_ge(s_js, i + (16 * layer + 1))
                    for j in range(16):
                        pool.wait_ge(s_oh_free, i * 16 + (T * layer + j + 1))
                        pool.sem_inc(s_pool_turn, 1)
                        pool.tensor_scalar(onehot[:, 1, j % 8, :], iota[:, :], js[:, 1, j:j + 1], None,
                                           ALU.is_equal).then_inc(s_oh2, 1)
                pool.wait_ge(s_used, SLAB0["vt", layer] + 2 * KB)
                pool.wait_ge(s_spill, 16 * (layer + 1))
                pool.dma_start(at(XT, 4096), spill).then_inc(s_reload, 16)
                if layer == 0:
                    pool.wait_ge(s_used, SLAB0["qk", 1])
                    pool.dma_start(at(K_KEYS, 2048), keys[1]).then_inc(s_keys, 16)
                    pool.dma_start(big[0:G_RANK, O_WGATE:O_WGATE + 1024], w_gate).then_inc(s_consts, 16)
                    pool.dma_start(at(O_WGL, 256), w_glow).then_inc(s_consts, 16)

        @block.scalar
        def _(act):
            pending = [None]
            count = [0]

            def chain(ins):
                ins.then_inc(s_act, 1)
                count[0] += 1
                act.wait_ge(s_act, count[0])

            def hi(slot, n):
                act.wait_ge(s_landed[slot], (n // RING + 1) * 16 if isinstance(n, int) else (n - slot) * 4 + 16)
                act.activation(w_hi[:, slot, :], w_raw[:, slot, :], ACT.Copy).then_inc(s_hi, 1)

            def flush():
                if pending[0]:
                    pending[0]()
                    pending[0] = None

            def ahead(n0):
                hi(0, n0)
                hi(1, n0 + 1)
                flush()
                hi(2, n0 + 2)
                hi(3, n0 + 3)

            def stream(name, layer, nblocks, evac, after=None):
                n0 = SLAB0[name, layer]
                evac(0)
                if after:
                    after(-1)

                def turn(i):
                    hi(0, i * 4 + n0)
                    hi(1, i * 4 + (n0 + 1))
                    evac(i * 2 - 1)
                    if after:
                        after(i * 2 - 2)
                    hi(2, i * 4 + (n0 + 2))
                    hi(3, i * 4 + (n0 + 3))
                    evac(i * 2)
                    if after:
                        after(i * 2 - 1)
                with act.Fori(1, nblocks // 2) as i:
                    turn(i)

                def last():
                    evac(nblocks - 1)
                    if after:
                        after(nblocks - 2)
                        after(nblocks - 1)
                pending[0] = last

            def stream_only(name, layer, nslabs):
                n0 = SLAB0[name, layer]
                with act.Fori(1, nslabs // 4) as i:
                    for s in range(4):
                        hi(s, i * 4 + (n0 + s))

            def parity(b, first):
                return b % 2 if isinstance(b, int) else first

            def block_to(name, layer, o, func=ACT.Copy, width=T, skip=0, scale=1.0, hi_part=None):
                n0 = SLAB0[name, layer]
                turnwise = [0]

                def evac(b):
                    if isinstance(b, int):
                        par = b % 2
                        dst = at(o + skip + b * width, T)
                    else:
                        par = 1 - turnwise[0] % 2
                        turnwise[0] += 1
                        dst = big[:, bass.ds(b * width + (o + skip), T)]
                    act.wait_ge(s_used, b * 2 + (n0 + 2))
                    act.activation(dst, bank(par, T), func, scale=scale).then_inc(s_evac, 1)
                return evac

            def v_groups(layer, ngroups, o, row):
                n0 = SLAB0["v", layer]
                for g in range(ngroups):
                    if g:
                        hi(0, n0 + 8 * g)
                        hi(1, n0 + 8 * g + 1)
                        flush()
                        hi(2, n0 + 8 * g + 2)
                        hi(3, n0 + 8 * g + 3)
                    for s in range(4):
                        hi(s, n0 + 8 * g + 4 + s)

                    def evac(g=g):
                        act.wait_ge(s_used, n0 + 8 * g + 8)
                        for tb in range(TB):
                            act.activation(at(o + row * tb + 512 * g, 512), bank(3 + 2 * (g % 2) + tb),
                                           ACT.Copy).then_inc(s_vevac, 1)
                    pending[0] = evac

            def norm(k, fill, ready):
                for c in range(4):
                    ready(c)
                    act.activation(at(HT + 1024 * c, 1024), at(XT + 1024 * c, 1024), ACT.Square).then_inc(s_sq, 1)
                act.wait_ge(s_sum, k + 1)
                act.activation(stdv[:, :], bank(2, T), ACT.Sqrt, bias=epst[:, 0:1], scale=1.0 / D).then_inc(s_std, 1)
                if fill is not None:
                    act_hi(fill, s_h, 4 * k)

            def act_hi(fill, src, base):
                for c in range(4):
                    act.wait_ge(src, base + c + 1)
                    act.activation(act_hi_t[:, 4 * c:4 * c + 4, :], at(HT + 1024 * c, 1024, 4), ACT.Copy).then_inc(s_ahi, 1)

            def even():
                act.wait_ge(s_pool, POOL_CONSTS)
                norm(0, FILL["h", 0], lambda c: act.wait_ge(s_x[c], 16))
                ahead(SLAB0["qk", 0])

                stream("qk", 0, 8, block_to("qk", 0, E_Q))
                ahead(SLAB0["v", 0])
                rows = lambda r: big[0:4, E_ROWS + T * r:E_ROWS + T * (r + 1)]
                act.wait_ge(s_grow, 1)
                chain(act.activation(rows(2), rows(1), ACT.Exp, scale=-1.0))
                act.activation(rows(2), rows(2), ACT.Ln, bias=1.0).then_inc(s_grow_act, 1)
                act.wait_ge(s_rows, 1)
                act.activation(rows(5), rows(1), ACT.Exp, scale=-1.0).then_inc(s_floor, 1)
                v_groups(0, 2, E_V, 1024)
                ahead(SLAB0["o", 0])
                stream("o", 0, 8, block_to("o", 0, E_SO, func=ACT.Sigmoid))
                ahead(SLAB0["p", 0])
                stream("p", 0, 8, block_to("p", 0, E_PT, width=E_PW, skip=E_PAD))
                ahead(SLAB0["out", 0])
                for h in range(M_HEADS):
                    act.wait_ge(s_dm, h + 1)
                    act.activation(at(E_PE + 384 * h, 384), at(E_PE + 384 * h, 384), ACT.Exp).then_inc(s_p, 1)
                for h in range(M_HEADS):
                    act.wait_ge(s_hn, h + 1)
                    act.wait_ge(s_num_ps, M_HEADS)
                    act.activation(at(E_V + 512 * h, 512), at(HT + 512 * h, 512), ACT.Square).then_inc(s_hsq, 1)
                act.wait_ge(s_ssq_ps, 1)
                act.activation(at(E_PE, 1024), banks(3, 2), ACT.Sqrt, bias=epst[:, 0:1], scale=1.0 / M_DV).then_inc(s_hstd, 1)
                for j in range(8):
                    act.wait_ge(s_pool_ps, j // 2 * 2 + 2)
                    b = (0, 0, 1, 1, 5, 5, 6, 6)[j]
                    act.activation(at(HT + 2048 + T * j, T), ps[:, b, T * (j % 2):T * (j % 2) + T], ACT.Copy,
                                   scale=gain[:, G_PS + j:G_PS + j + 1]).then_inc(s_pool_out, 1)
                for c in range(4):
                    if c < 2:
                        act.wait_ge(s_y, c + 1)
                    else:
                        act.wait_ge(s_pool_out, 4 * (c - 1))
                    act.activation(act_hi_t[:, 4 * c:4 * c + 4, :], at(HT + 1024 * c, 1024, 4), ACT.Copy).then_inc(s_ahi, 1)
                stream_only("out", 0, 32)

            def odd():
                norm(2, FILL["h", 1], lambda c: act.wait_ge(s_yadd, c + 1))
                ahead(SLAB0["qk", 1])
                n0 = SLAB0["qk", 1]
                stream("qk", 1, 16, block_to("qk", 1, O_Q))
                ahead(SLAB0["v", 1])
                act.wait_ge(s_gl_ps, 1)
                act.activation(big[0:G_RANK, O_GLT:O_GLT + T], ps[0:G_RANK, 7, 0:T], ACT.Copy).then_inc(s_gl, 1)
                v_groups(1, 4, O_V, 2048)
                ahead(SLAB0["r", 1])
                act.wait_ge(s_la, 1)
                chain(act.activation(at(O_KE + 2048, 2048), at(O_KE + 2048, 2048), ACT.Exp, scale=-1.0))
                act.activation(at(O_KE + 2048, 2048), at(O_KE + 2048, 2048), ACT.Ln, bias=1.0).then_inc(s_la_act, 1)
                stream("r", 1, 16, block_to("r", 1, O_R, func=ACT.Silu))
                ahead(SLAB0["out", 1])
                act.wait_ge(s_karg, 1)
                act.activation(at(O_QE, 2048), at(O_QE, 2048), ACT.Exp, scale=1.0 / G_TAU).then_inc(s_kexp, 1)
                for g in range(T // G_SUB):
                    n = G_SUB * (g + 1)
                    ke = at(O_KE + 2048 * (g % 2), 2048, 8)[:, :, 0:n]
                    act.wait_ge(s_karg, g + 2)
                    act.activation(ke, ke, ACT.Exp, scale=-1.0 / G_TAU).then_inc(s_kexp, 1)
                for h in range(G_HEADS):
                    act.wait_ge(s_o_ps, h + 1)
                    act.activation(at(HT + 1024 * h, 1024), banks((3, 5)[h % 2], 2), ACT.Copy).then_inc(s_o, 1)
                    act.activation(at(O_KE + 1024 * h, 1024), banks((3, 5)[h % 2], 2), ACT.Square).then_inc(s_osq, 1)
                act.wait_ge(s_ssq_ps, 2)
                act.activation(at(O_B, 1024), banks(0, 2), ACT.Sqrt, bias=epst[:, 0:1], scale=1.0 / G_DV).then_inc(s_hstd, 1)
                act_hi(FILL["y", 1], s_y, 2)
                stream_only("out", 1, 32)

            def experts(layer):
                norm_ready = BLOCK0["out", layer]
                ahead(SLAB0["wq", layer])
                norm(2 * layer + 1, FILL["k", layer], lambda c: act.wait_ge(s_evac, norm_ready + 4 * c + 4))
                qbase = SLAB0["wq", layer]
                sc = at(K_SC, 4096).rearrange("p (b h c n) -> p b h c n", b=TB, h=HEADS, c=2)
                q_turn = [0]

                def q_evac(b):
                    if isinstance(b, int):
                        par = b % 2
                    else:
                        par = 1 - q_turn[0] % 2
                        q_turn[0] += 1
                    act.wait_ge(s_used, b * 2 + (qbase + 2))
                    if not (isinstance(b, int) and b < 2 and layer == 0):
                        act.wait_ge(s_sc_ps, b + 16 * layer)
                    act.activation(at(K_QS + T * par, T), bank(par, T), ACT.Copy).then_inc(s_evac, 1)

                s_turn = [0]

                def sc_save(q):
                    if isinstance(q, int):
                        if q < 0:
                            return
                        par, head = q % 2, q // 2
                        act.wait_ge(s_sc_ps, 16 * layer + q + 2)
                        act.activation(sc[:, :, head, par, :], bank(2 + par, T, TB), ACT.Copy).then_inc(s_sc, 1)
                    else:
                        par = s_turn[0] % 2
                        s_turn[0] += 1
                        act.wait_ge(s_sc_ps, q + (16 * layer + 2))
                        src = big[:, bass.ds(q * P + K_SC, 2048 + P)]
                        dst = src.rearrange("p (a n) -> p a n", n=P)[:, 0:17:16, :]
                        act.activation(dst, bank(2 + par, T, TB), ACT.Copy).then_inc(s_sc, 1)
                stream("wq", layer, 16, q_evac, after=sc_save)
                ahead(SLAB0["u", layer])

                ubase = SLAB0["u", layer]

                def ge(b, par, first=False):
                    act.wait_ge(s_used, b * 2 + (ubase + 2))
                    dst = at(b * T, T) if isinstance(b, int) else big[:, bass.ds(b * T, T)]
                    act.activation(dst, bank(par, T), ACT.Gelu).then_inc(s_evac, 1)

                act.wait_ge(s_spill, 16 * (layer + 1))
                ge(0, 0)
                for s in range(4):
                    hi(s, ubase + 4 + s)
                    if s % 2:
                        ge(s // 2 + 1, (s // 2 + 1) % 2)

                def u_turn(i):
                    for s in range(8):
                        hi(s % 4, i * 8 + (ubase + s))
                        if s % 2:
                            ge(i * 4 + (s // 2 - 1), (s // 2 + 1) % 2)
                with act.Fori(1, ITEMS) as i:
                    u_turn(i)
                act.wait_ge(s_cvs, layer + 1)
                act.activation(cv[:, :, :], cv[:, :, :], ACT.Exp).then_inc(s_cexp, 1)
                with act.Fori(ITEMS, N_KEYS // 4) as i:
                    u_turn(i)
                pending[0] = lambda: ge(N_KEYS - 1, 1)
                ahead(SLAB0["vt", layer])

                vbase = SLAB0["vt", layer]
                act.wait_ge(s_g, T // 4 * (layer + 1) + 4)

                def c_hi(i, b):
                    blk = i * 4 + b
                    if not (isinstance(i, int) and i == 0):
                        act.wait_ge(s_used, i * 8 + (vbase + 2 * b - 6))
                    src = at(blk * T, T) if isinstance(i, int) else big[:, bass.ds(i * 4 * T + b * T, T)]
                    act.activation(act_hi_t[:, b, :], src, ACT.Copy).then_inc(s_chi, 1)
                for b in range(4):
                    c_hi(0, b)
                for s in range(4):
                    hi(s, vbase + 4 + s)
                with act.Fori(1, N_KEYS // 4) as i:
                    for b in range(4):
                        c_hi(i, b)
                        for h in range(2):
                            s = 2 * b + h
                            hi(s % 4, i * 8 + (vbase + s))

            even()
            experts(0)
            odd()
            experts(1)
            norm(4, None, lambda c: act.wait_ge(s_yadd, 4 + c + 1))

        @block.vector
        def _(dve):
            count = [0]

            def chain(ins):
                ins.then_inc(s_vec, 1)
                count[0] = count[0] + 1
                dve.wait_ge(s_vec, count[0])

            def lo(slot, n):
                dve.wait_ge(s_hi, n + 1)
                dve.tensor_tensor(w_lo[:, slot, :], w_raw[:, slot, :], w_hi[:, slot, :].bitcast(F32),
                                  ALU.subtract).then_inc(s_lo, 1)

            def ahead(n0):
                for s in range(RING):
                    lo(s, n0 + s)

            def stream(name, layer, nslabs):
                n0 = SLAB0[name, layer]
                with dve.Fori(1, nslabs // RING) as i:
                    for s in range(RING):
                        lo(s, i * RING + (n0 + s))

            def v_groups(layer, ngroups, between=None):
                n0 = SLAB0["v", layer]
                for g in range(ngroups):
                    for s in range(8):
                        if g or s >= 4:
                            lo(s % 4, n0 + 8 * g + s)
                    if between and g in between:
                        between[g]()

            def residual(layer):
                n0 = SLAB0["out", layer]

                def add(b, par):
                    dve.wait_ge(s_used, b * 2 + (n0 + 2))
                    dst = at(XT + b * T, T) if isinstance(b, int) else big[:, bass.ds(b * T + XT, T)]
                    dve.tensor_tensor(dst, dst, bank(par, T), ALU.add).then_inc(s_evac, 1)
                add(0, 0)
                with dve.Fori(1, KB // 2) as i:
                    lo(0, i * 4 + n0)
                    lo(1, i * 4 + (n0 + 1))
                    add(i * 2 - 1, 1)
                    lo(2, i * 4 + (n0 + 2))
                    lo(3, i * 4 + (n0 + 3))
                    add(i * 2, 0)
                lo(0, n0 + 32)
                lo(1, n0 + 33)
                add(KB - 1, 1)
                lo(2, n0 + 34)
                lo(3, n0 + 35)

            def act_lo(fill):
                for c in range(4):
                    dve.wait_ge(s_ahi, 4 * fill + c + 1)
                    dve.tensor_tensor(act_lo_t[:, 4 * c:4 * c + 4, :], at(HT + 1024 * c, 1024, 4),
                                      act_hi_t[:, 4 * c:4 * c + 4, :].bitcast(F32), ALU.subtract).then_inc(s_alo, 1)

            def norm(k, fill):
                dve.wait_ge(s_std, k + 1)
                dve.reciprocal(rstd[:, :], stdv[:, :]).then_inc(s_rstd, 1)
                dve.wait_ge(s_rstd, k + 1)
                for j in range(KB):
                    ins = dve.scalar_tensor_tensor(out=at(HT + T * j, T), in0=at(XT + T * j, T),
                                                   scalar=gain[:, G_NORM[k] + j:G_NORM[k] + j + 1],
                                                   in1=rstd[:, :], op0=ALU.mult, op1=ALU.mult)
                    if j % 4 == 3:
                        ins.then_inc(s_h, 1)
                if fill is not None:
                    act_lo(fill)

            def head_norm(nheads, tiles_per_head, gcol, rr, silu, fill, done):
                chain(dve.reciprocal(at(rr, nheads * T), at(rr, nheads * T)))
                for c in range(nheads * tiles_per_head // 4):
                    for j in range(4 * c, 4 * c + 4):
                        h = j // tiles_per_head
                        ins = dve.scalar_tensor_tensor(out=at(HT + T * j, T), in0=at(HT + T * j, T),
                                                       scalar=gain[:, gcol + j:gcol + j + 1],
                                                       in1=at(rr + T * h, T), op0=ALU.mult, op1=ALU.mult)
                    chain(ins)
                    dve.tensor_tensor(at(HT + 1024 * c, 1024), at(HT + 1024 * c, 1024),
                                      at(silu + 1024 * c, 1024), ALU.mult).then_inc(s_y, 1)
                act_lo(fill)

            def even():
                dve.wait_ge(s_consts, 16 * N_CONSTS)
                dve.wait_ge(s_pool, POOL_CONSTS)
                norm(0, FILL["h", 0])
                ahead(SLAB0["qk", 0])
                stream("qk", 0, 16)
                ahead(SLAB0["v", 0])
                rows = lambda r: big[0:4, E_ROWS + T * r:E_ROWS + T * (r + 1)]
                dve.wait_ge(s_gates_ps, 1)
                chain(dve.tensor_scalar(rows(0), ps[0:4, 7, 0:T], gbias[0:4, 0:1], None, ALU.add))
                chain(dve.tensor_scalar(rows(3), ps[32:36, 7, 0:T], gbias[0:4, 1:2], None, ALU.add))
                dve.scalar_tensor_tensor(out=rows(1), in0=rows(3), scalar=-1.0, in1=rows(3), op0=ALU.mult,
                                         op1=ALU.max).then_inc(s_grow, 1)
                dve.wait_ge(s_grow_act, 1)
                chain(dve.scalar_tensor_tensor(out=rows(1), in0=rows(3), scalar=0.0, in1=rows(2),
                                               op0=ALU.min, op1=ALU.subtract))
                chain(dve.memset(rows(2), 0.0))
                chain(dve.tensor_tensor_scan(rows(3), rows(1), rows(2), 0.0, ALU.add, ALU.add))
                chain(dve.tensor_tensor(rows(4), rows(0), rows(3), ALU.subtract))
                chain(dve.tensor_tensor_scan(rows(0), rows(4), rows(4), 0.0, ALU.max, ALU.max))
                chain(dve.tensor_scalar(rows(2), rows(0), -1.0, None, ALU.mult))
                dve.tensor_tensor(rows(1), rows(0), rows(3), ALU.add).then_inc(s_rows, 1)
                v_groups(0, 2)
                ahead(SLAB0["o", 0])
                stream("o", 0, 16)
                ahead(SLAB0["p", 0])
                stream("p", 0, 16)
                ahead(SLAB0["out", 0])

                def masked(h):
                    dve.wait_ge(s_d_ps, h + 1)
                    dve.tensor_tensor(at(E_PE + 384 * h, 384), bank(3 + h % 2, 384), at(E_MASK, 384),
                                      ALU.add).then_inc(s_dm, 1)

                def weights(h):
                    dve.wait_ge(s_p, h + 1)
                    dve.wait_ge(s_s_ps, h + 1)
                    pe_h = at(E_PE + 384 * h, 384)
                    dve.scalar_tensor_tensor(out=pe_h, in0=bank(5 + h % 2, 384), scalar=M_DK ** -0.5, in1=pe_h,
                                             op0=ALU.mult, op1=ALU.mult).then_inc(s_s, 1)

                def output(h):
                    dve.wait_ge(s_num_ps, h + 1)
                    chain(dve.tensor_copy(stdv[:, :], ps[:, 2, 0:T]))
                    chain(dve.scalar_tensor_tensor(out=rstd[:, :], in0=stdv[:, :], scalar=-1.0, in1=stdv[:, :],
                                                   op0=ALU.mult, op1=ALU.max))
                    chain(dve.tensor_tensor(rstd[:, :], rstd[:, :], ps[:, 2, T:2 * T], ALU.max))
                    chain(dve.reciprocal(stdv[:, :], rstd[:, :]))
                    dve.tensor_tensor(at(HT + 512 * h, 512, 2), bank(7, 512, 2),
                                      stdv[:, :].unsqueeze(1).broadcast_to([P, 2, T]), ALU.mult).then_inc(s_hn, 1)
                for h in range(M_HEADS):
                    masked(h)
                    weights(h)
                    if h:
                        output(h - 1)
                output(M_HEADS - 1)
                dve.wait_ge(s_hstd, 1)
                head_norm(M_HEADS, 2, G_EH, E_PE, E_SO, FILL["y", 0], 0)
                residual(0)

            def odd():
                norm(2, FILL["h", 1])
                ahead(SLAB0["qk", 1])
                stream("qk", 1, 32)
                ahead(SLAB0["v", 1])

                def biased(r):
                    dve.wait_ge(s_pre_ps, r + 1)
                    for j in range(4 * r, 4 * r + 4):
                        b = 7 if j % 4 < 2 else 2
                        ins = dve.tensor_scalar(at(O_KE + T * j, T), ps[:, b, T * (j % 2):T * (j % 2) + T],
                                                gain[:, G_BG + j:G_BG + j + 1], None, ALU.add)
                    ins.then_inc(s_bias, 1)
                v_groups(1, 4, {1: lambda: biased(0), 2: lambda: biased(1)})
                ahead(SLAB0["r", 1])
                dve.wait_ge(s_bias, 2)
                dve.scalar_tensor_tensor(out=at(O_KE + 2048, 2048), in0=at(O_KE, 2048), scalar=-1.0,
                                         in1=at(O_KE, 2048), op0=ALU.mult, op1=ALU.max).then_inc(s_la, 1)
                chain(dve.memset(rstd[:, :], 0.0))
                dve.wait_ge(s_la_act, 1)
                chain(dve.scalar_tensor_tensor(out=at(O_KE, 2048), in0=at(O_KE, 2048), scalar=0.0,
                                               in1=at(O_KE + 2048, 2048), op0=ALU.min, op1=ALU.subtract))
                for j in range(8):
                    ins = dve.tensor_tensor_scan(at(O_B + T * j, T), at(O_KE + T * j, T), rstd[:, :], 0.0,
                                                 ALU.add, ALU.add)
                chain(ins)
                stream("r", 1, 32)
                ahead(SLAB0["out", 1])
                b3 = at(O_B, 2048).rearrange("p (g t) -> p g t", t=G_SUB)
                mid = G_SUB // 2 - 1
                dve.tensor_tensor(at(O_QE, 2048).rearrange("p (g t) -> p g t", t=G_SUB), b3,
                                  b3[:, :, mid:mid + 1].broadcast_to([P, 128, G_SUB]), ALU.subtract).then_inc(s_karg, 1)

                def k_arg(g):
                    n = G_SUB * (g + 1)
                    ref = G_SUB * g + mid
                    if g >= 2:
                        dve.wait_ge(s_att_ps, g - 1)
                    b8 = at(O_B, 2048, 8)
                    dve.tensor_tensor(at(O_KE + 2048 * (g % 2), 2048, 8)[:, :, 0:n], b8[:, :, 0:n],
                                      b8[:, :, ref:ref + 1].broadcast_to([P, 8, n]), ALU.subtract).then_inc(s_karg, 1)

                def k_mul(g):
                    n = G_SUB * (g + 1)
                    dve.wait_ge(s_kexp, g + 2)
                    ke = at(O_KE + 2048 * (g % 2), 2048, 8)[:, :, 0:n]
                    dve.tensor_tensor(ke, ke, at(O_K, 2048, 8)[:, :, 0:n], ALU.mult).then_inc(s_ke, 1)
                k_arg(0)
                dve.wait_ge(s_kexp, 1)
                dve.scalar_tensor_tensor(out=at(O_QE, 2048), in0=at(O_QE, 2048), scalar=G_DK ** -0.5,
                                         in1=at(O_Q, 2048), op0=ALU.mult, op1=ALU.mult).then_inc(s_ke, 1)
                for g in range(1, T // G_SUB):
                    k_arg(g)
                    k_mul(g - 1)
                k_mul(T // G_SUB - 1)
                dve.wait_ge(s_att_ps, T // G_SUB)
                for hp in range(2):
                    dve.tensor_tensor(at(O_ATT + 512 * hp, 512, 2), bank(3 + hp, 512, 2),
                                      tri01[:, :].unsqueeze(1).broadcast_to([P, 2, T]), ALU.mult).then_inc(s_att, 1)
                for hp in range(2):
                    dve.tensor_tensor(at(O_ATT + 1024 + 512 * hp, 512, 2)[:, :, P:T], bank(5 + hp, 512, 2)[:, :, P:T],
                                      tri01[:, 0:P].unsqueeze(1).broadcast_to([P, 2, P]), ALU.mult).then_inc(s_att, 1)
                dve.wait_ge(s_hstd, 2)
                head_norm(G_HEADS, 4, G_OH, O_B, O_R, FILL["y", 1], 2)
                residual(1)

            def tk(o, n, k=None):
                return at(K_TK + o, n, k)
            s0, s1 = tk(0, 256, 2), tk(256, 256, 2)
            c0, c1 = tk(512, 256), tk(768, 256)
            sv = tk(1024, 32, 2)
            si = tk(1056, 32).bitcast(U32).rearrange("p (c k) -> p c k", c=2)
            sif = tk(1088, 32)
            ci = tk(1120, 16).bitcast(U32)
            cij = tk(1136, 32).bitcast(U32)
            cijf = tk(1168, 32)
            tv = tk(1200, 16)
            pick = tk(1216, 512)

            tk_count = [0]

            def tk_chain(ins):
                ins.then_inc(s_tk, 1)
                tk_count[0] += 1
                dve.wait_ge(s_tk, tk_count[0])

            def topk_steps(i):
                src = at(K_SC + 256 * i, 256) if isinstance(i, int) else big[:, bass.ds(i * 256 + K_SC, 256)]
                yield lambda: tk_chain(dve.tensor_copy(tk(0, 256), src))
                for p in range(2):
                    yield lambda p=p: tk_chain(dve.max(sv[:, p, 0:8], s0[:, p, :]))
                    yield lambda p=p: tk_chain(dve.max_index(si[:, p, 0:8], sv[:, p, 0:8], s0[:, p, :]))
                    yield lambda p=p: tk_chain(dve.match_replace(s1[:, p, :], sv[:, p, 0:8], s0[:, p, :], NEG))
                    yield lambda p=p: tk_chain(dve.max(sv[:, p, 8:16], s1[:, p, :]))
                    yield lambda p=p: tk_chain(dve.max_index(si[:, p, 8:16], sv[:, p, 8:16], s1[:, p, :]))
                yield lambda: tk_chain(dve.tensor_tensor(
                    c0.rearrange("p (i j) -> p i j", i=TOPK),
                    sv[:, 0, :].unsqueeze(2).broadcast_to([P, TOPK, TOPK]),
                    sv[:, 1, :].unsqueeze(1).broadcast_to([P, TOPK, TOPK]), ALU.add))
                yield lambda: tk_chain(dve.max(tv[:, 0:8], c0))
                yield lambda: tk_chain(dve.max_index(ci[:, 0:8], tv[:, 0:8], c0))
                yield lambda: tk_chain(dve.match_replace(c1, tv[:, 0:8], c0, NEG))
                yield lambda: tk_chain(dve.max(tv[:, 8:16], c1))
                yield lambda: tk_chain(dve.max_index(ci[:, 8:16], tv[:, 8:16], c1))
                yield lambda: tk_chain(dve.tensor_scalar(cij[:, 0:16], ci, 4, None, ALU.logical_shift_right))
                yield lambda: tk_chain(dve.tensor_scalar(cij[:, 16:32], ci, 15, None, ALU.bitwise_and))
                yield lambda: tk_chain(dve.tensor_copy(cijf, cij))
                yield lambda: tk_chain(dve.tensor_copy(sif, tk(1056, 32).bitcast(U32)))
                yield lambda: tk_chain(dve.tensor_tensor(
                    pick.rearrange("p (a j) -> p a j", j=TOPK), cijf.unsqueeze(2).broadcast_to([P, 32, TOPK]),
                    iota[:, 0:TOPK].unsqueeze(1).broadcast_to([P, 32, TOPK]), ALU.is_equal))
                yield lambda: tk_chain(dve.tensor_tensor(
                    pick.rearrange("p (c k j) -> p c k j", c=2, j=TOPK),
                    pick.rearrange("p (c k j) -> p c k j", c=2, j=TOPK),
                    sif.rearrange("p (c j) -> p c j", c=2).unsqueeze(2).broadcast_to([P, 2, TOPK, TOPK]), ALU.mult))
                if isinstance(i, int):
                    de, dc = e12[:, :, i, :], cv[:, i, :]
                else:
                    de = e12[:, :, bass.ds(i, 1), :].rearrange("p c a k -> p c (a k)")
                    dc = cv[:, bass.ds(i, 1), :].rearrange("p a k -> p (a k)")
                yield lambda: tk_chain(dve.tensor_reduce(de, pick.rearrange("p (c k j) -> p c k j", c=2, j=TOPK), AX.X, ALU.add))
                yield lambda: tk_chain(dve.tensor_copy(dc, tv))

            def experts(layer):
                norm(2 * layer + 1, FILL["k", layer])
                stream("wq", layer, 32)
                ubase = SLAB0["u", layer]
                ahead(ubase)
                dve.wait_ge(s_sc, 16 * (layer + 1) + 1)

                def u_turn(i, slabs, with_topk):
                    steps = list(topk_steps(i)) if with_topk else []
                    if with_topk:
                        dve.sem_clear(s_tk)
                        tk_count[0] = 0
                    per = -(-len(steps) // len(slabs))
                    for s in slabs:
                        lo(s % 4, i * 8 + (ubase + s))
                        for _ in range(per):
                            if steps:
                                steps.pop(0)()
                u_turn(0, range(4, 8), True)
                with dve.Fori(1, ITEMS) as i:
                    u_turn(i, range(8), True)
                chain(dve.tensor_copy(csum[:, :], cv[:, :, 0:1].rearrange("p i k -> p (i k)")))
                dve.tensor_tensor(cv[:, :, :], cv[:, :, :], csum[:, :].unsqueeze(2).broadcast_to([P, ITEMS, TOPK]),
                                  ALU.subtract).then_inc(s_cvs, 1)
                lo(0, ubase + 8 * ITEMS)
                lo(1, ubase + 8 * ITEMS + 1)
                dve.wait_ge(s_cexp, layer + 1)
                chain(dve.tensor_reduce(csum[:, :], cv[:, :, :], AX.X, ALU.add))
                chain(dve.reciprocal(csum[:, :], csum[:, :]))
                dve.tensor_tensor(cv[:, :, :], cv[:, :, :], csum[:, :].unsqueeze(2).broadcast_to([P, ITEMS, TOPK]),
                                  ALU.mult).then_inc(s_slots, 1)
                for s in range(2, 8):
                    lo(s % 4, ubase + 8 * ITEMS + s)
                with dve.Fori(ITEMS + 1, N_KEYS // 4) as i:
                    u_turn(i, range(8), False)
                ahead(SLAB0["vt", layer])

                dve.wait_ge(s_jt_ps, layer + 1)
                chain(dve.tensor_copy(jt[:, 0:2, :].rearrange("p c t -> p (c t)"), bank(3)))
                chain(dve.tensor_copy(jt[:, 2, :], bank(4, T)))
                dve.wait_ge(s_evac, BLOCK0["u", layer] + N_KEYS)
                with dve.Fori(0, T // 16) as i:
                    tok = i * 16 + T * layer
                    dve.wait_ge(s_oh2, tok + 16)
                    dve.tensor_copy(js[:, :, :], jt[:, :, bass.ds(i * 16, 16)]).then_inc(s_js, 1)
                    dve.wait_ge(s_js, i + (16 * layer + 1))

                    def spread(g):
                        dve.wait_ge(s_oh_free, i * 16 + (T * layer + 4 * g + 4 + 8))
                        dst = big[:, :].rearrange("p (e t) -> p t e", t=T)[:, bass.ds(i * 16 + 4 * g, 4), :]
                        dve.tensor_tensor(dst, dst, bank(4 + g, 512, 4), ALU.mult).then_inc(s_g, 1)
                    for g in range(4):
                        for j in range(4 * g, 4 * g + 4):
                            dve.wait_ge(s_oh_free, i * 16 + (T * layer + j + 1))
                            dve.tensor_scalar(onehot[:, 0, j % 8, :], iota[:, :], js[:, 0, j:j + 1],
                                              js[:, 2, j:j + 1], ALU.is_equal, ALU.mult).then_inc(s_oh1, 1)
                        if g:
                            spread(g - 1)
                    spread(3)

                vbase = SLAB0["vt", layer]

                def c_lo(i, b):
                    dve.wait_ge(s_chi, i * 4 + (N_KEYS * layer + b + 1))
                    src = at(b * T, T) if isinstance(i, int) else big[:, bass.ds(i * 4 * T + b * T, T)]
                    dve.tensor_tensor(act_lo_t[:, b, :], src, act_hi_t[:, b, :].bitcast(F32),
                                      ALU.subtract).then_inc(s_clo, 1)
                for b in range(4):
                    c_lo(0, b)
                for s in range(4):
                    lo(s, vbase + 4 + s)
                with dve.Fori(1, N_KEYS // 4) as i:
                    for b in range(4):
                        c_lo(i, b)
                        for s in (2 * b, 2 * b + 1):
                            lo(s % 4, i * 8 + (vbase + s))
                dve.wait_ge(s_used, vbase + 2 * N_KEYS)
                dve.wait_ge(s_reload, 16 * (layer + 1))
                for c in range(4):
                    x = at(XT + 1024 * c, 1024)
                    dve.tensor_tensor(x, x, banks(2 * c, 2), ALU.add).then_inc(s_yadd, 1)

            even()
            experts(0)
            odd()
            experts(1)
            norm(4, None)

        @block.tensor
        def _(pe):
            def three(out, wh, wl, xh, xl, start=False, stop=False, **kw):
                pe.matmul(out, wh, xl, start=start, stop=False, **kw)
                pe.matmul(out, wl, xh, start=False, stop=False, **kw)
                return pe.matmul(out, wh, xh, start=False, stop=stop, **kw)

            def half_block(slot, n, b, half, fill=None):
                pe.wait_ge(s_lo, n + 1)
                for k in range(8):
                    kb = 8 * half + k
                    if fill is not None and kb % 4 == 0:
                        pe.wait_ge(s_alo, 4 * fill + kb // 4 + 1)
                    c = slice(P * k, P * (k + 1))
                    ins = three(ps[:, b, 0:T], w_hi[:, slot, c], w_lo[:, slot, c], act_hi_t[:, kb, :],
                                act_lo_t[:, kb, :], start=kb == 0, stop=kb == KB - 1)
                ins.then_inc(s_used, 1)

            def gemm(name, layer, nblocks, fill=None, between=None, strict=False):
                n0, b0 = SLAB0[name, layer], BLOCK0[name, layer]

                def blk(i, par, first=False):
                    if first and strict:
                        pe.wait_ge(s_evac, b0)
                    elif not (isinstance(i, int) and b0 + 2 * i + par < 2):
                        pe.wait_ge(s_evac, i * 2 + (b0 + par - 1))
                    for half in range(2):
                        s = 2 * par + half
                        half_block(s, i * 4 + (n0 + s), par, half, fill if first and par == 0 else None)
                blk(0, 0, True)
                blk(0, 1, True)
                if between:
                    between(0)
                with pe.Fori(1, nblocks // 2) as i:
                    blk(i, 0)
                    if between:
                        between(i * 2 - 1, 1)
                    blk(i, 1)
                    if between:
                        between(i * 2, 0)
                if between:
                    between(nblocks - 1)

            def v_groups(layer, ngroups, between=None):
                n0 = SLAB0["v", layer]
                for g in range(ngroups):
                    if g >= 2:
                        pe.wait_ge(s_vevac, 4 * layer + 2 * (g - 1))
                    for q in range(8):
                        pe.wait_ge(s_lo, n0 + 8 * g + q + 1)
                        for k in range(2):
                            kb = 2 * q + k
                            c = slice(512 * k, 512 * (k + 1))
                            for tb in range(TB):
                                t = slice(P * tb, P * (tb + 1))
                                out = ps[:, 3 + 2 * (g % 2) + tb, :]
                                pe.matmul(out, act_lo_t[:, kb, t], w_hi[:, q % 4, c], start=kb == 0, stop=False)
                                pe.matmul(out, act_hi_t[:, kb, t], w_lo[:, q % 4, c], start=False, stop=False)
                                ins = pe.matmul(out, act_hi_t[:, kb, t], w_hi[:, q % 4, c], start=False,
                                                stop=kb == KB - 1)
                        ins.then_inc(s_used, 1)
                    if between and g in between:
                        between[g]()

            def norm_sum(k):
                if k in (2, 4):
                    pe.wait_ge(s_yadd, 2 * k - 2)
                for j in range(KB):
                    if j % 4 == 0:
                        pe.wait_ge(s_sq, 4 * k + j // 4 + 1)
                    ins = pe.matmul(ps[:, 2, 0:T], ones[:, :], at(HT + T * j, T), start=j == 0, stop=j == KB - 1)
                ins.then_inc(s_sum, 1)

            def even():
                pe.wait_ge(s_pool, POOL_CONSTS)
                pe.wait_ge(s_consts, 16 * N_CONSTS)
                norm_sum(0)
                gemm("qk", 0, 8, fill=FILL["h", 0])
                wg = at(E_WG, 16 * WG_W, 16)
                for j in range(KB):
                    ins = pe.matmul(ps[0:WG_W, 7, 0:T], wg[:, j, :], at(HT + T * j, T), start=j == 0, stop=j == KB - 1)
                ins.then_inc(s_gates_ps, 1)
                v_groups(0, 2)
                gemm("o", 0, 8)
                gemm("p", 0, 8)
                sel = big[0:4, E_SEL:E_SEL + 1024].rearrange("p (h t) -> p h t", h=4)
                rows = lambda r: big[0:4, E_ROWS + T * r:E_ROWS + T * (r + 1)]

                def scores(h):
                    if h == 0:
                        pe.wait_ge(s_rows, 1)
                        pe.wait_ge(s_vevac, 4)
                        pe.wait_ge(s_evac, BLOCK0["out", 0])
                    if h >= 2:
                        pe.wait_ge(s_dm, h - 1)
                    for o, s, t0 in ((0, 0, 0), (T, P, P)):
                        out = ps[:, 3 + h % 2, o:o + T - t0]
                        pe.matmul(out, sel[:, h, 0:P], rows(2)[:, t0:T], start=True, stop=False)
                        ins = pe.matmul(out, rows(4)[:, s:s + P], sel[:, h, t0:T], start=False, stop=True)
                    ins.then_inc(s_d_ps, 1)
                    if h >= 2:
                        pe.wait_ge(s_s, h - 1)
                    for o, s, t0 in ((0, 0, 0), (T, P, P)):
                        ins = pe.matmul(ps[:, 5 + h % 2, o:o + T - t0], at(E_K + T * h + s, P),
                                        at(E_Q + T * h + t0, T - t0), start=True, stop=True)
                    ins.then_inc(s_s_ps, 1)

                def outputs(h):
                    if h == 0:
                        pe.wait_ge(s_floor, 1)
                    else:
                        pe.wait_ge(s_hn, h)
                    pe.wait_ge(s_s, h + 1)
                    w = at(E_PE + 384 * h, 384)
                    for vt in range(2):
                        v = [at(E_V + 1024 * sb_ + 256 * h + P * vt, P) for sb_ in range(2)]
                        pe.matmul(ps[:, 7, T * vt:T * vt + T], v[0], w[:, 0:T], start=True, stop=True)
                        pe.matmul(ps[:, 7, T * vt + P:T * vt + T], v[1], w[:, T:384], start=False, stop=False,
                                  skip_group_check=True)
                    pe.matmul(ps[:, 2, 0:T], ones[:, :], w[:, 0:T], start=True, stop=True)
                    pe.matmul(ps[:, 2, P:T], ones[:, :], w[:, T:384], start=False, stop=False, skip_group_check=True)
                    pe.matmul(ps[:, 2, T:2 * T], sel[:, h, 0:P], rows(5), start=True, stop=True).then_inc(s_num_ps, 1)
                for h in range(M_HEADS):
                    scores(h)
                    if h:
                        outputs(h - 1)
                outputs(M_HEADS - 1)
                for h in range(M_HEADS):
                    pe.wait_ge(s_hsq, h + 1)
                    for vt in range(2):
                        ins = pe.matmul(ps[:, 3 + h // 2, T * (h % 2):T * (h % 2) + T], ones[:, :],
                                        at(E_V + 512 * h + T * vt, T), start=vt == 0, stop=vt == 1)
                ins.then_inc(s_ssq_ps, 1)
                pe.wait_ge(s_s, M_HEADS)
                for j in range(8):
                    g, dt = j // 2, j % 2
                    pe.wait_ge(s_mixed, g + 1)
                    b = (0, 0, 1, 1, 5, 5, 6, 6)[j]
                    for kc in range(2):
                        ins = pe.matmul(ps[:, b, T * (j % 2):T * (j % 2) + T],
                                        at(E_WPOOL + 512 * g + 256 * kc + P * dt, P),
                                        at(E_PT + E_PW * (2 * g + kc) + E_PAD, T), start=kc == 0, stop=kc == 1)
                    ins.then_inc(s_pool_ps, 1)
                pe.wait_ge(s_pool_out, 8)
                gemm("out", 0, 16, fill=FILL["y", 0], strict=True)

            def odd():
                norm_sum(2)
                gemm("qk", 1, 16, fill=FILL["h", 1])
                pe.wait_ge(s_consts, 16 * (N_CONSTS + 2))
                for j in range(KB):
                    ins = pe.matmul(ps[0:G_RANK, 7, 0:T], at(O_WGL + G_RANK * j, G_RANK), at(HT + T * j, T),
                                    start=j == 0, stop=j == KB - 1)
                ins.then_inc(s_gl_ps, 1)

                def gate(r):
                    pe.wait_ge(s_gl, 1)
                    if r:
                        pe.wait_ge(s_bias, 1)
                    for j in range(4 * r, 4 * r + 4):
                        b = 7 if j % 4 < 2 else 2
                        ins = pe.matmul(ps[:, b, T * (j % 2):T * (j % 2) + T],
                                        big[0:G_RANK, O_WGATE + P * j:O_WGATE + P * (j + 1)],
                                        big[0:G_RANK, O_GLT:O_GLT + T], start=True, stop=True)
                    ins.then_inc(s_pre_ps, 1)
                v_groups(1, 4, {0: lambda: gate(0), 1: lambda: gate(1)})
                gemm("r", 1, 16)
                pe.wait_ge(s_vevac, 12)
                for b in range(3, 7):
                    for o in range(0, 512, P):
                        pe.matmul(ps[:, b, o:o + P], zrow[0:1, :], zrow[0:1, :], start=True, stop=True)
                for g in range(T // G_SUB):
                    n = G_SUB * (g + 1)
                    pe.wait_ge(s_ke, g + 2)
                    ke = at(O_KE + 2048 * (g % 2), 2048, 8)
                    qe = at(O_QE, 2048, 8)
                    for h in range(G_HEADS):
                        for sb_ in range((n + P - 1) // P):
                            m = min(n - P * sb_, P)
                            c = T * (h % 2) + G_SUB * g
                            for j in (2 * h, 2 * h + 1):
                                ins = pe.matmul(ps[0:m, 3 + 2 * sb_ + h // 2, c:c + G_SUB],
                                                ke[:, j, P * sb_:P * sb_ + m], qe[:, j, G_SUB * g:n],
                                                start=j % 2 == 0, stop=j % 2 == 1)
                    ins.then_inc(s_att_ps, 1)
                for h in range(G_HEADS):
                    if h == 0:
                        pe.wait_ge(s_att, 4)
                    elif h >= 2:
                        pe.wait_ge(s_osq, h - 1)
                    for vt in range(4):
                        b, o = (3, 5)[h % 2] + vt // 2, T * (vt % 2)
                        v = [at(O_V + 2048 * sb_ + 512 * h + P * vt, P) for sb_ in range(2)]
                        w = [at(O_ATT + 1024 * sb_ + T * h, T) for sb_ in range(2)]
                        pe.matmul(ps[:, b, o:o + T], v[0], w[0], start=True, stop=True)
                        ins = pe.matmul(ps[:, b, o + P:o + T], v[1], w[1][:, P:T], start=False, stop=False,
                                        skip_group_check=True)
                    ins.then_inc(s_o_ps, 1)
                pe.wait_ge(s_evac, BLOCK0["out", 1])
                for h in range(G_HEADS):
                    pe.wait_ge(s_osq, h + 1)
                    for vt in range(4):
                        ins = pe.matmul(ps[:, h // 2, T * (h % 2):T * (h % 2) + T], ones[:, :],
                                        at(O_KE + 1024 * h + T * vt, T), start=vt == 0, stop=vt == 3)
                ins.then_inc(s_ssq_ps, 1)
                pe.wait_ge(s_hstd, 2)
                gemm("out", 1, 16, fill=FILL["y", 1], strict=True)

            def experts(layer):
                norm_sum(2 * layer + 1)
                pe.wait_ge(s_keys, 16 * (layer + 1))

                def key_scores(q, par=None):
                    par = q % 2 if par is None else par
                    pe.wait_ge(s_evac, q + (BLOCK0["wq", layer] + 1))
                    if not (isinstance(q, int) and q < 2):
                        pe.wait_ge(s_sc, q + 16 * layer)
                    rhs = at(K_KEYS + P * q, P) if isinstance(q, int) else big[:, bass.ds(q * P + K_KEYS, P)]
                    for tb in range(TB):
                        ins = pe.matmul(ps[:, 2 + par, P * tb:P * (tb + 1)], at(K_QS + T * par + P * tb, P), rhs,
                                        start=True, stop=True)
                    ins.then_inc(s_sc_ps, 1)
                gemm("wq", layer, 16, fill=FILL["k", layer], between=key_scores, strict=True)

                ub, u0_ = BLOCK0["u", layer], SLAB0["u", layer]
                with pe.Fori(0, N_KEYS // 4) as i:
                    for b in range(4):
                        pe.wait_ge(s_evac, i * 4 + (ub + b - 1))
                        for half in range(2):
                            s = 2 * b + half
                            half_block(s % 4, i * 8 + (u0_ + s), b % 2, half)
                pe.wait_ge(s_slots, layer + 1)
                for c in range(2):
                    for tb in range(TB):
                        pe.transpose(ps[:, 3, T * c + P * tb:T * c + P * (tb + 1)],
                                     e12[:, c, HEADS * tb:HEADS * (tb + 1), :].rearrange("p h k -> p (h k)"), ident[:, :])
                for tb in range(TB):
                    ins = pe.transpose(ps[:, 4, P * tb:P * (tb + 1)],
                                       cv[:, HEADS * tb:HEADS * (tb + 1), :].rearrange("p h k -> p (h k)"), ident[:, :])
                ins.then_inc(s_jt_ps, 1)
                with pe.Fori(0, T // 16) as i:
                    for j in range(16):
                        if j % 4 == 0:
                            pe.wait_ge(s_g, i * 4 + (T // 4 * layer + j // 4 + 1))
                        pe.wait_ge(s_oh1, i * 16 + (T * layer + j + 1))
                        pe.wait_ge(s_oh2, i * 16 + (T * layer + j + 17))
                        pe.matmul(ps[:, 4 + j // 4, P * (j % 4):P * (j % 4) + P], onehot[:, 1, j % 8, :],
                                  onehot[:, 0, j % 8, :], start=True, stop=True).then_inc(s_oh_free, 1)
                pe.wait_ge(s_g, T // 4 * (layer + 1) + 4)
                for b in range(8):
                    pe.matmul(ps[:, b, 0:2], zrow[0:1, :], zrow[0:1, 0:2], start=True, stop=False, skip_group_check=True)
                v0 = SLAB0["vt", layer]
                with pe.Fori(0, N_KEYS // 4) as i:
                    for b in range(4):
                        pe.wait_ge(s_clo, i * 4 + (N_KEYS * layer + b + 1))
                        for half in range(2):
                            s = 2 * b + half
                            pe.wait_ge(s_lo, i * 8 + (v0 + s + 1))
                            for k in range(8):
                                j = 8 * half + k
                                c = slice(P * k, P * (k + 1))
                                ins = three(ps[:, j // 2, T * (j % 2):T * (j % 2) + T], w_hi[:, s % 4, c],
                                            w_lo[:, s % 4, c], act_hi_t[:, b, :], act_lo_t[:, b, :],
                                            skip_group_check=True)
                            ins.then_inc(s_used, 1)

            even()
            experts(0)
            odd()
            experts(1)
            norm_sum(4)


INPUTS = ["xT", "dense0", "dense1", "u0", "u1", "v_tab", "keys", "gains", "gates_in", "w_pool", "inv_count",
          "w_glow", "w_gate"]


def lay_out(x, e_norm, e_w_in, e_b_igate, e_b_fgate, e_head_gain, e_w_pool, e_pool_scale, e_w_out,
            o_norm, o_w_in, o_w_gate, o_b_gate, o_head_gain, o_w_out,
            f_norm, f_w_q, f_sub_keys, f_u, f_v, final_norm):
    def blocks(w):
        n = w.shape[1] // P
        return w.reshape(2, 8, P, n, P).transpose(3, 0, 2, 1, 4).reshape(2 * n, P, SLAB)

    def groups(w):
        n = w.shape[1] // 512
        return w.reshape(8, 2, P, n, 512).transpose(3, 0, 2, 1, 4).reshape(8 * n, P, SLAB)

    def table(u):
        return u.reshape(N_KEYS, P, 2, 8, P).transpose(0, 2, 4, 3, 1).reshape(2 * N_KEYS, P, SLAB)

    def column(g):
        return g.reshape(-1, P).T

    a = np.ascontiguousarray
    we, wo = e_w_in[0], o_w_in[0]
    dense0 = np.concatenate([blocks(we[:, 0:1024]), groups(we[:, 1024:2048]), blocks(we[:, 2048:3072]),
                             blocks(we[:, 3080:4104]), blocks(e_w_out[0]), blocks(f_w_q[0])])
    dense1 = np.concatenate([blocks(wo[:, 0:2048]), groups(wo[:, 2048:4096]), blocks(wo[:, 4096:6144]),
                             blocks(o_w_out[0]), blocks(f_w_q[1])])
    gains = np.concatenate([column(g) for g in (e_norm[0], f_norm[0], o_norm[0], f_norm[1], final_norm,
                                                e_head_gain[0], e_pool_scale[0], o_head_gain[0], o_b_gate[0])], 1)
    gains = np.concatenate([gains, np.zeros((P, P - gains.shape[1]), gains.dtype)], 1)
    gates = np.zeros((P, KB + 1, 8), we.dtype)
    gates[:, 0:KB, :] = we[:, 3072:3080].reshape(KB, P, 8).transpose(1, 0, 2)
    gates[0:4, KB, 0] = e_b_igate[0]
    gates[0:4, KB, 1] = e_b_fgate[0]
    inv = np.stack([1.0 / np.minimum(np.arange(1, T + 1), w) for w in POOL_WINDOWS]).astype(np.float32)
    return {
        "xT": a(x[0].T.reshape(KB, P, T).transpose(1, 0, 2)),
        "dense0": a(dense0), "dense1": a(dense1), "u0": a(table(f_u[0])), "u1": a(table(f_u[1])),
        "v_tab": a(f_v), "keys": a(f_sub_keys.transpose(0, 4, 1, 2, 3).reshape(2, P, 2048)),
        "gains": a(gains), "gates_in": gates,
        "w_pool": a(e_w_pool[0].reshape(4, 2, P, POOL_GROUP).transpose(2, 0, 1, 3).reshape(P, 2048)),
        "inv_count": a(np.broadcast_to(inv.reshape(1, 1024), (P, 1024))),
        "w_glow": a(wo[:, 6144:6160].reshape(KB, P, G_RANK).transpose(1, 0, 2).reshape(P, KB * G_RANK)),
        "w_gate": a(o_w_gate[0]),
    }


def kernel(**inputs):
    import concourse.bacc as bacc
    from concourse.bass_utils import run_bass_kernel_spmd as run
    arrays = lay_out(**{k: np.asarray(v) for k, v in inputs.items()})
    nc = bacc.Bacc("TRN2", target_bir_lowering=False, num_devices=1)
    args = [nc.dram_tensor(f"in_{n}", arrays[n].shape, F32, kind="ExternalInput").ap() for n in INPUTS]
    out = nc.dram_tensor("out_0", (P, KB, T), F32, kind="ExternalOutput").ap()
    decoder_kernel(nc, *args, out)
    r = run(nc, [{f"in_{n}": arrays[n] for n in INPUTS}], core_ids=[0])
    got = np.asarray(r.results[0]["out_0"])
    return np.ascontiguousarray(got.transpose(2, 1, 0).reshape(1, T, D))
```

```python
from contextlib import ExitStack

import concourse.bass as bass
import numpy as np
from concourse import mybir

F32 = mybir.dt.float32
F32R = mybir.dt.float32r
BF16 = mybir.dt.bfloat16
U32 = mybir.dt.uint32
ALU = mybir.AluOpType
ACT = mybir.ActivationFunctionType
AX = mybir.AxisListType

P = 128
D = 2048
T = 256
TB = T // P
KB = D // P
EPS = 1e-6

M_HEADS, M_DK, M_DV = 4, 128, 256
M_WIDTH = M_HEADS * M_DV
POOL_WINDOWS = (2, 4, 8, 16)
POOL_GROUP = 256
G_HEADS, G_DK, G_DV = 4, 256, 512
G_RANK = 16
G_TAU = 16.0
G_SUB = 16

N_KEYS = 128
HEADS = 8
TOPK = 16
ITEMS = TB * HEADS
PARTS = 2
HALF = N_KEYS // PARTS
SC_TOKENS = 32
SC_TURNS = T // SC_TOKENS
WPARTS = 3
SC_FIRST = HALF // 4 + 1
COEFFS = 2 * HALF + (N_KEYS - HALF)

SLAB = 1024
RING = 4
NEG = -1e30

PHASES = [("qk", 0, 16), ("v", 0, 16), ("o", 0, 16), ("p", 0, 16), ("out", 0, 32), ("wq", 0, 32),
          ("u", 0, 256), ("vt", 0, 256),
          ("qk", 1, 32), ("v", 1, 32), ("r", 1, 32), ("out", 1, 32), ("wq", 1, 32),
          ("u", 1, 256), ("vt", 1, 256)]
SLAB0, _n = {}, 0
for _name, _layer, _k in PHASES:
    SLAB0[_name, _layer] = _n
    _n += _k
BLOCK0, _n = {}, 0
for _name, _layer, _k in PHASES:
    BLOCK0[_name, _layer] = _n
    if _name not in ("v", "vt"):
        _n += _k // 2
DENSE = [sum(k for n, l, k in PHASES if l == layer and n not in ("u", "vt")) for layer in range(2)]

XT, HT = 0, 4096
E_Q, E_K, E_V, E_SO = 8192, 9216, 10240, 12288
E_PAD, E_PW = 16, 16 + T
E_PT, E_S2, E_S4 = 14336, 16512, 18688
E_PE, E_MASK, E_WPOOL, E_ICNT, E_WG = 20864, 22400, 22912, 24960, 25984
E_ROWS, E_SEL = 26560, 28352
O_Q, O_K, O_V, O_R, O_B, O_KE, O_QE, O_ATT = 8192, 10240, 12288, 16384, 20480, 22528, 26624, 28672
O_KX, O_QX = O_KE + 2048, O_KE + 3072
O_WGATE, O_WGL, O_GLT = 26624, 27648, 27904
K_QS, K_TK, K_SC, K_KEYS = 20480, 20992, 24576, 30720


def decoder_kernel(nc, xT, dense0, dense1, u0, u1, v_tab, keys, gains, gates_in, w_pool, inv_count,
                   w_glow, w_gate, out):
    ctx = ExitStack()
    with ctx:
        def sb(name, shape, dt=F32):
            return ctx.enter_context(nc.sbuf_tensor(name, shape, dt))

        def S(name):
            return ctx.enter_context(nc.semaphore(name))

        spill = nc.dram_tensor("x_spill", (P, KB * T), F32).ap()

        big = sb("big", [P, 32768])
        act_hi_t = sb("act_hi_t", [P, KB, T], F32R)
        act_lo_t = sb("act_lo_t", [P, KB, T], F32R)
        ring_base = nc.sbuf_base
        w_raw = sb("w_raw", [P, RING, SLAB])
        w_lo = nc.alloc_sbuf_tensor_at("w_lo", [P, RING, SLAB], F32R, offset=ring_base)
        w_hi = sb("w_hi", [P, RING, SLAB], F32R)
        gain = sb("gain", [P, 128])
        gbias = sb("gbias", [P, 2])
        ones = sb("ones", [P, P])
        iota = sb("iota", [P, P])
        ident = sb("ident", [P, P])
        zrow = sb("zrow", [1, P])
        epst = sb("epst", [P, 1])
        credit = sb("credit", [1, 2])
        tri01 = sb("tri01", [P, T])
        stdv_base = nc.sbuf_base
        stdv = sb("stdv", [P, T])
        key1 = nc.alloc_sbuf_tensor_at("key1", [P, 8, HALF], BF16, offset=stdv_base)
        rstd = sb("rstd", [P, T])
        e12_base = nc.sbuf_base
        e12 = sb("e12", [P, 2, ITEMS, TOPK])
        cv = sb("cv", [P, ITEMS, TOPK])
        hot1 = nc.alloc_sbuf_tensor_at("hot1", [P, 8, WPARTS, HALF], BF16, offset=e12_base)
        hot2 = sb("hot2", [P, 8, P], BF16)
        csum = sb("csum", [P, ITEMS])
        jt = sb("jt", [P, 2, T])
        jw = sb("jw", [P, WPARTS, T], BF16)
        ps = ctx.enter_context(nc.psum_tensor("ps", [P, 8, 512], F32))

        s_x = [S(f"s_x{c}") for c in range(4)]
        s_landed = [S(f"s_landed{s}") for s in range(RING)]
        s_gain = S("s_gain")
        s_consts = S("s_consts")
        s_spill = S("s_spill")
        s_reload = S("s_reload")
        s_keys = S("s_keys")
        s_out = S("s_out")
        s_hi = S("s_hi")
        s_lo = S("s_lo")
        s_used = S("s_used")
        s_evac = S("s_evac")
        s_vevac = S("s_vevac")
        s_sq = S("s_sq")
        s_sum = S("s_sum")
        s_std = S("s_std")
        s_rstd = S("s_rstd")
        s_h = S("s_h")
        s_ahi = S("s_ahi")
        s_alo = S("s_alo")
        s_yadd = S("s_yadd")
        s_vec = S("s_vec")
        s_tk = S("s_tk")
        s_act = S("s_act")
        s_pool = S("s_pool")
        s_pool_turn = S("s_pool_turn")
        s_gates_ps = S("s_gates_ps")
        s_grow = S("s_grow")
        s_grow_act = S("s_grow_act")
        s_rows = S("s_rows")
        s_floor = S("s_floor")
        s_d_ps = S("s_d_ps")
        s_dm = S("s_dm")
        s_p = S("s_p")
        s_s_ps = S("s_s_ps")
        s_s = S("s_s")
        s_num_ps = S("s_num_ps")
        s_hn = S("s_hn")
        s_hsq = S("s_hsq")
        s_ssq_ps = S("s_ssq_ps")
        s_hstd = S("s_hstd")
        s_mixed = S("s_mixed")
        s_pool_ps = S("s_pool_ps")
        s_pool_out = S("s_pool_out")
        s_y = S("s_y")
        s_gl_ps = S("s_gl_ps")
        s_gl = S("s_gl")
        s_pre_ps = S("s_pre_ps")
        s_la = S("s_la")
        s_decay = S("s_decay")
        s_bias = S("s_bias")
        s_la_act = S("s_la_act")
        s_karg = S("s_karg")
        s_kexp = S("s_kexp")
        s_ke = S("s_ke")
        s_att_ps = S("s_att_ps")
        s_att = S("s_att")
        s_o_ps = S("s_o_ps")
        s_o = S("s_o")
        s_osq = S("s_osq")
        s_sc_ps = S("s_sc_ps")
        s_sc = S("s_sc")
        s_cvs = S("s_cvs")
        s_cexp = S("s_cexp")
        s_slots = S("s_slots")
        s_jt_ps = S("s_jt_ps")
        s_jt = S("s_jt")
        s_key1 = S("s_key1")
        s_hot1 = S("s_hot1")
        s_hot2 = S("s_hot2")
        s_hot_free = S("s_hot_free")
        s_g = S("s_g")
        s_chi = S("s_chi")
        s_clo = S("s_clo")

        def at(o, n, k=None):
            a = big[:, o:o + n]
            return a if k is None else a.rearrange("p (k t) -> p k t", k=k)

        O_BANK = (0, 3)

        def o_sum(h):
            return ps[:, (2, 7, 5, 6)[h], 0:T]

        G_PER = P // G_SUB

        def exp_count(g):
            return g + (2 if g < 2 else 4)

        def att_count(g):
            return g + (1 if g < 2 else 2)

        def sc_turns(layer, part):
            return (layer * PARTS + part) * SC_TURNS

        def bank(b, n=512, k=None):
            a = ps[:, b, 0:n]
            return a if k is None else a.rearrange("p (k t) -> p k t", k=k)

        def banks(b, nb):
            return ps[:, b:b + nb, :].rearrange("p b n -> p (b n)")

        G_NORM = [0, 16, 32, 48, 64]
        G_EH, G_PS, G_OH, G_BG = 80, 88, 96, 112
        N_CONSTS = 5
        POOL_CONSTS = 17
        WG_W = 36

        SQ_TILES = {0: 4, 1: KB, 2: 4, 3: KB, 4: 4}
        SQ0 = {k: sum(SQ_TILES[j] for j in range(k)) for k in range(5)}

        FILL = {("h", 0): 0, ("y", 0): 1, ("k", 0): 2, ("h", 1): 3, ("y", 1): 4, ("k", 1): 5}

        block = ctx.enter_context(nc.Block())

        @block.sync
        def _(sp):
            for c in range(4):
                sp.dma_start(at(XT + 1024 * c, 1024, 4), xT[:, 4 * c:4 * c + 4, :]).then_inc(s_x[c], 16)
            sp.dma_start(gain[:, :], gains).then_inc(s_gain, 16)

            def load(slot, n, src, wait=True):
                if wait:
                    sp.wait_ge(s_used, n - (RING - 1))
                sp.dma_start(w_raw[:, slot, :], src).then_inc(s_landed[slot], 16)

            for layer, (dense, u) in enumerate(((dense0, u0), (dense1, u1))):
                n0 = SLAB0["qk", layer]
                if layer == 0:
                    for s in range(RING):
                        load(s, s, dense[s], wait=False)
                with sp.Fori(1 if layer == 0 else 0, DENSE[layer] // RING) as i:
                    for s in range(RING):
                        load(s, i * RING + (n0 + s), dense[bass.ds(i * RING + s, 1)].rearrange("a p n -> (a p) n"))
                n0 = SLAB0["u", layer]
                with sp.Fori(0, 2 * N_KEYS // RING) as i:
                    for s in range(RING):
                        load(s, i * RING + (n0 + s), u[bass.ds(i * RING + s, 1)].rearrange("a p n -> (a p) n"))
                n0 = SLAB0["vt", layer]
                vrows = v_tab[layer].rearrange("(e p) (h n) -> e p h n", p=P, h=2)
                for h in range(2):
                    with sp.Fori(0, HALF // RING) as i:
                        for s in range(RING):
                            load(s, i * RING + (n0 + HALF * h + s),
                                 vrows[bass.ds(i * RING + s, 1), :, h, :].rearrange("a p n -> (a p) n"))
                with sp.Fori(HALF // 4, N_KEYS // 4) as i:
                    for s in range(2 * RING):
                        load(s % RING, i * 2 * RING + (n0 + s),
                             vrows[bass.ds(i * RING + s % RING, 1), :, s // RING, :].rearrange("a p n -> (a p) n"))
            for c in range(4):
                sp.wait_ge(s_h, 16 + c + 1)
                sp.dma_start(out[:, 4 * c:4 * c + 4, :], at(HT + 1024 * c, 1024, 4)).then_inc(s_out, 16)
            sp.wait_ge(s_out, 64)

        @block.gpsimd
        def _(pool):
            count = [0]

            def step(ins):
                ins.then_inc(s_pool, 1)
                count[0] += 1
                pool.wait_ge(s_pool, count[0])

            step(pool.memset(ones[:, :], 1.0))
            step(pool.memset(epst[:, :], EPS))
            step(pool.memset(at(E_WG, 16 * WG_W), 0.0))
            wg = at(E_WG, 16 * WG_W, 16)
            pool.dma_start(wg[:, :, 0:4], gates_in[:, 0:KB, 0:4]).then_inc(s_consts, 16)
            pool.dma_start(wg[:, :, 32:36], gates_in[:, 0:KB, 4:8]).then_inc(s_consts, 16)
            pool.dma_start(gbias[0:4, :], gates_in[0:4, KB, 0:2]).then_inc(s_consts, 16)
            pool.dma_start(at(E_WPOOL, 2048), w_pool).then_inc(s_consts, 16)
            pool.dma_start(at(E_ICNT, 1024), inv_count).then_inc(s_consts, 16)
            pool.dma_start(at(K_KEYS, 2048), keys[0]).then_inc(s_keys, 16)
            step(pool.memset(zrow[:, :], 0.0))
            step(pool.memset(ident[:, :], 0.0))
            step(pool.affine_select(out=ident[:, :], in_=ident[:, :], compare_op=ALU.not_equal, fill=1.0,
                                    base=0, pattern=[[-1, P]], channel_multiplier=1))
            step(pool.iota(iota[:, :], pattern=[[1, P]], base=0, channel_multiplier=0,
                           allow_small_or_imprecise_dtypes=True))
            step(pool.memset(tri01[:, :], 1.0))
            step(pool.affine_select(out=tri01[:, 0:P], in_=tri01[:, 0:P], compare_op=ALU.is_ge, fill=0.0,
                                    base=0, pattern=[[1, P]], channel_multiplier=-1))
            step(pool.memset(at(E_MASK, 384), 0.0))
            for b in (0, 2):
                m = at(E_MASK + P * b, P)
                step(pool.affine_select(out=m, in_=m, compare_op=ALU.is_ge, fill=NEG, base=0,
                                        pattern=[[1, P]], channel_multiplier=-1))
            sel = big[0:4, E_SEL:E_SEL + 1024].rearrange("p (h t) -> p h t", h=4)
            step(pool.memset(sel, 0.0))
            step(pool.affine_select(out=sel, in_=sel, compare_op=ALU.not_equal, fill=1.0, base=0,
                                    pattern=[[-1, 4], [0, T]], channel_multiplier=1))
            for o in (E_PT, E_S2, E_S4):
                step(pool.memset(at(o, 8 * E_PW, 8)[:, :, 0:E_PAD], 0.0))
            assert count[0] == POOL_CONSTS, count[0]
            pool.memset(credit[:, :], 0.0).then_inc(s_hot_free, 2)
            pool.wait_ge(s_hot_free, 2)
            pool.memset(credit[:, :], 0.0).then_inc(s_g, 4)
            pool.wait_ge(s_g, 4)
            pool.memset(credit[:, :], 0.0).then_inc(s_sc, 1)
            pool.wait_ge(s_sc, 1)
            pool.memset(credit[:, :], 0.0).then_inc(s_sc_ps, 1)

            def tiles(o, j0, shift=0):
                return at(o, 8 * E_PW, 8)[:, j0:8, E_PAD - shift:E_PAD - shift + T]

            pool.wait_ge(s_evac, BLOCK0["out", 0])
            step(pool.tensor_tensor(tiles(E_S2, 0), tiles(E_PT, 0), tiles(E_PT, 0, 1), ALU.add))
            step(pool.tensor_tensor(tiles(E_S4, 2), tiles(E_S2, 2), tiles(E_S2, 2, 2), ALU.add))
            step(pool.tensor_tensor(tiles(E_S2, 4), tiles(E_S4, 4), tiles(E_S4, 4, 4), ALU.add))
            step(pool.tensor_tensor(tiles(E_S4, 6), tiles(E_S2, 6), tiles(E_S2, 6, 8), ALU.add))
            pool.wait_ge(s_consts, 16 * N_CONSTS)
            for g in range(4):
                src = at(E_S2 if g % 2 == 0 else E_S4, 8 * E_PW, 8)[:, 2 * g:2 * g + 2, E_PAD:E_PW]
                pt = at(E_PT, 8 * E_PW, 8)[:, 2 * g:2 * g + 2, E_PAD:E_PW]
                inv = at(E_ICNT + T * g, T).unsqueeze(1).broadcast_to([P, 2, T])
                step(pool.tensor_tensor(src, src, inv, ALU.mult))
                pool.tensor_tensor(pt, src, pt, ALU.subtract).then_inc(s_mixed, 1)

            def exponents():
                b3 = at(O_B, 2048).rearrange("p (g t) -> p g t", t=G_SUB)
                b8 = at(O_B, 2048, 8)
                mid = G_SUB // 2 - 1
                pool.wait_ge(s_decay, 2)
                pool.tensor_tensor(at(O_QE, 2048).rearrange("p (g t) -> p g t", t=G_SUB), b3,
                                   b3[:, :, mid:mid + 1].broadcast_to([P, 128, G_SUB]), ALU.subtract).then_inc(s_karg, 1)
                for g in range(T // G_SUB):
                    s0, n = g // G_PER * P, G_SUB * (g % G_PER + 1)
                    ref = G_SUB * g + mid
                    if g == 2:
                        for o, t in ((O_QX, P), (O_KX, 0)):
                            pool.tensor_tensor(at(o, 1024, 8), b8[:, :, t:t + P],
                                               b8[:, :, P - 1:P].broadcast_to([P, 8, P]), ALU.subtract).then_inc(s_karg, 1)
                    if g >= 2:
                        pool.wait_ge(s_att_ps, att_count(g - 2))
                    pool.tensor_tensor(at(O_KE + 1024 * (g % 2), 1024, 8)[:, :, 0:n], b8[:, :, s0:s0 + n],
                                       b8[:, :, ref:ref + 1].broadcast_to([P, 8, n]), ALU.subtract).then_inc(s_karg, 1)

            for layer in range(2):
                if layer == 1:
                    exponents()
                pool.wait_ge(s_evac, BLOCK0["wq", layer])
                pool.dma_start(spill, at(XT, 4096)).then_inc(s_spill, 16)
                for part in range(PARTS):
                    with pool.Fori(0, SC_TURNS) as i:
                        for q in range(8):
                            pool.wait_ge(s_key1, i * 8 + (sc_turns(layer, part) * 8 + q + 1))
                            pool.sem_inc(s_pool_turn, 1)
                            b = 4 * (q % 2)
                            w = jw[:, :, bass.ds(i * SC_TOKENS + 4 * q, 4)].rearrange("p c t -> p t c")
                            pool.tensor_tensor(hot1[:, b:b + 4, :, :],
                                               key1[:, b:b + 4, :].unsqueeze(2).broadcast_to([P, 4, WPARTS, HALF]),
                                               w.unsqueeze(3).broadcast_to([P, 4, WPARTS, HALF]),
                                               ALU.mult).then_inc(s_hot1, 1)
                pool.wait_ge(s_used, SLAB0["vt", layer] + HALF + KB)
                pool.wait_ge(s_spill, 16 * (layer + 1))
                pool.dma_start(at(XT, 4096), spill).then_inc(s_reload, 16)
                if layer == 0:
                    pool.wait_ge(s_used, SLAB0["qk", 1])
                    pool.dma_start(at(K_KEYS, 2048), keys[1]).then_inc(s_keys, 16)
                    pool.dma_start(big[0:G_RANK, O_WGATE:O_WGATE + 1024], w_gate).then_inc(s_consts, 16)
                    pool.dma_start(at(O_WGL, 256), w_glow).then_inc(s_consts, 16)

        @block.scalar
        def _(act):
            pending = [None]
            count = [0]

            def chain(ins):
                ins.then_inc(s_act, 1)
                count[0] += 1
                act.wait_ge(s_act, count[0])

            def hi(slot, n):
                act.wait_ge(s_landed[slot], (n // RING + 1) * 16 if isinstance(n, int) else (n - slot) * 4 + 16)
                act.activation(w_hi[:, slot, :], w_raw[:, slot, :], ACT.Copy).then_inc(s_hi, 1)

            def flush():
                if pending[0]:
                    pending[0]()
                    pending[0] = None

            def ahead(n0):
                hi(0, n0)
                hi(1, n0 + 1)
                flush()
                hi(2, n0 + 2)
                hi(3, n0 + 3)

            def stream(name, layer, nblocks, evac, after=None):
                n0 = SLAB0[name, layer]
                evac(0)
                if after:
                    after(-1)

                def turn(i):
                    hi(0, i * 4 + n0)
                    hi(1, i * 4 + (n0 + 1))
                    evac(i * 2 - 1)
                    if after:
                        after(i * 2 - 2)
                    hi(2, i * 4 + (n0 + 2))
                    hi(3, i * 4 + (n0 + 3))
                    evac(i * 2)
                    if after:
                        after(i * 2 - 1)
                with act.Fori(1, nblocks // 2) as i:
                    turn(i)

                def last():
                    evac(nblocks - 1)
                    if after:
                        after(nblocks - 2)
                        after(nblocks - 1)
                pending[0] = last

            def block_to(name, layer, o, func=ACT.Copy, width=T, skip=0, scale=1.0, hi_part=None):
                n0 = SLAB0[name, layer]
                turnwise = [0]

                def evac(b):
                    if isinstance(b, int):
                        par = b % 2
                        dst = at(o + skip + b * width, T)
                    else:
                        par = 1 - turnwise[0] % 2
                        turnwise[0] += 1
                        dst = big[:, bass.ds(b * width + (o + skip), T)]
                    act.wait_ge(s_used, b * 2 + (n0 + 2))
                    act.activation(dst, bank(par, T), func, scale=scale).then_inc(s_evac, 1)
                return evac

            def v_groups(layer, ngroups, o, row, between=None):
                n0 = SLAB0["v", layer]
                for g in range(ngroups):
                    if g:
                        hi(0, n0 + 8 * g)
                        hi(1, n0 + 8 * g + 1)
                        flush()
                        hi(2, n0 + 8 * g + 2)
                        hi(3, n0 + 8 * g + 3)
                    if between and g in between:
                        between[g]()
                    for s in range(4):
                        hi(s, n0 + 8 * g + 4 + s)

                    def evac(g=g):
                        act.wait_ge(s_used, n0 + 8 * g + 8)
                        for tb in range(TB):
                            act.activation(at(o + row * tb + 512 * g, 512), bank(3 + 2 * (g % 2) + tb),
                                           ACT.Copy).then_inc(s_vevac, 1)
                    pending[0] = evac

            def square(c):
                act.activation(at(HT + 1024 * c, 1024), at(XT + 1024 * c, 1024), ACT.Square).then_inc(s_sq, 1)

            def norm(k, fill, n0=None):
                act.wait_ge(s_sum, k + 1)
                act.activation(stdv[:, :], bank(2, T), ACT.Sqrt, bias=epst[:, 0:1], scale=1.0 / D).then_inc(s_std, 1)
                if n0 is not None:
                    hi(2, n0 + 2)
                    hi(3, n0 + 3)
                if fill is not None:
                    act_hi(fill, s_h, 4 * k)

            def out_squares(layer):
                n0, b0 = SLAB0["out", layer], BLOCK0["out", layer]

                def sq(b):
                    act.wait_ge(s_evac, b + (b0 + 1))
                    if isinstance(b, int):
                        src, dst = at(XT + b * T, T), at(HT + b * T, T)
                    else:
                        src, dst = big[:, bass.ds(b * T + XT, T)], big[:, bass.ds(b * T + HT, T)]
                    act.activation(dst, src, ACT.Square).then_inc(s_sq, 1)

                def turn(i):
                    hi(0, i * 4 + n0)
                    hi(1, i * 4 + (n0 + 1))
                    sq(i * 2 - 2)
                    hi(2, i * 4 + (n0 + 2))
                    hi(3, i * 4 + (n0 + 3))
                    sq(i * 2 - 1)
                with act.Fori(1, KB // 2) as i:
                    turn(i)
                hi(0, n0 + 32)
                sq(KB - 2)
                hi(1, n0 + 33)
                sq(KB - 1)

            def act_hi(fill, src, base):
                for c in range(4):
                    act.wait_ge(src, base + c + 1)
                    act.activation(act_hi_t[:, 4 * c:4 * c + 4, :], at(HT + 1024 * c, 1024, 4), ACT.Copy).then_inc(s_ahi, 1)

            def even():
                act.wait_ge(s_pool, 2)
                for c in range(4):
                    act.wait_ge(s_x[c], 16)
                    square(c)
                hi(0, 0)
                hi(1, 1)
                norm(0, FILL["h", 0], 0)

                stream("qk", 0, 8, block_to("qk", 0, E_Q))
                ahead(SLAB0["v", 0])
                rows = lambda r: big[0:4, E_ROWS + T * r:E_ROWS + T * (r + 1)]
                act.wait_ge(s_grow, 1)
                chain(act.activation(rows(2), rows(1), ACT.Exp, scale=-1.0))
                act.activation(rows(2), rows(2), ACT.Ln, bias=1.0).then_inc(s_grow_act, 1)
                act.wait_ge(s_rows, 1)
                act.activation(rows(5), rows(1), ACT.Exp, scale=-1.0).then_inc(s_floor, 1)
                v_groups(0, 2, E_V, 1024)
                ahead(SLAB0["o", 0])
                stream("o", 0, 8, block_to("o", 0, E_SO, func=ACT.Sigmoid))
                ahead(SLAB0["p", 0])
                stream("p", 0, 8, block_to("p", 0, E_PT, width=E_PW, skip=E_PAD))
                ahead(SLAB0["out", 0])
                for h in range(M_HEADS):
                    act.wait_ge(s_dm, h + 1)
                    act.activation(at(E_PE + 384 * h, 384), at(E_PE + 384 * h, 384), ACT.Exp).then_inc(s_p, 1)
                for h in range(M_HEADS):
                    act.wait_ge(s_hn, h + 1)
                    act.wait_ge(s_num_ps, M_HEADS)
                    act.activation(at(E_V + 512 * h, 512), at(HT + 512 * h, 512), ACT.Square).then_inc(s_hsq, 1)
                for c in range(2):
                    act.wait_ge(s_ssq_ps, c + 1)
                    act.activation(at(E_PE + 512 * c, 512), bank(3 + c), ACT.Sqrt, bias=epst[:, 0:1],
                                   scale=1.0 / M_DV).then_inc(s_hstd, 1)
                for j in range(8):
                    act.wait_ge(s_pool_ps, j // 2 * 2 + 2)
                    b = (0, 0, 1, 1, 5, 5, 6, 6)[j]
                    act.activation(at(HT + 2048 + T * j, T), ps[:, b, T * (j % 2):T * (j % 2) + T], ACT.Copy,
                                   scale=gain[:, G_PS + j:G_PS + j + 1]).then_inc(s_pool_out, 1)
                for c in range(4):
                    if c < 2:
                        act.wait_ge(s_y, c + 1)
                    else:
                        act.wait_ge(s_pool_out, 4 * (c - 1))
                    act.activation(act_hi_t[:, 4 * c:4 * c + 4, :], at(HT + 1024 * c, 1024, 4), ACT.Copy).then_inc(s_ahi, 1)
                out_squares(0)

            def odd():
                n0 = SLAB0["qk", 1]
                for c in range(4):
                    if c == 2:
                        hi(0, n0)
                        hi(1, n0 + 1)
                    act.wait_ge(s_yadd, c + 1)
                    square(c)
                norm(2, FILL["h", 1], n0)
                stream("qk", 1, 16, block_to("qk", 1, O_Q))
                ahead(SLAB0["v", 1])
                act.wait_ge(s_gl_ps, 1)
                act.activation(big[0:G_RANK, O_GLT:O_GLT + T], ps[0:G_RANK, 7, 0:T], ACT.Copy).then_inc(s_gl, 1)

                def o_root(h):
                    act.wait_ge(s_ssq_ps, 2 + h + 1)
                    act.activation(at(O_B + T * h, T), o_sum(h), ACT.Sqrt, bias=epst[:, 0:1],
                                   scale=1.0 / G_DV).then_inc(s_hstd, 1)

                def decay_logs():
                    act.wait_ge(s_la, 1)
                    chain(act.activation(at(O_KE + 2048, 2048), at(O_KE + 2048, 2048), ACT.Exp, scale=-1.0))
                    act.activation(at(O_KE + 2048, 2048), at(O_KE + 2048, 2048), ACT.Ln, bias=1.0).then_inc(s_la_act, 1)
                v_groups(1, 4, O_V, 2048, {3: decay_logs})
                ahead(SLAB0["r", 1])
                act.wait_ge(s_karg, 1)
                act.activation(at(O_QE, 2048), at(O_QE, 2048), ACT.Exp, scale=1.0 / G_TAU).then_inc(s_kexp, 1)

                def k_exp(g):
                    if g == 2:
                        for o, sign in ((O_QX, 1.0), (O_KX, -1.0)):
                            act.wait_ge(s_karg, 4 if o == O_QX else 5)
                            act.activation(at(o, 1024), at(o, 1024), ACT.Exp, scale=sign / G_TAU).then_inc(s_kexp, 1)
                    n = G_SUB * (g % G_PER + 1)
                    ke = at(O_KE + 1024 * (g % 2), 1024, 8)[:, :, 0:n]
                    act.wait_ge(s_karg, exp_count(g))
                    act.activation(ke, ke, ACT.Exp, scale=-1.0 / G_TAU).then_inc(s_kexp, 1)
                r0 = SLAB0["r", 1]
                evac = block_to("r", 1, O_R, func=ACT.Silu)
                k_exp(0)
                k_exp(1)
                for b in range(KB):
                    evac(b)
                    if b < KB - 2:
                        hi(2 * b % 4, r0 + 2 * b + 4)
                        hi((2 * b + 1) % 4, r0 + 2 * b + 5)
                        k_exp(b + 2)
                    else:
                        hi(2 * b % 4, r0 + 2 * b + 4)
                        hi((2 * b + 1) % 4, r0 + 2 * b + 5)
                for h in range(G_HEADS):
                    act.wait_ge(s_o_ps, h + 1)
                    act.activation(at(O_KE + 1024 * h, 1024), banks(O_BANK[h % 2], 2), ACT.Square).then_inc(s_osq, 1)
                    act.activation(at(HT + 1024 * h, 1024), banks(O_BANK[h % 2], 2), ACT.Copy).then_inc(s_o, 1)
                    if h:
                        o_root(h - 1)
                o_root(G_HEADS - 1)
                act_hi(FILL["y", 1], s_y, 2)
                out_squares(1)

            def experts(layer):
                norm(2 * layer + 1, FILL["k", layer], SLAB0["wq", layer])
                qbase = SLAB0["wq", layer]
                sc = at(K_SC, 4096).rearrange("p (b h c n) -> p b h c n", b=TB, h=HEADS, c=2)
                q_turn = [0]

                def q_evac(b):
                    if isinstance(b, int):
                        par = b % 2
                    else:
                        par = 1 - q_turn[0] % 2
                        q_turn[0] += 1
                    act.wait_ge(s_used, b * 2 + (qbase + 2))
                    if not (isinstance(b, int) and b < 2 and layer == 0):
                        act.wait_ge(s_sc_ps, b + 16 * layer)
                    act.activation(at(K_QS + T * par, T), bank(par, T), ACT.Copy).then_inc(s_evac, 1)

                s_turn = [0]

                def sc_save(q):
                    if isinstance(q, int):
                        if q < 0:
                            return
                        par, head = q % 2, q // 2
                        act.wait_ge(s_sc_ps, 16 * layer + q + 2)
                        act.activation(sc[:, :, head, par, :], bank(2 + par, T, TB), ACT.Copy).then_inc(s_sc, 1)
                    else:
                        par = s_turn[0] % 2
                        s_turn[0] += 1
                        act.wait_ge(s_sc_ps, q + (16 * layer + 2))
                        src = big[:, bass.ds(q * P + K_SC, 2048 + P)]
                        dst = src.rearrange("p (a n) -> p a n", n=P)[:, 0:17:16, :]
                        act.activation(dst, bank(2 + par, T, TB), ACT.Copy).then_inc(s_sc, 1)
                stream("wq", layer, 16, q_evac, after=sc_save)
                ahead(SLAB0["u", layer])

                ubase = SLAB0["u", layer]

                def ge(b, par, first=False):
                    act.wait_ge(s_used, b * 2 + (ubase + 2))
                    dst = at(b * T, T) if isinstance(b, int) else big[:, bass.ds(b * T, T)]
                    act.activation(dst, bank(par, T), ACT.Gelu).then_inc(s_evac, 1)

                act.wait_ge(s_spill, 16 * (layer + 1))
                ge(0, 0)
                for s in range(4):
                    hi(s, ubase + 4 + s)
                    if s % 2:
                        ge(s // 2 + 1, (s // 2 + 1) % 2)

                def u_turn(i):
                    for s in range(8):
                        hi(s % 4, i * 8 + (ubase + s))
                        if s % 2:
                            ge(i * 4 + (s // 2 - 1), (s // 2 + 1) % 2)
                with act.Fori(1, ITEMS) as i:
                    u_turn(i)
                act.wait_ge(s_cvs, layer + 1)
                act.activation(cv[:, :, :], cv[:, :, :], ACT.Exp).then_inc(s_cexp, 1)
                with act.Fori(ITEMS, N_KEYS // 4) as i:
                    u_turn(i)

                vbase = SLAB0["vt", layer]
                hi(0, vbase)
                hi(1, vbase + 1)
                act.wait_ge(s_g, SC_TURNS * 4 * (2 * layer + 1) + 4)
                act.wait_ge(s_used, vbase - 1)

                def c_hi(block_, buf):
                    src = at(block_ * T, T) if isinstance(block_, int) else big[:, bass.ds(block_ * T, T)]
                    act.activation(act_hi_t[:, buf, :], src, ACT.Copy).then_inc(s_chi, 1)
                for b in range(4):
                    c_hi(b, b)
                ge(N_KEYS - 1, 1)
                hi(2, vbase + 2)
                hi(3, vbase + 3)
                for s in range(4, 8):
                    hi(s % 4, vbase + s)
                    c_hi(s, s)
                for h in range(2):
                    with act.Fori(1 - h, HALF // 8) as i:
                        for s in range(8):
                            hi(s % 4, i * 8 + (vbase + HALF * h + s))
                            c_hi(i * 8 + s, s)
                act.wait_ge(s_g, SC_TURNS * 8 * (layer + 1) + 4)
                with act.Fori(HALF // 4, N_KEYS // 4) as i:
                    for s in range(8):
                        hi(s % 4, i * 8 + (vbase + s))
                        if s < 4:
                            c_hi(i * 4 + s, s)

            even()
            experts(0)
            odd()
            experts(1)
            for c in range(4):
                act.wait_ge(s_yadd, 4 + c + 1)
                square(c)
            norm(4, None)

        @block.vector
        def _(dve):
            count = [0]

            def chain(ins):
                ins.then_inc(s_vec, 1)
                count[0] = count[0] + 1
                dve.wait_ge(s_vec, count[0])

            def lo(slot, n):
                dve.wait_ge(s_hi, n + 1)
                dve.tensor_tensor(w_lo[:, slot, :], w_raw[:, slot, :], w_hi[:, slot, :].bitcast(F32),
                                  ALU.subtract).then_inc(s_lo, 1)

            def ahead(n0):
                for s in range(RING):
                    lo(s, n0 + s)

            def stream(name, layer, nslabs):
                n0 = SLAB0[name, layer]
                with dve.Fori(1, nslabs // RING) as i:
                    for s in range(RING):
                        lo(s, i * RING + (n0 + s))

            def v_groups(layer, ngroups, between=None):
                n0 = SLAB0["v", layer]
                for g in range(ngroups):
                    for s in range(8):
                        if g or s >= 4:
                            lo(s % 4, n0 + 8 * g + s)
                        if between and (g, s) in between:
                            between[g, s]()

            def residual(layer):
                n0 = SLAB0["out", layer]

                def add(b, par):
                    dve.wait_ge(s_used, b * 2 + (n0 + 2))
                    dst = at(XT + b * T, T) if isinstance(b, int) else big[:, bass.ds(b * T + XT, T)]
                    dve.tensor_tensor(dst, dst, bank(par, T), ALU.add).then_inc(s_evac, 1)
                add(0, 0)
                with dve.Fori(1, KB // 2) as i:
                    lo(0, i * 4 + n0)
                    lo(1, i * 4 + (n0 + 1))
                    add(i * 2 - 1, 1)
                    lo(2, i * 4 + (n0 + 2))
                    lo(3, i * 4 + (n0 + 3))
                    add(i * 2, 0)
                lo(0, n0 + 32)
                lo(1, n0 + 33)
                add(KB - 1, 1)

            def chunk_lo(fill, c):
                dve.wait_ge(s_ahi, 4 * fill + c + 1)
                dve.tensor_tensor(act_lo_t[:, 4 * c:4 * c + 4, :], at(HT + 1024 * c, 1024, 4),
                                  act_hi_t[:, 4 * c:4 * c + 4, :].bitcast(F32), ALU.subtract).then_inc(s_alo, 1)

            def norm(k, fill, n0=None):
                dve.wait_ge(s_std, k + 1)
                dve.reciprocal(rstd[:, :], stdv[:, :]).then_inc(s_rstd, 1)
                dve.wait_ge(s_rstd, k + 1)
                for c in range(4):
                    for j in range(4 * c, 4 * c + 4):
                        ins = dve.scalar_tensor_tensor(out=at(HT + T * j, T), in0=at(XT + T * j, T),
                                                       scalar=gain[:, G_NORM[k] + j:G_NORM[k] + j + 1],
                                                       in1=rstd[:, :], op0=ALU.mult, op1=ALU.mult)
                    ins.then_inc(s_h, 1)
                    if fill is not None and c:
                        chunk_lo(fill, c - 1)
                if fill is not None:
                    chunk_lo(fill, 3)
                if n0 is not None:
                    lo(2, n0 + 2)
                    lo(3, n0 + 3)

            def head_norm(nheads, tiles_per_head, gcol, rr, silu, fill, std0):
                heads = 4 // tiles_per_head
                for c in range(nheads * tiles_per_head // 4):
                    dve.wait_ge(s_hstd, std0 + c + 1)
                    r = at(rr + T * heads * c, T * heads)
                    chain(dve.reciprocal(r, r))
                    for j in range(4 * c, 4 * c + 4):
                        h = j // tiles_per_head
                        ins = dve.scalar_tensor_tensor(out=at(HT + T * j, T), in0=at(HT + T * j, T),
                                                       scalar=gain[:, gcol + j:gcol + j + 1],
                                                       in1=at(rr + T * h, T), op0=ALU.mult, op1=ALU.mult)
                    chain(ins)
                    dve.tensor_tensor(at(HT + 1024 * c, 1024), at(HT + 1024 * c, 1024),
                                      at(silu + 1024 * c, 1024), ALU.mult).then_inc(s_y, 1)
                    if c:
                        chunk_lo(fill, c - 1)
                for c in range(nheads * tiles_per_head // 4 - 1, 4):
                    chunk_lo(fill, c)

            def even():
                dve.wait_ge(s_gain, 16)
                lo(0, 0)
                lo(1, 1)
                norm(0, FILL["h", 0], 0)
                stream("qk", 0, 16)
                ahead(SLAB0["v", 0])
                rows = lambda r: big[0:4, E_ROWS + T * r:E_ROWS + T * (r + 1)]
                dve.wait_ge(s_consts, 16 * N_CONSTS)
                dve.wait_ge(s_pool, POOL_CONSTS)
                dve.wait_ge(s_gates_ps, 1)
                chain(dve.tensor_scalar(rows(0), ps[0:4, 7, 0:T], gbias[0:4, 0:1], None, ALU.add))
                chain(dve.tensor_scalar(rows(3), ps[32:36, 7, 0:T], gbias[0:4, 1:2], None, ALU.add))
                dve.scalar_tensor_tensor(out=rows(1), in0=rows(3), scalar=-1.0, in1=rows(3), op0=ALU.mult,
                                         op1=ALU.max).then_inc(s_grow, 1)
                dve.wait_ge(s_grow_act, 1)
                chain(dve.scalar_tensor_tensor(out=rows(1), in0=rows(3), scalar=0.0, in1=rows(2),
                                               op0=ALU.min, op1=ALU.subtract))
                chain(dve.memset(rows(2), 0.0))
                chain(dve.tensor_tensor_scan(rows(3), rows(1), rows(2), 0.0, ALU.add, ALU.add))
                chain(dve.tensor_tensor(rows(4), rows(0), rows(3), ALU.subtract))
                chain(dve.tensor_tensor_scan(rows(0), rows(4), rows(4), 0.0, ALU.max, ALU.max))
                chain(dve.tensor_scalar(rows(2), rows(0), -1.0, None, ALU.mult))
                dve.tensor_tensor(rows(1), rows(0), rows(3), ALU.add).then_inc(s_rows, 1)
                v_groups(0, 2)
                ahead(SLAB0["o", 0])
                stream("o", 0, 16)
                ahead(SLAB0["p", 0])
                stream("p", 0, 16)
                ahead(SLAB0["out", 0])

                def masked(h):
                    dve.wait_ge(s_d_ps, h + 1)
                    dve.tensor_tensor(at(E_PE + 384 * h, 384), bank(3 + h % 2, 384), at(E_MASK, 384),
                                      ALU.add).then_inc(s_dm, 1)

                def weights(h):
                    dve.wait_ge(s_p, h + 1)
                    dve.wait_ge(s_s_ps, h + 1)
                    pe_h = at(E_PE + 384 * h, 384)
                    dve.scalar_tensor_tensor(out=pe_h, in0=bank(5 + h % 2, 384), scalar=M_DK ** -0.5, in1=pe_h,
                                             op0=ALU.mult, op1=ALU.mult).then_inc(s_s, 1)

                def output(h):
                    dve.wait_ge(s_num_ps, h + 1)
                    chain(dve.tensor_copy(stdv[:, :], ps[:, 2, 0:T]))
                    chain(dve.scalar_tensor_tensor(out=rstd[:, :], in0=stdv[:, :], scalar=-1.0, in1=stdv[:, :],
                                                   op0=ALU.mult, op1=ALU.max))
                    chain(dve.tensor_tensor(rstd[:, :], rstd[:, :], ps[:, 2, T:2 * T], ALU.max))
                    chain(dve.reciprocal(stdv[:, :], rstd[:, :]))
                    dve.tensor_tensor(at(HT + 512 * h, 512, 2), bank(7, 512, 2),
                                      stdv[:, :].unsqueeze(1).broadcast_to([P, 2, T]), ALU.mult).then_inc(s_hn, 1)
                for h in range(M_HEADS):
                    masked(h)
                    weights(h)
                    if h:
                        output(h - 1)
                output(M_HEADS - 1)
                head_norm(M_HEADS, 2, G_EH, E_PE, E_SO, FILL["y", 0], 0)
                residual(0)

            def odd():
                norm(2, FILL["h", 1], SLAB0["qk", 1])
                stream("qk", 1, 32)
                ahead(SLAB0["v", 1])

                def biased(r):
                    dve.wait_ge(s_pre_ps, r + 1)
                    for j in range(4 * r, 4 * r + 4):
                        b = 7 if j % 4 < 2 else 2
                        ins = dve.tensor_scalar(at(O_KE + T * j, T), ps[:, b, T * (j % 2):T * (j % 2) + T],
                                                gain[:, G_BG + j:G_BG + j + 1], None, ALU.add)
                    ins.then_inc(s_bias, 1)

                def magnitude():
                    biased(1)
                    dve.wait_ge(s_bias, 2)
                    dve.scalar_tensor_tensor(out=at(O_KE + 2048, 2048), in0=at(O_KE, 2048), scalar=-1.0,
                                             in1=at(O_KE, 2048), op0=ALU.mult, op1=ALU.max).then_inc(s_la, 1)

                def decay():
                    chain(dve.memset(rstd[:, :], 0.0))
                    dve.wait_ge(s_la_act, 1)
                    chain(dve.scalar_tensor_tensor(out=at(O_KE, 2048), in0=at(O_KE, 2048), scalar=0.0,
                                                   in1=at(O_KE + 2048, 2048), op0=ALU.min, op1=ALU.subtract))

                def decay_sum(js):
                    for j in js:
                        ins = dve.tensor_tensor_scan(at(O_B + T * j, T), at(O_KE + T * j, T), rstd[:, :], 0.0,
                                                     ALU.add, ALU.add)
                    ins.then_inc(s_decay, 1)
                v_groups(1, 4, {(1, 7): lambda: biased(0), (2, 7): magnitude, (3, 5): decay,
                                (3, 6): lambda: decay_sum(range(4)), (3, 7): lambda: decay_sum(range(4, 8))})
                ahead(SLAB0["r", 1])
                dve.wait_ge(s_kexp, 1)
                dve.scalar_tensor_tensor(out=at(O_QE, 2048), in0=at(O_QE, 2048), scalar=G_DK ** -0.5,
                                         in1=at(O_Q, 2048), op0=ALU.mult, op1=ALU.mult).then_inc(s_ke, 1)

                def k_mul(g):
                    if g == 2:
                        dve.wait_ge(s_kexp, 4)
                        dve.scalar_tensor_tensor(out=at(O_QX, 1024, 8), in0=at(O_QX, 1024, 8), scalar=G_DK ** -0.5,
                                                 in1=at(O_Q, 2048, 8)[:, :, P:T], op0=ALU.mult,
                                                 op1=ALU.mult).then_inc(s_ke, 1)
                        dve.wait_ge(s_kexp, 5)
                        dve.tensor_tensor(at(O_KX, 1024, 8), at(O_KX, 1024, 8), at(O_K, 2048, 8)[:, :, 0:P],
                                          ALU.mult).then_inc(s_ke, 1)
                    s0, n = g // G_PER * P, G_SUB * (g % G_PER + 1)
                    dve.wait_ge(s_kexp, exp_count(g))
                    ke = at(O_KE + 1024 * (g % 2), 1024, 8)[:, :, 0:n]
                    dve.tensor_tensor(ke, ke, at(O_K, 2048, 8)[:, :, s0:s0 + n], ALU.mult).then_inc(s_ke, 1)
                r0 = SLAB0["r", 1]
                for b in range(KB):
                    k_mul(b)
                    lo(2 * b % 4, r0 + 2 * b + 4)
                    lo((2 * b + 1) % 4, r0 + 2 * b + 5)
                dve.wait_ge(s_att_ps, T // G_SUB + 1)
                for hp in range(2):
                    dve.tensor_tensor(at(O_ATT + 512 * hp, 512, 2), bank(3 + hp, 512, 2),
                                      tri01[:, :].unsqueeze(1).broadcast_to([P, 2, T]), ALU.mult).then_inc(s_att, 1)
                    dve.tensor_tensor(at(O_ATT + 1024 + 512 * hp, 512, 2)[:, :, P:T], bank(5 + hp, 512, 2)[:, :, P:T],
                                      tri01[:, 0:P].unsqueeze(1).broadcast_to([P, 2, P]), ALU.mult).then_inc(s_att, 1)
                head_norm(G_HEADS, 4, G_OH, O_B, O_R, FILL["y", 1], 2)
                residual(1)

            def tk(o, n, k=None):
                return at(K_TK + o, n, k)
            s0, s1 = tk(0, 256, 2), tk(256, 256, 2)
            c0, c1 = tk(512, 256), tk(768, 256)
            sv = tk(1024, 32, 2)
            si = tk(1056, 32).bitcast(U32).rearrange("p (c k) -> p c k", c=2)
            sif = tk(1088, 32)
            ci = tk(1120, 16).bitcast(U32)
            cij = tk(1136, 32).bitcast(U32)
            cijf = tk(1168, 32)
            tv = tk(1200, 16)
            pick = tk(1216, 512)

            tk_count = [0]

            def tk_chain(ins):
                ins.then_inc(s_tk, 1)
                tk_count[0] += 1
                dve.wait_ge(s_tk, tk_count[0])

            def topk_steps(i):
                src = at(K_SC + 256 * i, 256) if isinstance(i, int) else big[:, bass.ds(i * 256 + K_SC, 256)]
                yield lambda: tk_chain(dve.tensor_copy(tk(0, 256), src))
                for p in range(2):
                    yield lambda p=p: tk_chain(dve.max(sv[:, p, 0:8], s0[:, p, :]))
                    yield lambda p=p: tk_chain(dve.max_index(si[:, p, 0:8], sv[:, p, 0:8], s0[:, p, :]))
                    yield lambda p=p: tk_chain(dve.match_replace(s1[:, p, :], sv[:, p, 0:8], s0[:, p, :], NEG))
                    yield lambda p=p: tk_chain(dve.max(sv[:, p, 8:16], s1[:, p, :]))
                    yield lambda p=p: tk_chain(dve.max_index(si[:, p, 8:16], sv[:, p, 8:16], s1[:, p, :]))
                yield lambda: tk_chain(dve.tensor_tensor(
                    c0.rearrange("p (i j) -> p i j", i=TOPK),
                    sv[:, 0, :].unsqueeze(2).broadcast_to([P, TOPK, TOPK]),
                    sv[:, 1, :].unsqueeze(1).broadcast_to([P, TOPK, TOPK]), ALU.add))
                yield lambda: tk_chain(dve.max(tv[:, 0:8], c0))
                yield lambda: tk_chain(dve.max_index(ci[:, 0:8], tv[:, 0:8], c0))
                yield lambda: tk_chain(dve.match_replace(c1, tv[:, 0:8], c0, NEG))
                yield lambda: tk_chain(dve.max(tv[:, 8:16], c1))
                yield lambda: tk_chain(dve.max_index(ci[:, 8:16], tv[:, 8:16], c1))
                yield lambda: tk_chain(dve.tensor_scalar(cij[:, 0:16], ci, 4, None, ALU.logical_shift_right))
                yield lambda: tk_chain(dve.tensor_scalar(cij[:, 16:32], ci, 15, None, ALU.bitwise_and))
                yield lambda: tk_chain(dve.tensor_copy(cijf, cij))
                yield lambda: tk_chain(dve.tensor_copy(sif, tk(1056, 32).bitcast(U32)))
                yield lambda: tk_chain(dve.tensor_tensor(
                    pick.rearrange("p (a j) -> p a j", j=TOPK), cijf.unsqueeze(2).broadcast_to([P, 32, TOPK]),
                    iota[:, 0:TOPK].unsqueeze(1).broadcast_to([P, 32, TOPK]), ALU.is_equal))
                yield lambda: tk_chain(dve.tensor_tensor(
                    pick.rearrange("p (c k j) -> p c k j", c=2, j=TOPK),
                    pick.rearrange("p (c k j) -> p c k j", c=2, j=TOPK),
                    sif.rearrange("p (c j) -> p c j", c=2).unsqueeze(2).broadcast_to([P, 2, TOPK, TOPK]), ALU.mult))
                if isinstance(i, int):
                    de, dc = e12[:, :, i, :], cv[:, i, :]
                else:
                    de = e12[:, :, bass.ds(i, 1), :].rearrange("p c a k -> p c (a k)")
                    dc = cv[:, bass.ds(i, 1), :].rearrange("p a k -> p (a k)")
                yield lambda: tk_chain(dve.tensor_reduce(de, pick.rearrange("p (c k j) -> p c k j", c=2, j=TOPK), AX.X, ALU.add))
                yield lambda: tk_chain(dve.tensor_copy(dc, tv))

            def experts(layer):
                norm(2 * layer + 1, FILL["k", layer], SLAB0["wq", layer])
                stream("wq", layer, 32)
                ubase = SLAB0["u", layer]
                ahead(ubase)
                dve.wait_ge(s_sc, 16 * (layer + 1) + 1)

                def u_turn(i, slabs, with_topk):
                    steps = list(topk_steps(i)) if with_topk else []
                    if with_topk:
                        dve.sem_clear(s_tk)
                        tk_count[0] = 0
                    per = -(-len(steps) // len(slabs))
                    for s in slabs:
                        lo(s % 4, i * 8 + (ubase + s))
                        for _ in range(per):
                            if steps:
                                steps.pop(0)()
                u_turn(0, range(4, 8), True)
                with dve.Fori(1, ITEMS) as i:
                    u_turn(i, range(8), True)
                chain(dve.tensor_copy(csum[:, :], cv[:, :, 0:1].rearrange("p i k -> p (i k)")))
                dve.tensor_tensor(cv[:, :, :], cv[:, :, :], csum[:, :].unsqueeze(2).broadcast_to([P, ITEMS, TOPK]),
                                  ALU.subtract).then_inc(s_cvs, 1)
                lo(0, ubase + 8 * ITEMS)
                lo(1, ubase + 8 * ITEMS + 1)
                dve.wait_ge(s_cexp, layer + 1)
                chain(dve.tensor_reduce(csum[:, :], cv[:, :, :], AX.X, ALU.add))
                chain(dve.reciprocal(csum[:, :], csum[:, :]))
                dve.tensor_tensor(cv[:, :, :], cv[:, :, :], csum[:, :].unsqueeze(2).broadcast_to([P, ITEMS, TOPK]),
                                  ALU.mult).then_inc(s_slots, 1)
                for s in range(2, 8):
                    lo(s % 4, ubase + 8 * ITEMS + s)
                dve.wait_ge(s_jt_ps, layer + 1)
                dve.tensor_copy(jt[:, :, :].rearrange("p c t -> p (c t)"), bank(3))
                chain(dve.tensor_copy(rstd[:, :], bank(4, T)))
                for c in range(WPARTS):
                    chain(dve.tensor_copy(jw[:, c, :], rstd[:, :]))
                    if c < WPARTS - 1:
                        chain(dve.tensor_tensor(rstd[:, :], rstd[:, :], jw[:, c, :], ALU.subtract))

                def spread(part, i, k):
                    dve.wait_ge(s_hot_free, i * 8 + (sc_turns(layer, part) * 8 + 2 * (k + 1) + 2))
                    grid = at(HALF * T * part, HALF * T).rearrange("p (e t) -> p t e", t=T)
                    t0 = i * SC_TOKENS + 8 * k
                    dst = grid[:, t0:t0 + 8, :] if isinstance(i, int) else grid[:, bass.ds(t0, 8), :]
                    dve.tensor_tensor(dst, dst, bank(4 + k, 512, 8), ALU.mult).then_inc(s_g, 1)

                def scatter(part, i, s, first=False):
                    done = sc_turns(layer, part)
                    if s in (4, 6):
                        spread(part, i, (s - 4) // 2)
                    elif s in (0, 2) and not first:
                        spread(part, i - 1, s // 2 + 2)
                    dve.wait_ge(s_hot_free, i * 8 + (done * 8 + s + 1))
                    t0, b = i * SC_TOKENS + 4 * s, 4 * (s % 2)
                    num = jt[:, :, t0:t0 + 4] if isinstance(i, int) else jt[:, :, bass.ds(t0, 4)]
                    dve.tensor_tensor(key1[:, b:b + 4, :],
                                      iota[:, HALF * part:HALF * (part + 1)].unsqueeze(1).broadcast_to([P, 4, HALF]),
                                      num[:, 0, :].unsqueeze(2).broadcast_to([P, 4, HALF]),
                                      ALU.is_equal).then_inc(s_key1, 1)
                    dve.tensor_tensor(hot2[:, b:b + 4, :], iota[:, :].unsqueeze(1).broadcast_to([P, 4, P]),
                                      num[:, 1, :].unsqueeze(2).broadcast_to([P, 4, P]),
                                      ALU.is_equal).then_inc(s_hot2, 1)

                def scatter_rest(part):
                    for k in (2, 3):
                        spread(part, SC_TURNS - 1, k)

                dve.wait_ge(s_evac, BLOCK0["u", layer] + HALF)
                for s in range(8):
                    lo(s % 4, ubase + 8 * SC_FIRST + s)
                    scatter(0, 0, s, first=True)
                with dve.Fori(1, SC_TURNS) as i:
                    for s in range(8):
                        lo(s % 4, i * 8 + (ubase + 8 * SC_FIRST + s))
                        scatter(0, i, s)
                for s in range(4):
                    lo(s, ubase + 8 * (SC_FIRST + SC_TURNS) + s)
                scatter_rest(0)
                for s in range(4, 8):
                    lo(s % 4, ubase + 8 * (SC_FIRST + SC_TURNS) + s)
                with dve.Fori(SC_FIRST + SC_TURNS + 1, N_KEYS // 4) as i:
                    for s in range(8):
                        lo(s % 4, i * 8 + (ubase + s))

                vbase = SLAB0["vt", layer]
                lo(0, vbase)
                lo(1, vbase + 1)

                def c_lo(block_, m, buf):
                    dve.wait_ge(s_chi, m + 1)
                    src = at(block_ * T, T) if isinstance(block_, int) else big[:, bass.ds(block_ * T, T)]
                    dve.tensor_tensor(act_lo_t[:, buf, :], src, act_hi_t[:, buf, :].bitcast(F32),
                                      ALU.subtract).then_inc(s_clo, 1)
                m0 = COEFFS * layer
                for b in range(4):
                    c_lo(b, m0 + b, b)
                lo(2, vbase + 2)
                lo(3, vbase + 3)
                dve.wait_ge(s_evac, BLOCK0["u", layer] + N_KEYS)
                for s in range(8):
                    if s >= 4:
                        lo(s % 4, vbase + s)
                        c_lo(s, m0 + s, s)
                    scatter(1, 0, s, first=True)
                with dve.Fori(1, SC_TURNS) as i:
                    for s in range(8):
                        lo(s % 4, i * 8 + (vbase + s))
                        c_lo(i * 8 + s, i * 8 + (m0 + s), s)
                        scatter(1, i, s)
                scatter_rest(1)
                with dve.Fori(0, HALF // 8) as i:
                    for s in range(8):
                        lo(s % 4, i * 8 + (vbase + HALF + s))
                        c_lo(i * 8 + s, i * 8 + (m0 + HALF + s), s)
                with dve.Fori(HALF // 4, N_KEYS // 4) as i:
                    for s in range(8):
                        lo(s % 4, i * 8 + (vbase + s))
                        if s < 4:
                            c_lo(i * 4 + s, i * 4 + (m0 + HALF + s), s)
                dve.wait_ge(s_reload, 16 * (layer + 1))
                for c in range(4):
                    if c == 2 and layer == 0:
                        lo(0, SLAB0["qk", 1])
                        lo(1, SLAB0["qk", 1] + 1)
                    dve.wait_ge(s_used, vbase + 2 * N_KEYS - (4 if c < 2 else 0))
                    x = at(XT + 1024 * c, 1024)
                    dve.tensor_tensor(x, x, banks(2 * c, 2), ALU.add).then_inc(s_yadd, 1)

            even()
            experts(0)
            odd()
            experts(1)
            norm(4, None)

        @block.tensor
        def _(pe):
            def three(out, wh, wl, xh, xl, start=False, stop=False, **kw):
                pe.matmul(out, wh, xl, start=start, stop=False, **kw)
                pe.matmul(out, wl, xh, start=False, stop=False, **kw)
                return pe.matmul(out, wh, xh, start=False, stop=stop, **kw)

            def half_block(slot, n, b, half, fill=None):
                pe.wait_ge(s_lo, n + 1)
                for k in range(8):
                    kb = 8 * half + k
                    if fill is not None and kb % 4 == 0:
                        pe.wait_ge(s_alo, 4 * fill + kb // 4 + 1)
                    c = slice(P * k, P * (k + 1))
                    ins = three(ps[:, b, 0:T], w_hi[:, slot, c], w_lo[:, slot, c], act_hi_t[:, kb, :],
                                act_lo_t[:, kb, :], start=kb == 0, stop=kb == KB - 1)
                ins.then_inc(s_used, 1)

            def gemm(name, layer, nblocks, fill=None, between=None, strict=False):
                n0, b0 = SLAB0[name, layer], BLOCK0[name, layer]

                def blk(i, par, first=False):
                    if first and strict:
                        pe.wait_ge(s_evac, b0)
                    elif not (isinstance(i, int) and b0 + 2 * i + par < 2):
                        pe.wait_ge(s_evac, i * 2 + (b0 + par - 1))
                    for half in range(2):
                        s = 2 * par + half
                        half_block(s, i * 4 + (n0 + s), par, half, fill if first and par == 0 else None)
                blk(0, 0, True)
                blk(0, 1, True)
                if between:
                    between(0)
                with pe.Fori(1, nblocks // 2) as i:
                    blk(i, 0)
                    if between:
                        between(i * 2 - 1, 1)
                    blk(i, 1)
                    if between:
                        between(i * 2, 0)
                if between:
                    between(nblocks - 1)

            def v_groups(layer, ngroups, between=None):
                n0 = SLAB0["v", layer]
                for g in range(ngroups):
                    if g >= 2:
                        pe.wait_ge(s_vevac, 4 * layer + 2 * (g - 1))
                    for q in range(8):
                        pe.wait_ge(s_lo, n0 + 8 * g + q + 1)
                        for k in range(2):
                            kb = 2 * q + k
                            c = slice(512 * k, 512 * (k + 1))
                            for tb in range(TB):
                                t = slice(P * tb, P * (tb + 1))
                                out = ps[:, 3 + 2 * (g % 2) + tb, :]
                                pe.matmul(out, act_lo_t[:, kb, t], w_hi[:, q % 4, c], start=kb == 0, stop=False)
                                pe.matmul(out, act_hi_t[:, kb, t], w_lo[:, q % 4, c], start=False, stop=False)
                                ins = pe.matmul(out, act_hi_t[:, kb, t], w_hi[:, q % 4, c], start=False,
                                                stop=kb == KB - 1)
                        ins.then_inc(s_used, 1)
                    if between and g in between:
                        between[g]()

            def norm_sum(k, tiles=range(KB)):
                for j in tiles:
                    if j % 4 == 0:
                        pe.wait_ge(s_sq, SQ0[k] + j // 4 + 1)
                    ins = pe.matmul(ps[:, 2, 0:T], ones[:, :], at(HT + T * j, T), start=j == 0, stop=j == KB - 1)
                if tiles[-1] == KB - 1:
                    ins.then_inc(s_sum, 1)

            def tile_sum(k):
                def add(b, par=0):
                    pe.wait_ge(s_sq, b + (SQ0[k] + 1))
                    if isinstance(b, int):
                        ins = pe.matmul(ps[:, 2, 0:T], ones[:, :], at(HT + T * b, T), start=b == 0, stop=b == KB - 1)
                        if b == KB - 1:
                            ins.then_inc(s_sum, 1)
                    else:
                        pe.matmul(ps[:, 2, 0:T], ones[:, :], big[:, bass.ds(b * T + HT, T)], start=False, stop=False)
                return add

            def even():
                pe.wait_ge(s_pool, 1)
                norm_sum(0)
                gemm("qk", 0, 8, fill=FILL["h", 0])
                pe.wait_ge(s_pool, POOL_CONSTS)
                pe.wait_ge(s_consts, 16 * N_CONSTS)
                wg = at(E_WG, 16 * WG_W, 16)
                for j in range(KB):
                    ins = pe.matmul(ps[0:WG_W, 7, 0:T], wg[:, j, :], at(HT + T * j, T), start=j == 0, stop=j == KB - 1)
                ins.then_inc(s_gates_ps, 1)
                v_groups(0, 2)
                gemm("o", 0, 8)
                gemm("p", 0, 8)
                sel = big[0:4, E_SEL:E_SEL + 1024].rearrange("p (h t) -> p h t", h=4)
                rows = lambda r: big[0:4, E_ROWS + T * r:E_ROWS + T * (r + 1)]

                def scores(h):
                    if h == 0:
                        pe.wait_ge(s_rows, 1)
                        pe.wait_ge(s_vevac, 4)
                        pe.wait_ge(s_evac, BLOCK0["out", 0])
                    if h >= 2:
                        pe.wait_ge(s_dm, h - 1)
                    for o, s, t0 in ((0, 0, 0), (T, P, P)):
                        out = ps[:, 3 + h % 2, o:o + T - t0]
                        pe.matmul(out, sel[:, h, 0:P], rows(2)[:, t0:T], start=True, stop=False)
                        ins = pe.matmul(out, rows(4)[:, s:s + P], sel[:, h, t0:T], start=False, stop=True)
                    ins.then_inc(s_d_ps, 1)
                    if h >= 2:
                        pe.wait_ge(s_s, h - 1)
                    for o, s, t0 in ((0, 0, 0), (T, P, P)):
                        ins = pe.matmul(ps[:, 5 + h % 2, o:o + T - t0], at(E_K + T * h + s, P),
                                        at(E_Q + T * h + t0, T - t0), start=True, stop=True)
                    ins.then_inc(s_s_ps, 1)

                def outputs(h):
                    if h == 0:
                        pe.wait_ge(s_floor, 1)
                    else:
                        pe.wait_ge(s_hn, h)
                    pe.wait_ge(s_s, h + 1)
                    w = at(E_PE + 384 * h, 384)
                    for vt in range(2):
                        v = [at(E_V + 1024 * sb_ + 256 * h + P * vt, P) for sb_ in range(2)]
                        pe.matmul(ps[:, 7, T * vt:T * vt + T], v[0], w[:, 0:T], start=True, stop=True)
                        pe.matmul(ps[:, 7, T * vt + P:T * vt + T], v[1], w[:, T:384], start=False, stop=False,
                                  skip_group_check=True)
                    pe.matmul(ps[:, 2, 0:T], ones[:, :], w[:, 0:T], start=True, stop=True)
                    pe.matmul(ps[:, 2, P:T], ones[:, :], w[:, T:384], start=False, stop=False, skip_group_check=True)
                    pe.matmul(ps[:, 2, T:2 * T], sel[:, h, 0:P], rows(5), start=True, stop=True).then_inc(s_num_ps, 1)
                for h in range(M_HEADS):
                    scores(h)
                    if h:
                        outputs(h - 1)
                outputs(M_HEADS - 1)
                for h in range(M_HEADS):
                    pe.wait_ge(s_hsq, h + 1)
                    for vt in range(2):
                        ins = pe.matmul(ps[:, 3 + h // 2, T * (h % 2):T * (h % 2) + T], ones[:, :],
                                        at(E_V + 512 * h + T * vt, T), start=vt == 0, stop=vt == 1)
                    if h % 2:
                        ins.then_inc(s_ssq_ps, 1)
                pe.wait_ge(s_s, M_HEADS)
                for j in range(8):
                    g, dt = j // 2, j % 2
                    pe.wait_ge(s_mixed, g + 1)
                    b = (0, 0, 1, 1, 5, 5, 6, 6)[j]
                    for kc in range(2):
                        ins = pe.matmul(ps[:, b, T * (j % 2):T * (j % 2) + T],
                                        at(E_WPOOL + 512 * g + 256 * kc + P * dt, P),
                                        at(E_PT + E_PW * (2 * g + kc) + E_PAD, T), start=kc == 0, stop=kc == 1)
                    ins.then_inc(s_pool_ps, 1)
                pe.wait_ge(s_pool_out, 8)
                gemm("out", 0, 16, fill=FILL["y", 0], strict=True, between=tile_sum(1))

            def odd():
                gemm("qk", 1, 16, fill=FILL["h", 1])
                pe.wait_ge(s_consts, 16 * (N_CONSTS + 2))
                for j in range(KB):
                    ins = pe.matmul(ps[0:G_RANK, 7, 0:T], at(O_WGL + G_RANK * j, G_RANK), at(HT + T * j, T),
                                    start=j == 0, stop=j == KB - 1)
                ins.then_inc(s_gl_ps, 1)

                def gate(r):
                    pe.wait_ge(s_gl, 1)
                    if r:
                        pe.wait_ge(s_bias, 1)
                    for j in range(4 * r, 4 * r + 4):
                        b = 7 if j % 4 < 2 else 2
                        ins = pe.matmul(ps[:, b, T * (j % 2):T * (j % 2) + T],
                                        big[0:G_RANK, O_WGATE + P * j:O_WGATE + P * (j + 1)],
                                        big[0:G_RANK, O_GLT:O_GLT + T], start=True, stop=True)
                    ins.then_inc(s_pre_ps, 1)
                v_groups(1, 4, {0: lambda: gate(0), 1: lambda: gate(1)})
                pe.wait_ge(s_vevac, 12)
                for b in range(3, 7):
                    for o in range(0, 512, P):
                        pe.matmul(ps[:, b, o:o + P], zrow[0:1, :], zrow[0:1, :], start=True, stop=True)

                def group(g):
                    if g == 2:
                        pe.wait_ge(s_ke, 5)
                        for j in range(8):
                            c = T * (j // 2 % 2) + P
                            ins = pe.matmul(ps[:, 3 + j // 4, c:c + P], at(O_KX, 1024, 8)[:, j, :],
                                            at(O_QX, 1024, 8)[:, j, :], start=j % 2 == 0, stop=j % 2 == 1)
                        ins.then_inc(s_att_ps, 1)
                    sb_, n = g // G_PER, G_SUB * (g % G_PER + 1)
                    pe.wait_ge(s_ke, exp_count(g))
                    ke = at(O_KE + 1024 * (g % 2), 1024, 8)
                    qe = at(O_QE, 2048, 8)
                    for j in range(8):
                        c = T * (j // 2 % 2) + G_SUB * g
                        ins = pe.matmul(ps[0:n, 3 + 2 * sb_ + j // 4, c:c + G_SUB], ke[:, j, 0:n],
                                        qe[:, j, G_SUB * g:G_SUB * (g + 1)], start=j % 2 == 0, stop=j % 2 == 1)
                    ins.then_inc(s_att_ps, 1)
                r0 = SLAB0["r", 1]
                for b in range(KB):
                    pe.wait_ge(s_evac, BLOCK0["r", 1] + b - 1)
                    for half in range(2):
                        half_block((2 * b + half) % 4, r0 + 2 * b + half, b % 2, half)
                    group(b)

                def o_ssq(h):
                    pe.wait_ge(s_osq, h + 1)
                    for vt in range(4):
                        ins = pe.matmul(o_sum(h), ones[:, :], at(O_KE + 1024 * h + T * vt, T), start=vt == 0,
                                        stop=vt == 3)
                    ins.then_inc(s_ssq_ps, 1)
                pe.wait_ge(s_evac, BLOCK0["out", 1])
                pe.wait_ge(s_att, 4)
                for h in range(G_HEADS):
                    if h >= 2:
                        pe.wait_ge(s_o, h - 1)
                    for vt in range(4):
                        b, o = O_BANK[h % 2] + vt // 2, T * (vt % 2)
                        v = [at(O_V + 2048 * sb_ + 512 * h + P * vt, P) for sb_ in range(2)]
                        w = [at(O_ATT + 1024 * sb_ + T * h, T) for sb_ in range(2)]
                        pe.matmul(ps[:, b, o:o + T], v[0], w[0], start=True, stop=True)
                        ins = pe.matmul(ps[:, b, o + P:o + T], v[1], w[1][:, P:T], start=False, stop=False,
                                        skip_group_check=True)
                    ins.then_inc(s_o_ps, 1)
                    if h:
                        o_ssq(h - 1)
                o_ssq(G_HEADS - 1)
                pe.wait_ge(s_o, G_HEADS)
                gemm("out", 1, 16, fill=FILL["y", 1], strict=True, between=tile_sum(3))

            def experts(layer):
                pe.wait_ge(s_keys, 16 * (layer + 1))

                def key_scores(q, par=None):
                    par = q % 2 if par is None else par
                    pe.wait_ge(s_evac, q + (BLOCK0["wq", layer] + 1))
                    if not (isinstance(q, int) and q < 2):
                        pe.wait_ge(s_sc, q + 16 * layer)
                    rhs = at(K_KEYS + P * q, P) if isinstance(q, int) else big[:, bass.ds(q * P + K_KEYS, P)]
                    for tb in range(TB):
                        ins = pe.matmul(ps[:, 2 + par, P * tb:P * (tb + 1)], at(K_QS + T * par + P * tb, P), rhs,
                                        start=True, stop=True)
                    ins.then_inc(s_sc_ps, 1)
                gemm("wq", layer, 16, fill=FILL["k", layer], between=key_scores, strict=True)

                ub, u0_ = BLOCK0["u", layer], SLAB0["u", layer]

                def u_turn(i, after=None):
                    for b in range(4):
                        pe.wait_ge(s_evac, i * 4 + (ub + b - 1))
                        for half in range(2):
                            s = 2 * b + half
                            half_block(s % 4, i * 8 + (u0_ + s), b % 2, half)
                            if after:
                                after(s)

                def slots(s):
                    if s != 3:
                        return
                    pe.wait_ge(s_slots, layer + 1)
                    for c in range(2):
                        for tb in range(TB):
                            pe.transpose(ps[:, 3, T * c + P * tb:T * c + P * (tb + 1)],
                                         e12[:, c, HEADS * tb:HEADS * (tb + 1), :].rearrange("p h k -> p (h k)"),
                                         ident[:, :])
                    for tb in range(TB):
                        ins = pe.transpose(ps[:, 4, P * tb:P * (tb + 1)],
                                           cv[:, HEADS * tb:HEADS * (tb + 1), :].rearrange("p h k -> p (h k)"),
                                           ident[:, :])
                    ins.then_inc(s_jt_ps, 1)

                def scatter(part, i, s):
                    done = sc_turns(layer, part)
                    if s % 2 == 0:
                        pe.wait_ge(s_g, i * 4 + (done * 4 + s // 2 + 1))
                    pe.wait_ge(s_hot2, i * 8 + (done * 8 + s + 1))
                    pe.wait_ge(s_hot1, i * 8 + (done * 8 + s + 1))
                    for x in range(4):
                        t = 4 * (s % 2) + x
                        for c in range(WPARTS):
                            ins = pe.matmul(ps[:, 4 + s // 2, HALF * t:HALF * (t + 1)], hot2[:, t, :],
                                            hot1[:, t, c, :], start=c == 0, stop=c == WPARTS - 1)
                    ins.then_inc(s_hot_free, 1)

                with pe.Fori(0, SC_FIRST - 1) as i:
                    u_turn(i)
                u_turn(SC_FIRST - 1, slots)
                with pe.Fori(0, SC_TURNS) as i:
                    u_turn(i + SC_FIRST, lambda s: scatter(0, i, s))
                with pe.Fori(SC_FIRST + SC_TURNS, N_KEYS // 4) as i:
                    u_turn(i)

                def open_banks(first):
                    for b in range(first, first + 4):
                        pe.matmul(ps[:, b, 0:2], zrow[0:1, :], zrow[0:1, 0:2], start=True, stop=False,
                                  skip_group_check=True)
                v0, m0 = SLAB0["vt", layer], COEFFS * layer

                def v_slab(i, s, half, buf):
                    pe.wait_ge(s_lo, i * 8 + (v0 + s + 1))
                    for k in range(8):
                        j = 8 * half + k
                        c = slice(P * k, P * (k + 1))
                        ins = three(ps[:, j // 2, T * (j % 2):T * (j % 2) + T], w_hi[:, s % 4, c],
                                    w_lo[:, s % 4, c], act_hi_t[:, buf, :], act_lo_t[:, buf, :],
                                    skip_group_check=True)
                    ins.then_inc(s_used, 1)
                pe.wait_ge(s_evac, ub + N_KEYS)
                open_banks(0)
                with pe.Fori(0, SC_TURNS) as i:
                    for s in range(8):
                        pe.wait_ge(s_clo, i * 8 + (m0 + s + 1))
                        v_slab(i, s, 0, s)
                        scatter(1, i, s)
                pe.wait_ge(s_g, SC_TURNS * 8 * (layer + 1) + 4)
                open_banks(4)
                with pe.Fori(SC_TURNS, 2 * SC_TURNS) as i:
                    for s in range(8):
                        pe.wait_ge(s_clo, i * 8 + (m0 + s + 1))
                        v_slab(i, s, 1, s)

                def rest(i, before_last=None):
                    for s in range(8):
                        if s < 4:
                            pe.wait_ge(s_clo, i * 4 + (m0 + HALF + s + 1))
                        if s == 7 and before_last:
                            before_last()
                        v_slab(i, s, s // 4, s % 4)
                with pe.Fori(HALF // 4, N_KEYS // 4 - 1) as i:
                    rest(i)

                def early_sum():
                    pe.wait_ge(s_yadd, 4 * layer + 2)
                    norm_sum(2 * layer + 2, range(8))
                rest(N_KEYS // 4 - 1, early_sum)
                norm_sum(2 * layer + 2, range(8, KB))

            even()
            experts(0)
            odd()
            experts(1)


INPUTS = ["xT", "dense0", "dense1", "u0", "u1", "v_tab", "keys", "gains", "gates_in", "w_pool", "inv_count",
          "w_glow", "w_gate"]


def lay_out(x, e_norm, e_w_in, e_b_igate, e_b_fgate, e_head_gain, e_w_pool, e_pool_scale, e_w_out,
            o_norm, o_w_in, o_w_gate, o_b_gate, o_head_gain, o_w_out,
            f_norm, f_w_q, f_sub_keys, f_u, f_v, final_norm):
    def blocks(w):
        n = w.shape[1] // P
        return w.reshape(2, 8, P, n, P).transpose(3, 0, 2, 1, 4).reshape(2 * n, P, SLAB)

    def groups(w):
        n = w.shape[1] // 512
        return w.reshape(8, 2, P, n, 512).transpose(3, 0, 2, 1, 4).reshape(8 * n, P, SLAB)

    def table(u):
        return u.reshape(N_KEYS, P, 2, 8, P).transpose(0, 2, 4, 3, 1).reshape(2 * N_KEYS, P, SLAB)

    def column(g):
        return g.reshape(-1, P).T

    a = np.ascontiguousarray
    we, wo = e_w_in[0], o_w_in[0]
    dense0 = np.concatenate([blocks(we[:, 0:1024]), groups(we[:, 1024:2048]), blocks(we[:, 2048:3072]),
                             blocks(we[:, 3080:4104]), blocks(e_w_out[0]), blocks(f_w_q[0])])
    dense1 = np.concatenate([blocks(wo[:, 0:2048]), groups(wo[:, 2048:4096]), blocks(wo[:, 4096:6144]),
                             blocks(o_w_out[0]), blocks(f_w_q[1])])
    gains = np.concatenate([column(g) for g in (e_norm[0], f_norm[0], o_norm[0], f_norm[1], final_norm,
                                                e_head_gain[0], e_pool_scale[0], o_head_gain[0], o_b_gate[0])], 1)
    gains = np.concatenate([gains, np.zeros((P, P - gains.shape[1]), gains.dtype)], 1)
    gates = np.zeros((P, KB + 1, 8), we.dtype)
    gates[:, 0:KB, :] = we[:, 3072:3080].reshape(KB, P, 8).transpose(1, 0, 2)
    gates[0:4, KB, 0] = e_b_igate[0]
    gates[0:4, KB, 1] = e_b_fgate[0]
    inv = np.stack([1.0 / np.minimum(np.arange(1, T + 1), w) for w in POOL_WINDOWS]).astype(np.float32)
    return {
        "xT": a(x[0].T.reshape(KB, P, T).transpose(1, 0, 2)),
        "dense0": a(dense0), "dense1": a(dense1), "u0": a(table(f_u[0])), "u1": a(table(f_u[1])),
        "v_tab": a(f_v), "keys": a(f_sub_keys.transpose(0, 4, 1, 2, 3).reshape(2, P, 2048)),
        "gains": a(gains), "gates_in": gates,
        "w_pool": a(e_w_pool[0].reshape(4, 2, P, POOL_GROUP).transpose(2, 0, 1, 3).reshape(P, 2048)),
        "inv_count": a(np.broadcast_to(inv.reshape(1, 1024), (P, 1024))),
        "w_glow": a(wo[:, 6144:6160].reshape(KB, P, G_RANK).transpose(1, 0, 2).reshape(P, KB * G_RANK)),
        "w_gate": a(o_w_gate[0]),
    }


def kernel(**inputs):
    import concourse.bacc as bacc
    from concourse.bass_utils import run_bass_kernel_spmd as run
    arrays = lay_out(**{k: np.asarray(v) for k, v in inputs.items()})
    nc = bacc.Bacc("TRN2", target_bir_lowering=False, num_devices=1)
    args = [nc.dram_tensor(f"in_{n}", arrays[n].shape, F32, kind="ExternalInput").ap() for n in INPUTS]
    out = nc.dram_tensor("out_0", (P, KB, T), F32, kind="ExternalOutput").ap()
    decoder_kernel(nc, *args, out)
    r = run(nc, [{f"in_{n}": arrays[n] for n in INPUTS}], core_ids=[0])
    got = np.asarray(r.results[0]["out_0"])
    return np.ascontiguousarray(got.transpose(2, 1, 0).reshape(1, T, D))
```

```python
from contextlib import ExitStack

import concourse.bass as bass
import numpy as np
from concourse import mybir

F32 = mybir.dt.float32
F32R = mybir.dt.float32r
BF16 = mybir.dt.bfloat16
U32 = mybir.dt.uint32
ALU = mybir.AluOpType
ACT = mybir.ActivationFunctionType
AX = mybir.AxisListType

P = 128
D = 2048
T = 256
TB = T // P
KB = D // P
EPS = 1e-6

M_HEADS, M_DK, M_DV = 4, 128, 256
M_WIDTH = M_HEADS * M_DV
POOL_WINDOWS = (2, 4, 8, 16)
POOL_GROUP = 256
G_HEADS, G_DK, G_DV = 4, 256, 512
G_RANK = 16
G_TAU = 16.0
G_SUB = 16

N_KEYS = 128
HEADS = 8
TOPK = 16
ITEMS = TB * HEADS
PARTS = 2
HALF = N_KEYS // PARTS
SC_TOKENS = 32
SC_TURNS = T // SC_TOKENS
WPARTS = 3
PIECES = 8
PIECE = KB * T // PIECES
SC_FIRST = HALF // 4 + 1
COEFFS = 2 * HALF + (N_KEYS - HALF)

SLAB = 1024
RING = 4
NEG = -1e30

PHASES = [("qk", 0, 16), ("v", 0, 16), ("p", 0, 16), ("o", 0, 16), ("out", 0, 32), ("wq", 0, 32),
          ("u", 0, 256), ("vt", 0, 256),
          ("qk", 1, 32), ("r", 1, 32), ("v", 1, 32), ("out", 1, 32), ("wq", 1, 32),
          ("u", 1, 256), ("vt", 1, 256)]
SLAB0, _n = {}, 0
for _name, _layer, _k in PHASES:
    SLAB0[_name, _layer] = _n
    _n += _k
BLOCK0, _n = {}, 0
for _name, _layer, _k in PHASES:
    BLOCK0[_name, _layer] = _n
    if _name not in ("v", "vt"):
        _n += _k // 2
DENSE = [sum(k for n, l, k in PHASES if l == layer and n not in ("u", "vt")) for layer in range(2)]

XT, HT = 0, 4096
E_Q, E_K, E_V, E_SO = 8192, 9216, 10240, 12288
E_PAD, E_PW = 16, 16 + T
E_PT, E_S2, E_S4 = 14336, 16512, 18688
E_PE, E_MASK, E_WPOOL, E_ICNT, E_WG = 20864, 22400, 22912, 24960, 25984
E_ROWS, E_SEL = 26560, 28352
O_Q, O_K, O_V, O_R, O_B, O_KE, O_QE, O_ATT = 8192, 10240, 12288, 16384, 20480, 22528, 26624, 28672
O_KX, O_QX = O_KE + 2048, O_KE + 3072
O_WGATE, O_WGL, O_GLT = 26624, 27648, 27904
K_QS, K_TK, K_SC, K_KEYS = 20480, 20992, 24576, 30720


def decoder_kernel(nc, xT, dense0, dense1, u0, u1, v_tab, keys, gains, gates_in, w_pool, inv_count,
                   w_glow, w_gate, out):
    ctx = ExitStack()
    with ctx:
        def sb(name, shape, dt=F32):
            return ctx.enter_context(nc.sbuf_tensor(name, shape, dt))

        def S(name):
            return ctx.enter_context(nc.semaphore(name))

        spill = nc.dram_tensor("x_spill", (P, KB * T), F32).ap()

        big = sb("big", [P, 32768])
        act_hi_t = sb("act_hi_t", [P, KB, T], F32R)
        act_lo_t = sb("act_lo_t", [P, KB, T], F32R)
        ring_base = nc.sbuf_base
        w_raw = sb("w_raw", [P, RING, SLAB])
        w_lo = nc.alloc_sbuf_tensor_at("w_lo", [P, RING, SLAB], F32R, offset=ring_base)
        w_hi = sb("w_hi", [P, RING, SLAB], F32R)
        gain = sb("gain", [P, 128])
        gbias = sb("gbias", [P, 2])
        ones = sb("ones", [P, P])
        iota = sb("iota", [P, P])
        ident = sb("ident", [P, P])
        zrow = sb("zrow", [1, P])
        epst = sb("epst", [P, 1])
        credit = sb("credit", [1, 2])
        tri01 = sb("tri01", [P, T])
        stdv_base = nc.sbuf_base
        stdv = sb("stdv", [P, T])
        key1 = nc.alloc_sbuf_tensor_at("key1", [P, 8, HALF], BF16, offset=stdv_base)
        rstd = sb("rstd", [P, T])
        e12_base = nc.sbuf_base
        e12 = sb("e12", [P, 2, ITEMS, TOPK])
        cv = sb("cv", [P, ITEMS, TOPK])
        hot1 = nc.alloc_sbuf_tensor_at("hot1", [P, 8, WPARTS, HALF], BF16, offset=e12_base)
        hot2 = sb("hot2", [P, 8, P], BF16)
        csum = sb("csum", [P, ITEMS])
        jt = sb("jt", [P, 2, T])
        jw = sb("jw", [P, WPARTS, T], BF16)
        ps = ctx.enter_context(nc.psum_tensor("ps", [P, 8, 512], F32))

        s_x = [S(f"s_x{c}") for c in range(4)]
        s_landed = [S(f"s_landed{s}") for s in range(RING)]
        s_gain = S("s_gain")
        s_consts = S("s_consts")
        s_spill = S("s_spill")
        s_reload = S("s_reload")
        s_keys = S("s_keys")
        s_out = S("s_out")
        s_hi = S("s_hi")
        s_lo = S("s_lo")
        s_used = S("s_used")
        s_evac = S("s_evac")
        s_vevac = S("s_vevac")
        s_sq = S("s_sq")
        s_acc = S("s_acc")
        s_sum = S("s_sum")
        s_std = S("s_std")
        s_rstd = S("s_rstd")
        s_h = S("s_h")
        s_ahi = S("s_ahi")
        s_alo = S("s_alo")
        s_yadd = S("s_yadd")
        s_vec = S("s_vec")
        s_tk = S("s_tk")
        s_act = S("s_act")
        s_pool = S("s_pool")
        s_pool_turn = S("s_pool_turn")
        s_gates_ps = S("s_gates_ps")
        s_grow = S("s_grow")
        s_grow_act = S("s_grow_act")
        s_rows = S("s_rows")
        s_floor = S("s_floor")
        s_d_ps = S("s_d_ps")
        s_dm = S("s_dm")
        s_p = S("s_p")
        s_s_ps = S("s_s_ps")
        s_s = S("s_s")
        s_num_ps = S("s_num_ps")
        s_hn = S("s_hn")
        s_hsq = S("s_hsq")
        s_ssq_ps = S("s_ssq_ps")
        s_hstd = S("s_hstd")
        s_mixed = S("s_mixed")
        s_pool_ps = S("s_pool_ps")
        s_pool_out = S("s_pool_out")
        s_y = S("s_y")
        s_gl_ps = S("s_gl_ps")
        s_gl = S("s_gl")
        s_pre_ps = S("s_pre_ps")
        s_la = S("s_la")
        s_decay = S("s_decay")
        s_bias = S("s_bias")
        s_la_act = S("s_la_act")
        s_karg = S("s_karg")
        s_kexp = S("s_kexp")
        s_ke = S("s_ke")
        s_att_ps = S("s_att_ps")
        s_att = S("s_att")
        s_o_ps = S("s_o_ps")
        s_o = S("s_o")
        s_osq = S("s_osq")
        s_silu = S("s_silu")
        s_sc_ps = S("s_sc_ps")
        s_sc = S("s_sc")
        s_cvs = S("s_cvs")
        s_cexp = S("s_cexp")
        s_slots = S("s_slots")
        s_jt_ps = S("s_jt_ps")
        s_jt = S("s_jt")
        s_key1 = S("s_key1")
        s_hot1 = S("s_hot1")
        s_hot2 = S("s_hot2")
        s_hot_free = S("s_hot_free")
        s_g = S("s_g")
        s_chi = S("s_chi")
        s_clo = S("s_clo")

        def at(o, n, k=None):
            a = big[:, o:o + n]
            return a if k is None else a.rearrange("p (k t) -> p k t", k=k)

        def pool_bank(j):
            return ps[:, (5, 6, 7, 2)[j // 2], T * (j % 2):T * (j % 2) + T]

        SCORES_AT, OUTPUTS_AT = (0, 1, 3, 5), (2, 4, 6, 7)

        V_BANKS = ((0, 1), (2, 7))
        O_BANK = 3

        def o_sum(h):
            return ps[:, 5 + h % 2, 0:T]

        GLA_AT = 7
        KE_BUFS = 4

        def ke_buf(g):
            return at(O_V + 1024 * (g % KE_BUFS), 1024, 8)

        G_PER = P // G_SUB

        def exp_count(g):
            return g + (2 if g < 2 else 4)

        def att_count(g):
            return g + (1 if g < 2 else 2)

        def sc_turns(layer, part):
            return (layer * PARTS + part) * SC_TURNS

        def bank(b, n=512, k=None):
            a = ps[:, b, 0:n]
            return a if k is None else a.rearrange("p (k t) -> p k t", k=k)

        def banks(b, nb):
            return ps[:, b:b + nb, :].rearrange("p b n -> p (b n)")

        G_NORM = [0, 16, 32, 48, 64]
        G_EH, G_PS, G_OH, G_BG = 80, 88, 96, 112
        N_CONSTS = 5
        POOL_CONSTS = 17
        WG_W = 36

        SQ_TILES = {0: 4, 1: KB, 2: 4, 3: KB, 4: 4}
        SQ0 = {k: sum(SQ_TILES[j] for j in range(k)) for k in range(5)}

        CHUNKS = KB // 2
        FILL = {("h", 0): 0, ("y", 0): 1, ("k", 0): 2, ("h", 1): 3, ("y", 1): 4, ("k", 1): 5}

        block = ctx.enter_context(nc.Block())

        @block.sync
        def _(sp):
            for c in range(4):
                sp.dma_start(at(XT + 1024 * c, 1024, 4), xT[:, 4 * c:4 * c + 4, :]).then_inc(s_x[c], 16)
            sp.dma_start(gain[:, :], gains).then_inc(s_gain, 16)

            def load(slot, n, src, wait=True):
                if wait:
                    sp.wait_ge(s_used, n - (RING - 1))
                sp.dma_start(w_raw[:, slot, :], src).then_inc(s_landed[slot], 16)

            for layer, (dense, u) in enumerate(((dense0, u0), (dense1, u1))):
                n0 = SLAB0["qk", layer]
                if layer == 0:
                    for s in range(RING):
                        load(s, s, dense[s], wait=False)
                with sp.Fori(1 if layer == 0 else 0, DENSE[layer] // RING) as i:
                    for s in range(RING):
                        load(s, i * RING + (n0 + s), dense[bass.ds(i * RING + s, 1)].rearrange("a p n -> (a p) n"))
                n0 = SLAB0["u", layer]
                with sp.Fori(0, 2 * N_KEYS // RING) as i:
                    for s in range(RING):
                        load(s, i * RING + (n0 + s), u[bass.ds(i * RING + s, 1)].rearrange("a p n -> (a p) n"))
                n0 = SLAB0["vt", layer]
                vrows = v_tab[layer].rearrange("(e p) (h n) -> e p h n", p=P, h=2)
                for h in range(2):
                    with sp.Fori(0, HALF // RING) as i:
                        for s in range(RING):
                            load(s, i * RING + (n0 + HALF * h + s),
                                 vrows[bass.ds(i * RING + s, 1), :, h, :].rearrange("a p n -> (a p) n"))
                with sp.Fori(HALF // 4, N_KEYS // 4) as i:
                    for s in range(2 * RING):
                        load(s % RING, i * 2 * RING + (n0 + s),
                             vrows[bass.ds(i * RING + s % RING, 1), :, s // RING, :].rearrange("a p n -> (a p) n"))
            for c in range(4):
                sp.wait_ge(s_h, CHUNKS * 4 + 2 * (c + 1))
                sp.dma_start(out[:, 4 * c:4 * c + 4, :], at(HT + 1024 * c, 1024, 4)).then_inc(s_out, 16)
            sp.wait_ge(s_out, 64)

        @block.gpsimd
        def _(pool):
            count = [0]

            def step(ins):
                ins.then_inc(s_pool, 1)
                count[0] += 1
                pool.wait_ge(s_pool, count[0])

            step(pool.memset(ones[:, :], 1.0))
            step(pool.memset(epst[:, :], EPS))
            step(pool.memset(at(E_WG, 16 * WG_W), 0.0))
            wg = at(E_WG, 16 * WG_W, 16)
            pool.dma_start(wg[:, :, 0:4], gates_in[:, 0:KB, 0:4]).then_inc(s_consts, 16)
            pool.dma_start(wg[:, :, 32:36], gates_in[:, 0:KB, 4:8]).then_inc(s_consts, 16)
            pool.dma_start(gbias[0:4, :], gates_in[0:4, KB, 0:2]).then_inc(s_consts, 16)
            pool.dma_start(at(E_WPOOL, 2048), w_pool).then_inc(s_consts, 16)
            pool.dma_start(at(E_ICNT, 1024), inv_count).then_inc(s_consts, 16)
            pool.dma_start(at(K_KEYS, 2048), keys[0]).then_inc(s_keys, 16)
            step(pool.memset(zrow[:, :], 0.0))
            step(pool.memset(ident[:, :], 0.0))
            step(pool.affine_select(out=ident[:, :], in_=ident[:, :], compare_op=ALU.not_equal, fill=1.0,
                                    base=0, pattern=[[-1, P]], channel_multiplier=1))
            step(pool.iota(iota[:, :], pattern=[[1, P]], base=0, channel_multiplier=0,
                           allow_small_or_imprecise_dtypes=True))
            step(pool.memset(tri01[:, :], 1.0))
            step(pool.affine_select(out=tri01[:, 0:P], in_=tri01[:, 0:P], compare_op=ALU.is_ge, fill=0.0,
                                    base=0, pattern=[[1, P]], channel_multiplier=-1))
            step(pool.memset(at(E_MASK, 384), 0.0))
            for b in (0, 2):
                m = at(E_MASK + P * b, P)
                step(pool.affine_select(out=m, in_=m, compare_op=ALU.is_ge, fill=NEG, base=0,
                                        pattern=[[1, P]], channel_multiplier=-1))
            sel = big[0:4, E_SEL:E_SEL + 1024].rearrange("p (h t) -> p h t", h=4)
            step(pool.memset(sel, 0.0))
            step(pool.affine_select(out=sel, in_=sel, compare_op=ALU.not_equal, fill=1.0, base=0,
                                    pattern=[[-1, 4], [0, T]], channel_multiplier=1))
            for o in (E_PT, E_S2, E_S4):
                step(pool.memset(at(o, 8 * E_PW, 8)[:, :, 0:E_PAD], 0.0))
            assert count[0] == POOL_CONSTS, count[0]
            pool.memset(credit[:, :], 0.0).then_inc(s_hot_free, 2)
            pool.wait_ge(s_hot_free, 2)
            pool.memset(credit[:, :], 0.0).then_inc(s_g, 4)
            pool.wait_ge(s_g, 4)
            pool.memset(credit[:, :], 0.0).then_inc(s_sc, 1)
            pool.wait_ge(s_sc, 1)
            pool.memset(credit[:, :], 0.0).then_inc(s_sc_ps, 1)

            def tiles(o, j0, shift=0):
                return at(o, 8 * E_PW, 8)[:, j0:8, E_PAD - shift:E_PAD - shift + T]

            pool.wait_ge(s_evac, BLOCK0["o", 0])
            step(pool.tensor_tensor(tiles(E_S2, 0), tiles(E_PT, 0), tiles(E_PT, 0, 1), ALU.add))
            step(pool.tensor_tensor(tiles(E_S4, 2), tiles(E_S2, 2), tiles(E_S2, 2, 2), ALU.add))
            step(pool.tensor_tensor(tiles(E_S2, 4), tiles(E_S4, 4), tiles(E_S4, 4, 4), ALU.add))
            step(pool.tensor_tensor(tiles(E_S4, 6), tiles(E_S2, 6), tiles(E_S2, 6, 8), ALU.add))
            pool.wait_ge(s_consts, 16 * N_CONSTS)
            for g in range(4):
                src = at(E_S2 if g % 2 == 0 else E_S4, 8 * E_PW, 8)[:, 2 * g:2 * g + 2, E_PAD:E_PW]
                pt = at(E_PT, 8 * E_PW, 8)[:, 2 * g:2 * g + 2, E_PAD:E_PW]
                inv = at(E_ICNT + T * g, T).unsqueeze(1).broadcast_to([P, 2, T])
                step(pool.tensor_tensor(src, src, inv, ALU.mult))
                pool.tensor_tensor(pt, src, pt, ALU.subtract).then_inc(s_mixed, 1)

            def exponents():
                b3 = at(O_B, 2048).rearrange("p (g t) -> p g t", t=G_SUB)
                b8 = at(O_B, 2048, 8)
                mid = G_SUB // 2 - 1
                pool.wait_ge(s_decay, 2)
                pool.tensor_tensor(at(O_QE, 2048).rearrange("p (g t) -> p g t", t=G_SUB), b3,
                                   b3[:, :, mid:mid + 1].broadcast_to([P, 128, G_SUB]), ALU.subtract).then_inc(s_karg, 1)
                for g in range(T // G_SUB):
                    s0, n = g // G_PER * P, G_SUB * (g % G_PER + 1)
                    ref = G_SUB * g + mid
                    if g == 2:
                        for o, t in ((O_QX, P), (O_KX, 0)):
                            pool.tensor_tensor(at(o, 1024, 8), b8[:, :, t:t + P],
                                               b8[:, :, P - 1:P].broadcast_to([P, 8, P]), ALU.subtract).then_inc(s_karg, 1)
                    if g >= KE_BUFS:
                        pool.wait_ge(s_att_ps, att_count(g - KE_BUFS))
                    pool.tensor_tensor(ke_buf(g)[:, :, 0:n], b8[:, :, s0:s0 + n],
                                       b8[:, :, ref:ref + 1].broadcast_to([P, 8, n]), ALU.subtract).then_inc(s_karg, 1)

            def add_squares(k, tiles):
                for j in range(1, tiles):
                    pool.wait_ge(s_sq, SQ0[k] + (j if SQ_TILES[k] == KB else j // 4) + 1)
                    first = at(HT, T) if j == 1 else rstd[:, :]
                    ins = pool.tensor_tensor(rstd[:, :], first, at(HT + T * j, T), ALU.add)
                    if j < tiles - 1:
                        step(ins)
                ins.then_inc(s_acc, 1)

            for layer in range(2):
                if layer == 1:
                    exponents()
                add_squares(2 * layer + 1, KB)
                pool.wait_ge(s_evac, BLOCK0["wq", layer])
                for c in range(PIECES):
                    pool.wait_ge(s_used, SLAB0["wq", layer] + 3 * c + 1)
                    pool.dma_start(spill[:, PIECE * c:PIECE * (c + 1)], at(XT + PIECE * c, PIECE)).then_inc(s_spill, 16)
                for part in range(PARTS):
                    with pool.Fori(0, SC_TURNS) as i:
                        for q in range(8):
                            pool.wait_ge(s_key1, i * 8 + (sc_turns(layer, part) * 8 + q + 1))
                            pool.sem_inc(s_pool_turn, 1)
                            b = 4 * (q % 2)
                            w = jw[:, :, bass.ds(i * SC_TOKENS + 4 * q, 4)].rearrange("p c t -> p t c")
                            pool.tensor_tensor(hot1[:, b:b + 4, :, :],
                                               key1[:, b:b + 4, :].unsqueeze(2).broadcast_to([P, 4, WPARTS, HALF]),
                                               w.unsqueeze(3).broadcast_to([P, 4, WPARTS, HALF]),
                                               ALU.mult).then_inc(s_hot1, 1)
                pool.wait_ge(s_spill, 16 * PIECES * (layer + 1))
                for c in range(PIECES):
                    pool.wait_ge(s_used, SLAB0["vt", layer] + HALF + KB + 4 * c)
                    pool.dma_start(at(XT + PIECE * c, PIECE), spill[:, PIECE * c:PIECE * (c + 1)]).then_inc(s_reload, 16)
                add_squares(2 * layer + 2, KB // 2)
                if layer == 0:
                    pool.wait_ge(s_used, SLAB0["qk", 1])
                    pool.dma_start(at(K_KEYS, 2048), keys[1]).then_inc(s_keys, 16)
                    pool.dma_start(big[0:G_RANK, O_WGATE:O_WGATE + 1024], w_gate).then_inc(s_consts, 16)
                    pool.dma_start(at(O_WGL, 256), w_glow).then_inc(s_consts, 16)

        @block.scalar
        def _(act):
            pending = [None]
            count = [0]

            def chain(ins):
                ins.then_inc(s_act, 1)
                count[0] += 1
                act.wait_ge(s_act, count[0])

            def hi(slot, n):
                act.wait_ge(s_landed[slot], (n // RING + 1) * 16 if isinstance(n, int) else (n - slot) * 4 + 16)
                act.activation(w_hi[:, slot, :], w_raw[:, slot, :], ACT.Copy).then_inc(s_hi, 1)

            def flush():
                if pending[0]:
                    pending[0]()
                    pending[0] = None

            def ahead(n0):
                hi(0, n0)
                hi(1, n0 + 1)
                flush()
                hi(2, n0 + 2)
                hi(3, n0 + 3)

            def stream(name, layer, nblocks, evac, after=None):
                n0 = SLAB0[name, layer]
                evac(0)
                if after:
                    after(-1)

                def turn(i):
                    hi(0, i * 4 + n0)
                    hi(1, i * 4 + (n0 + 1))
                    evac(i * 2 - 1)
                    if after:
                        after(i * 2 - 2)
                    hi(2, i * 4 + (n0 + 2))
                    hi(3, i * 4 + (n0 + 3))
                    evac(i * 2)
                    if after:
                        after(i * 2 - 1)
                with act.Fori(1, nblocks // 2) as i:
                    turn(i)

                def last():
                    evac(nblocks - 1)
                    if after:
                        after(nblocks - 2)
                        after(nblocks - 1)
                pending[0] = last

            def block_to(name, layer, o, func=ACT.Copy, width=T, skip=0, scale=1.0, hi_part=None):
                n0 = SLAB0[name, layer]
                turnwise = [0]

                def evac(b):
                    if isinstance(b, int):
                        par = b % 2
                        dst = at(o + skip + b * width, T)
                    else:
                        par = 1 - turnwise[0] % 2
                        turnwise[0] += 1
                        dst = big[:, bass.ds(b * width + (o + skip), T)]
                    act.wait_ge(s_used, b * 2 + (n0 + 2))
                    act.activation(dst, bank(par, T), func, scale=scale).then_inc(s_evac, 1)
                return evac

            def v_groups(layer, ngroups, o, row):
                n0 = SLAB0["v", layer]
                for g in range(ngroups):
                    if g:
                        hi(0, n0 + 8 * g)
                        hi(1, n0 + 8 * g + 1)
                        flush()
                        hi(2, n0 + 8 * g + 2)
                        hi(3, n0 + 8 * g + 3)
                    for s in range(4):
                        hi(s, n0 + 8 * g + 4 + s)

                    def evac(g=g):
                        act.wait_ge(s_used, n0 + 8 * g + 8)
                        for tb in range(TB):
                            act.activation(at(o + row * tb + 512 * g, 512), bank(3 + 2 * (g % 2) + tb),
                                           ACT.Copy).then_inc(s_vevac, 1)
                    pending[0] = evac

            def square(c):
                act.activation(at(HT + 1024 * c, 1024), at(XT + 1024 * c, 1024), ACT.Square).then_inc(s_sq, 1)

            def norm(k, fill, n0=None):
                act.wait_ge(s_sum, k + 1)
                act.activation(stdv[:, :], bank(2, T), ACT.Sqrt, bias=epst[:, 0:1], scale=1.0 / D).then_inc(s_std, 1)
                if n0 is not None:
                    hi(2, n0 + 2)
                    hi(3, n0 + 3)
                if fill is not None:
                    act_hi(s_h, CHUNKS * k)

            def out_squares(layer):
                n0, b0 = SLAB0["out", layer], BLOCK0["out", layer]

                def sq(b):
                    act.wait_ge(s_evac, b + (b0 + 1))
                    if isinstance(b, int):
                        src, dst = at(XT + b * T, T), at(HT + b * T, T)
                    else:
                        src, dst = big[:, bass.ds(b * T + XT, T)], big[:, bass.ds(b * T + HT, T)]
                    act.activation(dst, src, ACT.Square).then_inc(s_sq, 1)

                def turn(i):
                    hi(0, i * 4 + n0)
                    hi(1, i * 4 + (n0 + 1))
                    sq(i * 2 - 2)
                    hi(2, i * 4 + (n0 + 2))
                    hi(3, i * 4 + (n0 + 3))
                    sq(i * 2 - 1)
                with act.Fori(1, KB // 2) as i:
                    turn(i)
                hi(0, n0 + 32)
                sq(KB - 2)
                hi(1, n0 + 33)
                sq(KB - 1)

            def next_two(name, layer, b):
                n = SLAB0[name, layer] + 2 * b + 4
                hi(n % RING, n)
                hi((n + 1) % RING, n + 1)

            def chunk_hi(c):
                act.activation(act_hi_t[:, 2 * c:2 * c + 2, :], at(HT + 512 * c, 512, 2), ACT.Copy).then_inc(s_ahi, 1)

            def act_hi(src, base):
                for c in range(CHUNKS):
                    act.wait_ge(src, base + c + 1)
                    chunk_hi(c)

            def even():
                act.wait_ge(s_pool, 2)
                for c in range(4):
                    act.wait_ge(s_x[c], 16)
                    square(c)
                hi(0, 0)
                hi(1, 1)
                norm(0, FILL["h", 0], 0)

                stream("qk", 0, 8, block_to("qk", 0, E_Q))
                ahead(SLAB0["v", 0])
                rows = lambda r: big[0:4, E_ROWS + T * r:E_ROWS + T * (r + 1)]
                act.wait_ge(s_grow, 1)
                chain(act.activation(rows(2), rows(1), ACT.Exp, scale=-1.0))
                act.activation(rows(2), rows(2), ACT.Ln, bias=1.0).then_inc(s_grow_act, 1)
                act.wait_ge(s_rows, 1)
                act.activation(rows(5), rows(1), ACT.Exp, scale=-1.0).then_inc(s_floor, 1)
                v_groups(0, 2, E_V, 1024)
                ahead(SLAB0["p", 0])

                def exponentials(h):
                    act.wait_ge(s_dm, h + 1)
                    act.activation(at(E_PE + 384 * h, 384), at(E_PE + 384 * h, 384), ACT.Exp).then_inc(s_p, 1)

                def squares():
                    act.wait_ge(s_num_ps, M_HEADS)
                    for h in range(M_HEADS):
                        act.wait_ge(s_hn, h + 1)
                        act.activation(at(E_V + 512 * h, 512), at(HT + 2048 + 512 * h, 512), ACT.Square).then_inc(s_hsq, 1)

                def roots():
                    for c in range(2):
                        act.wait_ge(s_ssq_ps, c + 1)
                        act.activation(at(E_PE + 512 * c, 512), bank(3 + c), ACT.Sqrt, bias=epst[:, 0:1],
                                       scale=1.0 / M_DV).then_inc(s_hstd, 1)

                def pooled(tiles):
                    for j in tiles:
                        act.wait_ge(s_pool_ps, j // 2 * 2 + 2)
                        act.activation(at(HT + T * j, T), pool_bank(j), ACT.Copy,
                                       scale=gain[:, G_PS + j:G_PS + j + 1]).then_inc(s_pool_out, 1)
                evac = block_to("p", 0, E_PT, width=E_PW, skip=E_PAD)
                beside = {b: (lambda h=h: exponentials(h)) for h, b in enumerate(SCORES_AT)}
                for b in range(8):
                    evac(b)
                    next_two("p", 0, b)
                    if b in beside:
                        beside[b]()
                evac = block_to("o", 0, E_SO, func=ACT.Sigmoid)
                beside = {0: squares, 1: roots, 4: lambda: pooled(range(4)), 5: lambda: pooled(range(4, 8))}
                for b in range(7):
                    evac(b)
                    next_two("o", 0, b)
                    if b in beside:
                        beside[b]()
                act.wait_ge(s_pool_out, 8)
                act.wait_ge(s_used, SLAB0["out", 0] - 1)
                for c in range(CHUNKS // 2):
                    chunk_hi(c)
                evac(7)
                for h in range(M_HEADS):
                    act.wait_ge(s_y, h + 1)
                    chunk_hi(CHUNKS // 2 + h)
                next_two("o", 0, 7)
                out_squares(0)

            def odd():
                n0 = SLAB0["qk", 1]
                for c in range(4):
                    if c == 2:
                        hi(0, n0)
                        hi(1, n0 + 1)
                    act.wait_ge(s_yadd, c + 1)
                    square(c)
                norm(2, FILL["h", 1], n0)
                stream("qk", 1, 16, block_to("qk", 1, O_Q))
                ahead(SLAB0["r", 1])
                act.wait_ge(s_gl_ps, 1)
                act.activation(big[0:G_RANK, O_GLT:O_GLT + T], ps[0:G_RANK, 7, 0:T], ACT.Copy).then_inc(s_gl, 1)

                def o_root(h):
                    act.wait_ge(s_ssq_ps, 2 + h + 1)
                    act.activation(at(O_B + T * h, T), o_sum(h), ACT.Sqrt, bias=epst[:, 0:1],
                                   scale=1.0 / G_DV).then_inc(s_hstd, 1)

                def decay_exp():
                    act.wait_ge(s_la, 1)
                    chain(act.activation(at(O_KE + 2048, 2048), at(O_KE + 2048, 2048), ACT.Exp, scale=-1.0))

                def decay_ln():
                    act.activation(at(O_KE + 2048, 2048), at(O_KE + 2048, 2048), ACT.Ln, bias=1.0).then_inc(s_la_act, 1)
                def k_exp(g):
                    if g == 2:
                        for o, sign in ((O_QX, 1.0), (O_KX, -1.0)):
                            act.wait_ge(s_karg, 4 if o == O_QX else 5)
                            act.activation(at(o, 1024), at(o, 1024), ACT.Exp, scale=sign / G_TAU).then_inc(s_kexp, 1)
                    n = G_SUB * (g % G_PER + 1)
                    ke = ke_buf(g)[:, :, 0:n]
                    act.wait_ge(s_karg, exp_count(g))
                    act.activation(ke, ke, ACT.Exp, scale=-1.0 / G_TAU).then_inc(s_kexp, 1)

                def q_exp():
                    act.wait_ge(s_karg, 1)
                    act.activation(at(O_QE, 2048), at(O_QE, 2048), ACT.Exp, scale=1.0 / G_TAU).then_inc(s_kexp, 1)
                evac = block_to("r", 1, O_R)
                for b in range(KB):
                    evac(b)
                    next_two("r", 1, b)
                    if b == 2:
                        decay_exp()
                    if b == 3:
                        decay_ln()
                    if b == GLA_AT - 1:
                        q_exp()
                    if GLA_AT <= b < GLA_AT + 8:
                        k_exp(2 * (b - GLA_AT))
                        k_exp(2 * (b - GLA_AT) + 1)

                def v_evac(g):
                    act.wait_ge(s_used, SLAB0["v", 1] + 8 * g + 8)
                    for tb in range(TB):
                        act.activation(at(O_V + 2048 * tb + 512 * g, 512), bank(V_BANKS[g % 2][tb]),
                                       ACT.Copy).then_inc(s_vevac, 1)

                def o_evac(h):
                    act.wait_ge(s_o_ps, h + 1)
                    act.activation(at(O_KE + 1024 * h, 1024), banks(O_BANK, 2), ACT.Square).then_inc(s_osq, 1)
                    act.activation(at(HT + 1024 * h, 1024), banks(O_BANK, 2), ACT.Copy).then_inc(s_o, 1)
                act.wait_ge(s_evac, BLOCK0["out", 1])
                for g in range(G_HEADS):
                    for q in range(8):
                        if g and q == 0:
                            v_evac(g - 1)
                        if g == G_HEADS - 1 and q == 6:
                            act.wait_ge(s_used, SLAB0["out", 1] - 2)
                            for c in range(6):
                                act.wait_ge(s_y, M_HEADS + c + 1)
                                chunk_hi(c)
                            v_evac(g)
                        if g == G_HEADS - 1 and q == 7:
                            o_evac(g)
                        if g and q == 2:
                            o_evac(g - 1)
                        if g and q == 4:
                            o_root(g - 1)
                        if g == 0 and q < 4:
                            act.activation(at(O_R + 1024 * q, 1024), at(O_R + 1024 * q, 1024), ACT.Silu).then_inc(s_silu, 1)
                        n = SLAB0["v", 1] + 8 * g + q + 4
                        hi(n % RING, n)
                o_root(G_HEADS - 1)
                for c in (6, 7):
                    act.wait_ge(s_y, M_HEADS + c + 1)
                    chunk_hi(c)
                out_squares(1)

            def experts(layer):
                norm(2 * layer + 1, FILL["k", layer], SLAB0["wq", layer])
                qbase = SLAB0["wq", layer]
                sc = at(K_SC, 4096).rearrange("p (b h c n) -> p b h c n", b=TB, h=HEADS, c=2)
                q_turn = [0]

                def q_evac(b):
                    if isinstance(b, int):
                        par = b % 2
                    else:
                        par = 1 - q_turn[0] % 2
                        q_turn[0] += 1
                    act.wait_ge(s_used, b * 2 + (qbase + 2))
                    if not (isinstance(b, int) and b < 2 and layer == 0):
                        act.wait_ge(s_sc_ps, b + 16 * layer)
                    act.activation(at(K_QS + T * par, T), bank(par, T), ACT.Copy).then_inc(s_evac, 1)

                s_turn = [0]

                def sc_save(q):
                    if isinstance(q, int):
                        if q < 0:
                            return
                        par, head = q % 2, q // 2
                        act.wait_ge(s_sc_ps, 16 * layer + q + 2)
                        act.activation(sc[:, :, head, par, :], bank(2 + par, T, TB), ACT.Copy).then_inc(s_sc, 1)
                    else:
                        par = s_turn[0] % 2
                        s_turn[0] += 1
                        act.wait_ge(s_sc_ps, q + (16 * layer + 2))
                        src = big[:, bass.ds(q * P + K_SC, 2048 + P)]
                        dst = src.rearrange("p (a n) -> p a n", n=P)[:, 0:17:16, :]
                        act.activation(dst, bank(2 + par, T, TB), ACT.Copy).then_inc(s_sc, 1)
                stream("wq", layer, 16, q_evac, after=sc_save)
                ahead(SLAB0["u", layer])

                ubase = SLAB0["u", layer]

                def ge(b, par, first=False):
                    act.wait_ge(s_used, b * 2 + (ubase + 2))
                    dst = at(b * T, T) if isinstance(b, int) else big[:, bass.ds(b * T, T)]
                    act.activation(dst, bank(par, T), ACT.Gelu).then_inc(s_evac, 1)

                act.wait_ge(s_spill, 16 * PIECES * (layer + 1))
                ge(0, 0)
                for s in range(4):
                    hi(s, ubase + 4 + s)
                    if s % 2:
                        ge(s // 2 + 1, (s // 2 + 1) % 2)

                def u_turn(i):
                    for s in range(8):
                        hi(s % 4, i * 8 + (ubase + s))
                        if s % 2:
                            ge(i * 4 + (s // 2 - 1), (s // 2 + 1) % 2)
                with act.Fori(1, ITEMS) as i:
                    u_turn(i)
                act.wait_ge(s_cvs, layer + 1)
                act.activation(cv[:, :, :], cv[:, :, :], ACT.Exp).then_inc(s_cexp, 1)
                with act.Fori(ITEMS, N_KEYS // 4) as i:
                    u_turn(i)

                vbase = SLAB0["vt", layer]
                hi(0, vbase)
                hi(1, vbase + 1)
                act.wait_ge(s_g, SC_TURNS * 4 * (2 * layer + 1) + 4)
                act.wait_ge(s_used, vbase - 1)

                def c_hi(block_, buf):
                    src = at(block_ * T, T) if isinstance(block_, int) else big[:, bass.ds(block_ * T, T)]
                    act.activation(act_hi_t[:, buf, :], src, ACT.Copy).then_inc(s_chi, 1)
                for b in range(4):
                    c_hi(b, b)
                ge(N_KEYS - 1, 1)
                hi(2, vbase + 2)
                hi(3, vbase + 3)
                for s in range(4, 8):
                    hi(s % 4, vbase + s)
                    c_hi(s, s)
                for h in range(2):
                    with act.Fori(1 - h, HALF // 8) as i:
                        for s in range(8):
                            hi(s % 4, i * 8 + (vbase + HALF * h + s))
                            c_hi(i * 8 + s, s)
                act.wait_ge(s_g, SC_TURNS * 8 * (layer + 1) + 4)
                with act.Fori(HALF // 4, N_KEYS // 4) as i:
                    for s in range(8):
                        hi(s % 4, i * 8 + (vbase + s))
                        if s < 4:
                            c_hi(i * 4 + s, s)

            even()
            experts(0)
            odd()
            experts(1)
            for c in range(4):
                act.wait_ge(s_yadd, 4 + c + 1)
                square(c)
            norm(4, None)

        @block.vector
        def _(dve):
            count = [0]

            def chain(ins):
                ins.then_inc(s_vec, 1)
                count[0] = count[0] + 1
                dve.wait_ge(s_vec, count[0])

            def lo(slot, n):
                dve.wait_ge(s_hi, n + 1)
                dve.tensor_tensor(w_lo[:, slot, :], w_raw[:, slot, :], w_hi[:, slot, :].bitcast(F32),
                                  ALU.subtract).then_inc(s_lo, 1)

            def ahead(n0):
                for s in range(RING):
                    lo(s, n0 + s)

            def stream(name, layer, nslabs):
                n0 = SLAB0[name, layer]
                with dve.Fori(1, nslabs // RING) as i:
                    for s in range(RING):
                        lo(s, i * RING + (n0 + s))

            def v_groups(layer, ngroups):
                n0 = SLAB0["v", layer]
                for g in range(ngroups):
                    for s in range(8):
                        if g or s >= 4:
                            lo(s % 4, n0 + 8 * g + s)

            def residual(layer):
                n0 = SLAB0["out", layer]

                def add(b, par):
                    dve.wait_ge(s_used, b * 2 + (n0 + 2))
                    dst = at(XT + b * T, T) if isinstance(b, int) else big[:, bass.ds(b * T + XT, T)]
                    dve.tensor_tensor(dst, dst, bank(par, T), ALU.add).then_inc(s_evac, 1)
                add(0, 0)
                with dve.Fori(1, KB // 2) as i:
                    lo(0, i * 4 + n0)
                    lo(1, i * 4 + (n0 + 1))
                    add(i * 2 - 1, 1)
                    lo(2, i * 4 + (n0 + 2))
                    lo(3, i * 4 + (n0 + 3))
                    add(i * 2, 0)
                lo(0, n0 + 32)
                lo(1, n0 + 33)
                add(KB - 1, 1)

            def next_two(name, layer, b):
                n = SLAB0[name, layer] + 2 * b + 4
                lo(n % RING, n)
                lo((n + 1) % RING, n + 1)

            def chunk_lo(fill, c):
                dve.wait_ge(s_ahi, CHUNKS * fill + c + 1)
                dve.tensor_tensor(act_lo_t[:, 2 * c:2 * c + 2, :], at(HT + 512 * c, 512, 2),
                                  act_hi_t[:, 2 * c:2 * c + 2, :].bitcast(F32), ALU.subtract).then_inc(s_alo, 1)

            def norm(k, fill, n0=None):
                dve.wait_ge(s_std, k + 1)
                dve.reciprocal(rstd[:, :], stdv[:, :]).then_inc(s_rstd, 1)
                dve.wait_ge(s_rstd, k + 1)
                for c in range(CHUNKS):
                    for j in (2 * c, 2 * c + 1):
                        ins = dve.scalar_tensor_tensor(out=at(HT + T * j, T), in0=at(XT + T * j, T),
                                                       scalar=gain[:, G_NORM[k] + j:G_NORM[k] + j + 1],
                                                       in1=rstd[:, :], op0=ALU.mult, op1=ALU.mult)
                    ins.then_inc(s_h, 1)
                    if fill is not None and c:
                        chunk_lo(fill, c - 1)
                if fill is not None:
                    chunk_lo(fill, CHUNKS - 1)
                if n0 is not None:
                    lo(2, n0 + 2)
                    lo(3, n0 + 3)

            def even():
                dve.wait_ge(s_gain, 16)
                lo(0, 0)
                lo(1, 1)
                norm(0, FILL["h", 0], 0)
                stream("qk", 0, 16)
                ahead(SLAB0["v", 0])
                rows = lambda r: big[0:4, E_ROWS + T * r:E_ROWS + T * (r + 1)]
                dve.wait_ge(s_consts, 16 * N_CONSTS)
                dve.wait_ge(s_pool, POOL_CONSTS)
                dve.wait_ge(s_gates_ps, 1)
                chain(dve.tensor_scalar(rows(0), ps[0:4, 7, 0:T], gbias[0:4, 0:1], None, ALU.add))
                chain(dve.tensor_scalar(rows(3), ps[32:36, 7, 0:T], gbias[0:4, 1:2], None, ALU.add))
                dve.scalar_tensor_tensor(out=rows(1), in0=rows(3), scalar=-1.0, in1=rows(3), op0=ALU.mult,
                                         op1=ALU.max).then_inc(s_grow, 1)
                dve.wait_ge(s_grow_act, 1)
                chain(dve.scalar_tensor_tensor(out=rows(1), in0=rows(3), scalar=0.0, in1=rows(2),
                                               op0=ALU.min, op1=ALU.subtract))
                chain(dve.memset(rows(2), 0.0))
                chain(dve.tensor_tensor_scan(rows(3), rows(1), rows(2), 0.0, ALU.add, ALU.add))
                chain(dve.tensor_tensor(rows(4), rows(0), rows(3), ALU.subtract))
                chain(dve.tensor_tensor_scan(rows(0), rows(4), rows(4), 0.0, ALU.max, ALU.max))
                chain(dve.tensor_scalar(rows(2), rows(0), -1.0, None, ALU.mult))
                dve.tensor_tensor(rows(1), rows(0), rows(3), ALU.add).then_inc(s_rows, 1)
                v_groups(0, 2)
                ahead(SLAB0["p", 0])

                def masked(h):
                    dve.wait_ge(s_d_ps, h + 1)
                    dve.tensor_tensor(at(E_PE + 384 * h, 384), bank(3 + h % 2, 384), at(E_MASK, 384),
                                      ALU.add).then_inc(s_dm, 1)

                def weights(h):
                    dve.wait_ge(s_p, h + 1)
                    dve.wait_ge(s_s_ps, h + 1)
                    pe_h = at(E_PE + 384 * h, 384)
                    dve.scalar_tensor_tensor(out=pe_h, in0=bank(5 + h % 2, 384), scalar=M_DK ** -0.5, in1=pe_h,
                                             op0=ALU.mult, op1=ALU.mult).then_inc(s_s, 1)

                def output(h):
                    dve.wait_ge(s_num_ps, h + 1)
                    chain(dve.tensor_copy(stdv[:, :], ps[:, 2, 0:T]))
                    chain(dve.scalar_tensor_tensor(out=rstd[:, :], in0=stdv[:, :], scalar=-1.0, in1=stdv[:, :],
                                                   op0=ALU.mult, op1=ALU.max))
                    chain(dve.tensor_tensor(rstd[:, :], rstd[:, :], ps[:, 2, T:2 * T], ALU.max))
                    chain(dve.reciprocal(stdv[:, :], rstd[:, :]))
                    dve.tensor_tensor(at(HT + 2048 + 512 * h, 512, 2), bank(7, 512, 2),
                                      stdv[:, :].unsqueeze(1).broadcast_to([P, 2, T]), ALU.mult).then_inc(s_hn, 1)

                def head_scores(h):
                    masked(h)
                    weights(h)

                def normalised(h):
                    dve.wait_ge(s_hstd, h // 2 + 1)
                    r = at(E_PE + T * h, T)
                    chain(dve.reciprocal(r, r))
                    for j in (2 * h, 2 * h + 1):
                        tile = at(HT + 2048 + T * j, T)
                        ins = dve.scalar_tensor_tensor(out=tile, in0=tile, scalar=gain[:, G_EH + j:G_EH + j + 1],
                                                       in1=r, op0=ALU.mult, op1=ALU.mult)
                    chain(ins)

                def gated(h):
                    dve.wait_ge(s_evac, BLOCK0["o", 0] + 2 * h + 2)
                    y = at(HT + 2048 + 512 * h, 512)
                    dve.tensor_tensor(y, y, at(E_SO + 512 * h, 512), ALU.mult).then_inc(s_y, 1)
                beside = {b: (lambda h=h: head_scores(h)) for h, b in enumerate(SCORES_AT)}
                beside.update({b: (lambda h=h: output(h)) for h, b in enumerate(OUTPUTS_AT)})
                for b in range(8):
                    next_two("p", 0, b)
                    beside[b]()
                beside = {b: (lambda h=b - 2: normalised(h)) for b in range(2, 6)}
                for b in range(7):
                    next_two("o", 0, b)
                    if b in beside:
                        beside[b]()
                for h in range(3):
                    gated(h)
                for c in range(CHUNKS // 2):
                    chunk_lo(FILL["y", 0], c)
                gated(3)
                for c in range(CHUNKS // 2, CHUNKS):
                    chunk_lo(FILL["y", 0], c)
                next_two("o", 0, 7)
                residual(0)

            def odd():
                norm(2, FILL["h", 1], SLAB0["qk", 1])
                stream("qk", 1, 32)
                ahead(SLAB0["r", 1])

                def biased(r):
                    dve.wait_ge(s_pre_ps, r + 1)
                    for j in range(4 * r, 4 * r + 4):
                        b = 7 if j % 4 < 2 else 2
                        ins = dve.tensor_scalar(at(O_KE + T * j, T), ps[:, b, T * (j % 2):T * (j % 2) + T],
                                                gain[:, G_BG + j:G_BG + j + 1], None, ALU.add)
                    ins.then_inc(s_bias, 1)

                def magnitude():
                    biased(1)
                    dve.wait_ge(s_bias, 2)
                    dve.scalar_tensor_tensor(out=at(O_KE + 2048, 2048), in0=at(O_KE, 2048), scalar=-1.0,
                                             in1=at(O_KE, 2048), op0=ALU.mult, op1=ALU.max).then_inc(s_la, 1)

                def decay():
                    chain(dve.memset(rstd[:, :], 0.0))
                    dve.wait_ge(s_la_act, 1)
                    chain(dve.scalar_tensor_tensor(out=at(O_KE, 2048), in0=at(O_KE, 2048), scalar=0.0,
                                                   in1=at(O_KE + 2048, 2048), op0=ALU.min, op1=ALU.subtract))

                def decay_sum(js):
                    for j in js:
                        ins = dve.tensor_tensor_scan(at(O_B + T * j, T), at(O_KE + T * j, T), rstd[:, :], 0.0,
                                                     ALU.add, ALU.add)
                    ins.then_inc(s_decay, 1)

                def q_mul():
                    dve.wait_ge(s_kexp, 1)
                    dve.scalar_tensor_tensor(out=at(O_QE, 2048), in0=at(O_QE, 2048), scalar=G_DK ** -0.5,
                                             in1=at(O_Q, 2048), op0=ALU.mult, op1=ALU.mult).then_inc(s_ke, 1)

                def k_mul(g):
                    if g == 2:
                        dve.wait_ge(s_kexp, 4)
                        dve.scalar_tensor_tensor(out=at(O_QX, 1024, 8), in0=at(O_QX, 1024, 8), scalar=G_DK ** -0.5,
                                                 in1=at(O_Q, 2048, 8)[:, :, P:T], op0=ALU.mult,
                                                 op1=ALU.mult).then_inc(s_ke, 1)
                        dve.wait_ge(s_kexp, 5)
                        dve.tensor_tensor(at(O_KX, 1024, 8), at(O_KX, 1024, 8), at(O_K, 2048, 8)[:, :, 0:P],
                                          ALU.mult).then_inc(s_ke, 1)
                    s0, n = g // G_PER * P, G_SUB * (g % G_PER + 1)
                    dve.wait_ge(s_kexp, exp_count(g))
                    ke = ke_buf(g)[:, :, 0:n]
                    dve.tensor_tensor(ke, ke, at(O_K, 2048, 8)[:, :, s0:s0 + n], ALU.mult).then_inc(s_ke, 1)

                def causal():
                    dve.wait_ge(s_att_ps, T // G_SUB + 1)
                    for hp in range(2):
                        dve.tensor_tensor(at(O_ATT + 512 * hp, 512, 2), bank(3 + hp, 512, 2),
                                          tri01[:, :].unsqueeze(1).broadcast_to([P, 2, T]), ALU.mult).then_inc(s_att, 1)
                        dve.tensor_tensor(at(O_ATT + 1024 + 512 * hp, 512, 2)[:, :, P:T],
                                          bank(5 + hp, 512, 2)[:, :, P:T],
                                          tri01[:, 0:P].unsqueeze(1).broadcast_to([P, 2, P]), ALU.mult).then_inc(s_att, 1)
                beside = {0: [lambda: biased(0)], 1: [magnitude], 4: [decay, lambda: decay_sum(range(4))],
                          5: [lambda: decay_sum(range(4, 8))]}
                for i in range(8):
                    beside[GLA_AT + i] = [lambda i=i: k_mul(2 * i), lambda i=i: k_mul(2 * i + 1)]
                beside[GLA_AT - 1] = [q_mul]
                for b in range(KB):
                    next_two("r", 1, b)
                    for f in beside.get(b, []):
                        f()

                def head(h, half):
                    r = at(O_B + T * h, T)
                    if half == 0:
                        dve.wait_ge(s_hstd, 2 + h + 1)
                        dve.wait_ge(s_silu, h + 1)
                        chain(dve.reciprocal(r, r))
                    for c in (2 * h + half,):
                        for j in (2 * c, 2 * c + 1):
                            ins = dve.scalar_tensor_tensor(out=at(HT + T * j, T), in0=at(HT + T * j, T),
                                                           scalar=gain[:, G_OH + j:G_OH + j + 1], in1=r,
                                                           op0=ALU.mult, op1=ALU.mult)
                        chain(ins)
                        dve.tensor_tensor(at(HT + 512 * c, 512), at(HT + 512 * c, 512), at(O_R + 512 * c, 512),
                                          ALU.mult).then_inc(s_y, 1)
                for g in range(G_HEADS):
                    for q in range(8):
                        if g == G_HEADS - 1 and q == 6:
                            for c in range(6):
                                chunk_lo(FILL["y", 1], c)
                        if g == 0 and q == 0:
                            causal()
                        if g and q in (4, 5):
                            head(g - 1, q - 4)
                        n = SLAB0["v", 1] + 8 * g + q + 4
                        lo(n % RING, n)
                head(G_HEADS - 1, 0)
                head(G_HEADS - 1, 1)
                chunk_lo(FILL["y", 1], 6)
                chunk_lo(FILL["y", 1], 7)
                residual(1)

            def tk(o, n, k=None):
                return at(K_TK + o, n, k)
            s0, s1 = tk(0, 256, 2), tk(256, 256, 2)
            c0, c1 = tk(512, 256), tk(768, 256)
            sv = tk(1024, 32, 2)
            si = tk(1056, 32).bitcast(U32).rearrange("p (c k) -> p c k", c=2)
            sif = tk(1088, 32)
            ci = tk(1120, 16).bitcast(U32)
            cij = tk(1136, 32).bitcast(U32)
            cijf = tk(1168, 32)
            tv = tk(1200, 16)
            pick = tk(1216, 512)

            tk_count = [0]

            def tk_chain(ins):
                ins.then_inc(s_tk, 1)
                tk_count[0] += 1
                dve.wait_ge(s_tk, tk_count[0])

            def topk_steps(i):
                src = at(K_SC + 256 * i, 256) if isinstance(i, int) else big[:, bass.ds(i * 256 + K_SC, 256)]
                yield lambda: tk_chain(dve.tensor_copy(tk(0, 256), src))
                for p in range(2):
                    yield lambda p=p: tk_chain(dve.max(sv[:, p, 0:8], s0[:, p, :]))
                    yield lambda p=p: tk_chain(dve.max_index(si[:, p, 0:8], sv[:, p, 0:8], s0[:, p, :]))
                    yield lambda p=p: tk_chain(dve.match_replace(s1[:, p, :], sv[:, p, 0:8], s0[:, p, :], NEG))
                    yield lambda p=p: tk_chain(dve.max(sv[:, p, 8:16], s1[:, p, :]))
                    yield lambda p=p: tk_chain(dve.max_index(si[:, p, 8:16], sv[:, p, 8:16], s1[:, p, :]))
                yield lambda: tk_chain(dve.tensor_tensor(
                    c0.rearrange("p (i j) -> p i j", i=TOPK),
                    sv[:, 0, :].unsqueeze(2).broadcast_to([P, TOPK, TOPK]),
                    sv[:, 1, :].unsqueeze(1).broadcast_to([P, TOPK, TOPK]), ALU.add))
                yield lambda: tk_chain(dve.max(tv[:, 0:8], c0))
                yield lambda: tk_chain(dve.max_index(ci[:, 0:8], tv[:, 0:8], c0))
                yield lambda: tk_chain(dve.match_replace(c1, tv[:, 0:8], c0, NEG))
                yield lambda: tk_chain(dve.max(tv[:, 8:16], c1))
                yield lambda: tk_chain(dve.max_index(ci[:, 8:16], tv[:, 8:16], c1))
                yield lambda: tk_chain(dve.tensor_scalar(cij[:, 0:16], ci, 4, None, ALU.logical_shift_right))
                yield lambda: tk_chain(dve.tensor_scalar(cij[:, 16:32], ci, 15, None, ALU.bitwise_and))
                yield lambda: tk_chain(dve.tensor_copy(cijf, cij))
                yield lambda: tk_chain(dve.tensor_copy(sif, tk(1056, 32).bitcast(U32)))
                yield lambda: tk_chain(dve.tensor_tensor(
                    pick.rearrange("p (a j) -> p a j", j=TOPK), cijf.unsqueeze(2).broadcast_to([P, 32, TOPK]),
                    iota[:, 0:TOPK].unsqueeze(1).broadcast_to([P, 32, TOPK]), ALU.is_equal))
                yield lambda: tk_chain(dve.tensor_tensor(
                    pick.rearrange("p (c k j) -> p c k j", c=2, j=TOPK),
                    pick.rearrange("p (c k j) -> p c k j", c=2, j=TOPK),
                    sif.rearrange("p (c j) -> p c j", c=2).unsqueeze(2).broadcast_to([P, 2, TOPK, TOPK]), ALU.mult))
                if isinstance(i, int):
                    de, dc = e12[:, :, i, :], cv[:, i, :]
                else:
                    de = e12[:, :, bass.ds(i, 1), :].rearrange("p c a k -> p c (a k)")
                    dc = cv[:, bass.ds(i, 1), :].rearrange("p a k -> p (a k)")
                yield lambda: tk_chain(dve.tensor_reduce(de, pick.rearrange("p (c k j) -> p c k j", c=2, j=TOPK), AX.X, ALU.add))
                yield lambda: tk_chain(dve.tensor_copy(dc, tv))

            def experts(layer):
                norm(2 * layer + 1, FILL["k", layer], SLAB0["wq", layer])
                stream("wq", layer, 32)
                ubase = SLAB0["u", layer]
                ahead(ubase)
                dve.wait_ge(s_sc, 16 * (layer + 1) + 1)

                def u_turn(i, slabs, with_topk):
                    steps = list(topk_steps(i)) if with_topk else []
                    if with_topk:
                        dve.sem_clear(s_tk)
                        tk_count[0] = 0
                    per = -(-len(steps) // len(slabs))
                    for s in slabs:
                        lo(s % 4, i * 8 + (ubase + s))
                        for _ in range(per):
                            if steps:
                                steps.pop(0)()
                u_turn(0, range(4, 8), True)
                with dve.Fori(1, ITEMS) as i:
                    u_turn(i, range(8), True)
                chain(dve.tensor_copy(csum[:, :], cv[:, :, 0:1].rearrange("p i k -> p (i k)")))
                dve.tensor_tensor(cv[:, :, :], cv[:, :, :], csum[:, :].unsqueeze(2).broadcast_to([P, ITEMS, TOPK]),
                                  ALU.subtract).then_inc(s_cvs, 1)
                lo(0, ubase + 8 * ITEMS)
                lo(1, ubase + 8 * ITEMS + 1)
                dve.wait_ge(s_cexp, layer + 1)
                chain(dve.tensor_reduce(csum[:, :], cv[:, :, :], AX.X, ALU.add))
                chain(dve.reciprocal(csum[:, :], csum[:, :]))
                dve.tensor_tensor(cv[:, :, :], cv[:, :, :], csum[:, :].unsqueeze(2).broadcast_to([P, ITEMS, TOPK]),
                                  ALU.mult).then_inc(s_slots, 1)
                for s in range(2, 8):
                    lo(s % 4, ubase + 8 * ITEMS + s)
                dve.wait_ge(s_jt_ps, layer + 1)
                dve.tensor_copy(jt[:, :, :].rearrange("p c t -> p (c t)"), bank(3))
                chain(dve.tensor_copy(rstd[:, :], bank(4, T)))
                for c in range(WPARTS):
                    chain(dve.tensor_copy(jw[:, c, :], rstd[:, :]))
                    if c < WPARTS - 1:
                        chain(dve.tensor_tensor(rstd[:, :], rstd[:, :], jw[:, c, :], ALU.subtract))

                def spread(part, i, k):
                    dve.wait_ge(s_hot_free, i * 8 + (sc_turns(layer, part) * 8 + 2 * (k + 1) + 2))
                    grid = at(HALF * T * part, HALF * T).rearrange("p (e t) -> p t e", t=T)
                    t0 = i * SC_TOKENS + 8 * k
                    dst = grid[:, t0:t0 + 8, :] if isinstance(i, int) else grid[:, bass.ds(t0, 8), :]
                    dve.tensor_tensor(dst, dst, bank(4 + k, 512, 8), ALU.mult).then_inc(s_g, 1)

                def scatter(part, i, s, first=False):
                    done = sc_turns(layer, part)
                    if s in (4, 6):
                        spread(part, i, (s - 4) // 2)
                    elif s in (0, 2) and not first:
                        spread(part, i - 1, s // 2 + 2)
                    dve.wait_ge(s_hot_free, i * 8 + (done * 8 + s + 1))
                    t0, b = i * SC_TOKENS + 4 * s, 4 * (s % 2)
                    num = jt[:, :, t0:t0 + 4] if isinstance(i, int) else jt[:, :, bass.ds(t0, 4)]
                    dve.tensor_tensor(key1[:, b:b + 4, :],
                                      iota[:, HALF * part:HALF * (part + 1)].unsqueeze(1).broadcast_to([P, 4, HALF]),
                                      num[:, 0, :].unsqueeze(2).broadcast_to([P, 4, HALF]),
                                      ALU.is_equal).then_inc(s_key1, 1)
                    dve.tensor_tensor(hot2[:, b:b + 4, :], iota[:, :].unsqueeze(1).broadcast_to([P, 4, P]),
                                      num[:, 1, :].unsqueeze(2).broadcast_to([P, 4, P]),
                                      ALU.is_equal).then_inc(s_hot2, 1)

                def scatter_rest(part):
                    for k in (2, 3):
                        spread(part, SC_TURNS - 1, k)

                dve.wait_ge(s_evac, BLOCK0["u", layer] + HALF)
                for s in range(8):
                    lo(s % 4, ubase + 8 * SC_FIRST + s)
                    scatter(0, 0, s, first=True)
                with dve.Fori(1, SC_TURNS) as i:
                    for s in range(8):
                        lo(s % 4, i * 8 + (ubase + 8 * SC_FIRST + s))
                        scatter(0, i, s)
                for s in range(4):
                    lo(s, ubase + 8 * (SC_FIRST + SC_TURNS) + s)
                scatter_rest(0)
                for s in range(4, 8):
                    lo(s % 4, ubase + 8 * (SC_FIRST + SC_TURNS) + s)
                with dve.Fori(SC_FIRST + SC_TURNS + 1, N_KEYS // 4) as i:
                    for s in range(8):
                        lo(s % 4, i * 8 + (ubase + s))

                vbase = SLAB0["vt", layer]
                lo(0, vbase)
                lo(1, vbase + 1)

                def c_lo(block_, m, buf):
                    dve.wait_ge(s_chi, m + 1)
                    src = at(block_ * T, T) if isinstance(block_, int) else big[:, bass.ds(block_ * T, T)]
                    dve.tensor_tensor(act_lo_t[:, buf, :], src, act_hi_t[:, buf, :].bitcast(F32),
                                      ALU.subtract).then_inc(s_clo, 1)
                m0 = COEFFS * layer
                scatter(1, 0, 0, first=True)
                scatter(1, 0, 1, first=True)
                for b in range(4):
                    c_lo(b, m0 + b, b)
                lo(2, vbase + 2)
                lo(3, vbase + 3)
                scatter(1, 0, 2, first=True)
                scatter(1, 0, 3, first=True)
                dve.wait_ge(s_evac, BLOCK0["u", layer] + N_KEYS)
                for s in range(4, 8):
                    lo(s % 4, vbase + s)
                    c_lo(s, m0 + s, s)
                    scatter(1, 0, s, first=True)
                with dve.Fori(1, SC_TURNS) as i:
                    for s in range(8):
                        lo(s % 4, i * 8 + (vbase + s))
                        c_lo(i * 8 + s, i * 8 + (m0 + s), s)
                        scatter(1, i, s)
                scatter_rest(1)
                with dve.Fori(0, HALF // 8) as i:
                    for s in range(8):
                        lo(s % 4, i * 8 + (vbase + HALF + s))
                        c_lo(i * 8 + s, i * 8 + (m0 + HALF + s), s)
                with dve.Fori(HALF // 4, N_KEYS // 4) as i:
                    for s in range(8):
                        lo(s % 4, i * 8 + (vbase + s))
                        if s < 4:
                            c_lo(i * 4 + s, i * 4 + (m0 + HALF + s), s)
                dve.wait_ge(s_reload, 16 * PIECES * (layer + 1))
                for c in range(4):
                    if c == 2 and layer == 0:
                        lo(0, SLAB0["qk", 1])
                        lo(1, SLAB0["qk", 1] + 1)
                    dve.wait_ge(s_used, vbase + 2 * N_KEYS - (4 if c < 2 else 0))
                    x = at(XT + 1024 * c, 1024)
                    dve.tensor_tensor(x, x, banks(2 * c, 2), ALU.add).then_inc(s_yadd, 1)

            even()
            experts(0)
            odd()
            experts(1)
            norm(4, None)

        @block.tensor
        def _(pe):
            def three(out, wh, wl, xh, xl, start=False, stop=False, **kw):
                pe.matmul(out, wh, xl, start=start, stop=False, **kw)
                pe.matmul(out, wl, xh, start=False, stop=False, **kw)
                return pe.matmul(out, wh, xh, start=False, stop=stop, **kw)

            def half_block(slot, n, b, half, fill=None):
                pe.wait_ge(s_lo, n + 1)
                for k in range(8):
                    kb = 8 * half + k
                    if fill is not None and kb % 2 == 0:
                        pe.wait_ge(s_alo, CHUNKS * fill + kb // 2 + 1)
                    c = slice(P * k, P * (k + 1))
                    ins = three(ps[:, b, 0:T], w_hi[:, slot, c], w_lo[:, slot, c], act_hi_t[:, kb, :],
                                act_lo_t[:, kb, :], start=kb == 0, stop=kb == KB - 1)
                ins.then_inc(s_used, 1)

            def gemm(name, layer, nblocks, fill=None, between=None, strict=False, opening=None):
                n0, b0 = SLAB0[name, layer], BLOCK0[name, layer]

                def blk(i, par, first=False):
                    if first and strict:
                        pe.wait_ge(s_evac, b0)
                    elif not (isinstance(i, int) and b0 + 2 * i + par < 2):
                        pe.wait_ge(s_evac, i * 2 + (b0 + par - 1))
                    for half in range(2):
                        s = 2 * par + half
                        half_block(s, i * 4 + (n0 + s), par, half, fill if first and par == 0 else None)
                if opening:
                    opening()
                else:
                    blk(0, 0, True)
                    blk(0, 1, True)
                if between:
                    between(0)
                with pe.Fori(1, nblocks // 2) as i:
                    blk(i, 0)
                    if between:
                        between(i * 2 - 1, 1)
                    blk(i, 1)
                    if between:
                        between(i * 2, 0)
                if between:
                    between(nblocks - 1)

            def v_groups(layer, ngroups):
                n0 = SLAB0["v", layer]
                for g in range(ngroups):
                    if g >= 2:
                        pe.wait_ge(s_vevac, 4 * layer + 2 * (g - 1))
                    for q in range(8):
                        pe.wait_ge(s_lo, n0 + 8 * g + q + 1)
                        for k in range(2):
                            kb = 2 * q + k
                            c = slice(512 * k, 512 * (k + 1))
                            for tb in range(TB):
                                t = slice(P * tb, P * (tb + 1))
                                out = ps[:, 3 + 2 * (g % 2) + tb, :]
                                pe.matmul(out, act_lo_t[:, kb, t], w_hi[:, q % 4, c], start=kb == 0, stop=False)
                                pe.matmul(out, act_hi_t[:, kb, t], w_lo[:, q % 4, c], start=False, stop=False)
                                ins = pe.matmul(out, act_hi_t[:, kb, t], w_hi[:, q % 4, c], start=False,
                                                stop=kb == KB - 1)
                        ins.then_inc(s_used, 1)

            def norm_sum(k, tiles=range(0)):
                if k:
                    pe.wait_ge(s_acc, k)
                    ins = pe.matmul(ps[:, 2, 0:T], ones[:, :], rstd[:, :], start=True, stop=not tiles)
                for j in tiles:
                    if j % 4 == 0:
                        pe.wait_ge(s_sq, SQ0[k] + j // 4 + 1)
                    ins = pe.matmul(ps[:, 2, 0:T], ones[:, :], at(HT + T * j, T), start=j == 0, stop=j == KB - 1)
                ins.then_inc(s_sum, 1)

            def even():
                pe.wait_ge(s_pool, 1)
                norm_sum(0, range(KB))
                gemm("qk", 0, 8, fill=FILL["h", 0])
                pe.wait_ge(s_pool, POOL_CONSTS)
                pe.wait_ge(s_consts, 16 * N_CONSTS)
                wg = at(E_WG, 16 * WG_W, 16)
                for j in range(KB):
                    ins = pe.matmul(ps[0:WG_W, 7, 0:T], wg[:, j, :], at(HT + T * j, T), start=j == 0, stop=j == KB - 1)
                ins.then_inc(s_gates_ps, 1)
                v_groups(0, 2)
                sel = big[0:4, E_SEL:E_SEL + 1024].rearrange("p (h t) -> p h t", h=4)
                rows = lambda r: big[0:4, E_ROWS + T * r:E_ROWS + T * (r + 1)]

                def scores(h):
                    if h == 0:
                        pe.wait_ge(s_rows, 1)
                        pe.wait_ge(s_vevac, 4)
                        pe.wait_ge(s_evac, BLOCK0["p", 0])
                    if h >= 2:
                        pe.wait_ge(s_dm, h - 1)
                    for o, s, t0 in ((0, 0, 0), (T, P, P)):
                        out = ps[:, 3 + h % 2, o:o + T - t0]
                        pe.matmul(out, sel[:, h, 0:P], rows(2)[:, t0:T], start=True, stop=False)
                        ins = pe.matmul(out, rows(4)[:, s:s + P], sel[:, h, t0:T], start=False, stop=True)
                    ins.then_inc(s_d_ps, 1)
                    if h >= 2:
                        pe.wait_ge(s_s, h - 1)
                    for o, s, t0 in ((0, 0, 0), (T, P, P)):
                        ins = pe.matmul(ps[:, 5 + h % 2, o:o + T - t0], at(E_K + T * h + s, P),
                                        at(E_Q + T * h + t0, T - t0), start=True, stop=True)
                    ins.then_inc(s_s_ps, 1)

                def outputs(h):
                    if h == 0:
                        pe.wait_ge(s_floor, 1)
                    else:
                        pe.wait_ge(s_hn, h)
                    pe.wait_ge(s_s, h + 1)
                    w = at(E_PE + 384 * h, 384)
                    for vt in range(2):
                        v = [at(E_V + 1024 * sb_ + 256 * h + P * vt, P) for sb_ in range(2)]
                        pe.matmul(ps[:, 7, T * vt:T * vt + T], v[0], w[:, 0:T], start=True, stop=True)
                        pe.matmul(ps[:, 7, T * vt + P:T * vt + T], v[1], w[:, T:384], start=False, stop=False,
                                  skip_group_check=True)
                    pe.matmul(ps[:, 2, 0:T], ones[:, :], w[:, 0:T], start=True, stop=True)
                    pe.matmul(ps[:, 2, P:T], ones[:, :], w[:, T:384], start=False, stop=False, skip_group_check=True)
                    pe.matmul(ps[:, 2, T:2 * T], sel[:, h, 0:P], rows(5), start=True, stop=True).then_inc(s_num_ps, 1)

                def pooling(tiles):
                    for j in tiles:
                        g, dt = j // 2, j % 2
                        pe.wait_ge(s_mixed, g + 1)
                        for kc in range(2):
                            ins = pe.matmul(pool_bank(j), at(E_WPOOL + 512 * g + 256 * kc + P * dt, P),
                                            at(E_PT + E_PW * (2 * g + kc) + E_PAD, T), start=kc == 0, stop=kc == 1)
                        ins.then_inc(s_pool_ps, 1)

                def square_sums():
                    pe.wait_ge(s_dm, M_HEADS)
                    for h in range(M_HEADS):
                        pe.wait_ge(s_hsq, h + 1)
                        for vt in range(2):
                            ins = pe.matmul(ps[:, 3 + h // 2, T * (h % 2):T * (h % 2) + T], ones[:, :],
                                            at(E_V + 512 * h + T * vt, T), start=vt == 0, stop=vt == 1)
                        if h % 2:
                            ins.then_inc(s_ssq_ps, 1)

                def blocks(name, beside):
                    b0, n0 = BLOCK0[name, 0], SLAB0[name, 0]
                    for b in range(8):
                        pe.wait_ge(s_evac, b0 + b - 1)
                        for half in range(2):
                            half_block((2 * b + half) % 4, n0 + 2 * b + half, b % 2, half)
                        if b in beside:
                            beside[b]()
                beside = {b: (lambda h=h: scores(h)) for h, b in enumerate(SCORES_AT)}
                beside.update({b: (lambda h=h: outputs(h)) for h, b in enumerate(OUTPUTS_AT)})
                blocks("p", beside)
                blocks("o", {1: square_sums, 4: lambda: pooling(range(4)), 5: lambda: pooling(range(4, 8))})
                pe.wait_ge(s_pool_out, 8)
                gemm("out", 0, 16, fill=FILL["y", 0], strict=True)
                norm_sum(1)

            def odd():
                gemm("qk", 1, 16, fill=FILL["h", 1])
                pe.wait_ge(s_consts, 16 * (N_CONSTS + 2))
                for j in range(KB):
                    ins = pe.matmul(ps[0:G_RANK, 7, 0:T], at(O_WGL + G_RANK * j, G_RANK), at(HT + T * j, T),
                                    start=j == 0, stop=j == KB - 1)
                ins.then_inc(s_gl_ps, 1)

                def gate(r):
                    pe.wait_ge(s_gl, 1)
                    if r:
                        pe.wait_ge(s_bias, 1)
                    for j in range(4 * r, 4 * r + 4):
                        b = 7 if j % 4 < 2 else 2
                        ins = pe.matmul(ps[:, b, T * (j % 2):T * (j % 2) + T],
                                        big[0:G_RANK, O_WGATE + P * j:O_WGATE + P * (j + 1)],
                                        big[0:G_RANK, O_GLT:O_GLT + T], start=True, stop=True)
                    ins.then_inc(s_pre_ps, 1)
                for b in range(3, 7):
                    for o in range(0, 512, P):
                        pe.matmul(ps[:, b, o:o + P], zrow[0:1, :], zrow[0:1, :], start=True, stop=True)

                def group(g):
                    if g == 2:
                        pe.wait_ge(s_ke, 5)
                        for j in range(8):
                            c = T * (j // 2 % 2) + P
                            ins = pe.matmul(ps[:, 3 + j // 4, c:c + P], at(O_KX, 1024, 8)[:, j, :],
                                            at(O_QX, 1024, 8)[:, j, :], start=j % 2 == 0, stop=j % 2 == 1)
                        ins.then_inc(s_att_ps, 1)
                    sb_, n = g // G_PER, G_SUB * (g % G_PER + 1)
                    pe.wait_ge(s_ke, exp_count(g))
                    ke = ke_buf(g)
                    qe = at(O_QE, 2048, 8)
                    for j in range(8):
                        c = T * (j // 2 % 2) + G_SUB * g
                        ins = pe.matmul(ps[0:n, 3 + 2 * sb_ + j // 4, c:c + G_SUB], ke[:, j, 0:n],
                                        qe[:, j, G_SUB * g:G_SUB * (g + 1)], start=j % 2 == 0, stop=j % 2 == 1)
                    ins.then_inc(s_att_ps, 1)
                r0 = SLAB0["r", 1]
                for b in range(KB):
                    pe.wait_ge(s_evac, BLOCK0["r", 1] + b - 1)
                    for half in range(2):
                        half_block((2 * b + half) % 4, r0 + 2 * b + half, b % 2, half)
                    if b < 2:
                        gate(b)
                    if GLA_AT < b <= GLA_AT + 8:
                        group(2 * (b - GLA_AT - 1))
                        group(2 * (b - GLA_AT - 1) + 1)

                def o_head(h):
                    pe.wait_ge(s_vevac, 4 + 2 * (h + 1))
                    pe.wait_ge(s_att, 4)
                    if h:
                        pe.wait_ge(s_o, h)
                    for vt in range(4):
                        b, o = O_BANK + vt // 2, T * (vt % 2)
                        v = [at(O_V + 2048 * sb_ + 512 * h + P * vt, P) for sb_ in range(2)]
                        w = [at(O_ATT + 1024 * sb_ + T * h, T) for sb_ in range(2)]
                        pe.matmul(ps[:, b, o:o + T], v[0], w[0], start=True, stop=True)
                        ins = pe.matmul(ps[:, b, o + P:o + T], v[1], w[1][:, P:T], start=False, stop=False,
                                        skip_group_check=True)
                    ins.then_inc(s_o_ps, 1)

                def o_ssq(h):
                    pe.wait_ge(s_osq, h + 1)
                    if h >= 2:
                        pe.wait_ge(s_hstd, 2 + h - 1)
                    for vt in range(4):
                        ins = pe.matmul(o_sum(h), ones[:, :], at(O_KE + 1024 * h + T * vt, T), start=vt == 0,
                                        stop=vt == 3)
                    ins.then_inc(s_ssq_ps, 1)
                pe.wait_ge(s_evac, BLOCK0["out", 1])
                v0 = SLAB0["v", 1]
                for g in range(G_HEADS):
                    if g >= 2:
                        pe.wait_ge(s_vevac, 4 + 2 * (g - 1))
                    for q in range(8):
                        pe.wait_ge(s_lo, v0 + 8 * g + q + 1)
                        for k in range(2):
                            kb = 2 * q + k
                            c = slice(512 * k, 512 * (k + 1))
                            for tb in range(TB):
                                t = slice(P * tb, P * (tb + 1))
                                out = bank(V_BANKS[g % 2][tb])
                                pe.matmul(out, act_lo_t[:, kb, t], w_hi[:, q % 4, c], start=kb == 0, stop=False)
                                pe.matmul(out, act_hi_t[:, kb, t], w_lo[:, q % 4, c], start=False, stop=False)
                                ins = pe.matmul(out, act_hi_t[:, kb, t], w_hi[:, q % 4, c], start=False,
                                                stop=kb == KB - 1)
                        ins.then_inc(s_used, 1)
                        if g and q == 1:
                            o_head(g - 1)
                        if g and q == 3:
                            o_ssq(g - 1)

                def opening():
                    n0 = SLAB0["out", 1]

                    def part(slot, b, kbs):
                        pe.wait_ge(s_lo, n0 + slot + 1)
                        for kb in kbs:
                            if kb % 2 == 0:
                                pe.wait_ge(s_alo, CHUNKS * FILL["y", 1] + kb // 2 + 1)
                            c = slice(P * (kb % 8), P * (kb % 8 + 1))
                            ins = three(ps[:, b, 0:T], w_hi[:, slot, c], w_lo[:, slot, c], act_hi_t[:, kb, :],
                                        act_lo_t[:, kb, :], start=kb == 0, stop=kb == KB - 1)
                        return ins
                    part(0, 0, range(8)).then_inc(s_used, 1)
                    o_head(G_HEADS - 1)
                    part(1, 0, range(8, 12))
                    o_ssq(G_HEADS - 1)
                    part(2, 1, range(8))
                    part(3, 1, range(8, 12))
                    part(1, 0, range(12, 16)).then_inc(s_used, 2)
                    part(3, 1, range(12, 16)).then_inc(s_used, 1)
                gemm("out", 1, 16, opening=opening)
                norm_sum(3)

            def experts(layer):
                pe.wait_ge(s_keys, 16 * (layer + 1))

                def key_scores(q, par=None):
                    par = q % 2 if par is None else par
                    pe.wait_ge(s_evac, q + (BLOCK0["wq", layer] + 1))
                    if not (isinstance(q, int) and q < 2):
                        pe.wait_ge(s_sc, q + 16 * layer)
                    rhs = at(K_KEYS + P * q, P) if isinstance(q, int) else big[:, bass.ds(q * P + K_KEYS, P)]
                    for tb in range(TB):
                        ins = pe.matmul(ps[:, 2 + par, P * tb:P * (tb + 1)], at(K_QS + T * par + P * tb, P), rhs,
                                        start=True, stop=True)
                    ins.then_inc(s_sc_ps, 1)
                gemm("wq", layer, 16, fill=FILL["k", layer], between=key_scores, strict=True)

                ub, u0_ = BLOCK0["u", layer], SLAB0["u", layer]

                def u_turn(i, after=None):
                    for b in range(4):
                        pe.wait_ge(s_evac, i * 4 + (ub + b - 1))
                        for half in range(2):
                            s = 2 * b + half
                            half_block(s % 4, i * 8 + (u0_ + s), b % 2, half)
                            if after:
                                after(s)

                def slots(s):
                    if s != 3:
                        return
                    pe.wait_ge(s_slots, layer + 1)
                    for c in range(2):
                        for tb in range(TB):
                            pe.transpose(ps[:, 3, T * c + P * tb:T * c + P * (tb + 1)],
                                         e12[:, c, HEADS * tb:HEADS * (tb + 1), :].rearrange("p h k -> p (h k)"),
                                         ident[:, :])
                    for tb in range(TB):
                        ins = pe.transpose(ps[:, 4, P * tb:P * (tb + 1)],
                                           cv[:, HEADS * tb:HEADS * (tb + 1), :].rearrange("p h k -> p (h k)"),
                                           ident[:, :])
                    ins.then_inc(s_jt_ps, 1)

                def scatter(part, i, s):
                    done = sc_turns(layer, part)
                    if s % 2 == 0:
                        pe.wait_ge(s_g, i * 4 + (done * 4 + s // 2 + 1))
                    pe.wait_ge(s_hot2, i * 8 + (done * 8 + s + 1))
                    pe.wait_ge(s_hot1, i * 8 + (done * 8 + s + 1))
                    for x in range(4):
                        t = 4 * (s % 2) + x
                        for c in range(WPARTS):
                            ins = pe.matmul(ps[:, 4 + s // 2, HALF * t:HALF * (t + 1)], hot2[:, t, :],
                                            hot1[:, t, c, :], start=c == 0, stop=c == WPARTS - 1)
                    ins.then_inc(s_hot_free, 1)

                with pe.Fori(0, SC_FIRST - 1) as i:
                    u_turn(i)
                u_turn(SC_FIRST - 1, slots)
                with pe.Fori(0, SC_TURNS) as i:
                    u_turn(i + SC_FIRST, lambda s: scatter(0, i, s))
                with pe.Fori(SC_FIRST + SC_TURNS, N_KEYS // 4) as i:
                    u_turn(i)

                def open_banks(first):
                    for b in range(first, first + 4):
                        pe.matmul(ps[:, b, 0:2], zrow[0:1, :], zrow[0:1, 0:2], start=True, stop=False,
                                  skip_group_check=True)
                v0, m0 = SLAB0["vt", layer], COEFFS * layer

                def v_slab(i, s, half, buf):
                    pe.wait_ge(s_lo, i * 8 + (v0 + s + 1))
                    for k in range(8):
                        j = 8 * half + k
                        c = slice(P * k, P * (k + 1))
                        ins = three(ps[:, j // 2, T * (j % 2):T * (j % 2) + T], w_hi[:, s % 4, c],
                                    w_lo[:, s % 4, c], act_hi_t[:, buf, :], act_lo_t[:, buf, :],
                                    skip_group_check=True)
                    ins.then_inc(s_used, 1)
                pe.wait_ge(s_evac, ub + N_KEYS)
                open_banks(0)
                with pe.Fori(0, SC_TURNS) as i:
                    for s in range(8):
                        pe.wait_ge(s_clo, i * 8 + (m0 + s + 1))
                        v_slab(i, s, 0, s)
                        scatter(1, i, s)
                pe.wait_ge(s_g, SC_TURNS * 8 * (layer + 1) + 4)
                open_banks(4)
                with pe.Fori(SC_TURNS, 2 * SC_TURNS) as i:
                    for s in range(8):
                        pe.wait_ge(s_clo, i * 8 + (m0 + s + 1))
                        v_slab(i, s, 1, s)

                def rest(i):
                    for s in range(8):
                        if s < 4:
                            pe.wait_ge(s_clo, i * 4 + (m0 + HALF + s + 1))
                        v_slab(i, s, s // 4, s % 4)
                with pe.Fori(HALF // 4, N_KEYS // 4) as i:
                    rest(i)
                pe.wait_ge(s_yadd, 4 * layer + 2)
                norm_sum(2 * layer + 2, range(8, KB))

            even()
            experts(0)
            odd()
            experts(1)


INPUTS = ["xT", "dense0", "dense1", "u0", "u1", "v_tab", "keys", "gains", "gates_in", "w_pool", "inv_count",
          "w_glow", "w_gate"]


def lay_out(x, e_norm, e_w_in, e_b_igate, e_b_fgate, e_head_gain, e_w_pool, e_pool_scale, e_w_out,
            o_norm, o_w_in, o_w_gate, o_b_gate, o_head_gain, o_w_out,
            f_norm, f_w_q, f_sub_keys, f_u, f_v, final_norm):
    def blocks(w):
        n = w.shape[1] // P
        return w.reshape(2, 8, P, n, P).transpose(3, 0, 2, 1, 4).reshape(2 * n, P, SLAB)

    def groups(w):
        n = w.shape[1] // 512
        return w.reshape(8, 2, P, n, 512).transpose(3, 0, 2, 1, 4).reshape(8 * n, P, SLAB)

    def table(u):
        return u.reshape(N_KEYS, P, 2, 8, P).transpose(0, 2, 4, 3, 1).reshape(2 * N_KEYS, P, SLAB)

    def column(g):
        return g.reshape(-1, P).T

    a = np.ascontiguousarray
    we, wo = e_w_in[0], o_w_in[0]
    dense0 = np.concatenate([blocks(we[:, 0:1024]), groups(we[:, 1024:2048]), blocks(we[:, 3080:4104]),
                             blocks(we[:, 2048:3072]), blocks(np.concatenate([e_w_out[0][M_WIDTH:], e_w_out[0][:M_WIDTH]])),
                             blocks(f_w_q[0])])
    dense1 = np.concatenate([blocks(wo[:, 0:2048]), blocks(wo[:, 4096:6144]), groups(wo[:, 2048:4096]),
                             blocks(o_w_out[0]), blocks(f_w_q[1])])
    gains = np.concatenate([column(g) for g in (e_norm[0], f_norm[0], o_norm[0], f_norm[1], final_norm,
                                                e_head_gain[0], e_pool_scale[0], o_head_gain[0], o_b_gate[0])], 1)
    gains = np.concatenate([gains, np.zeros((P, P - gains.shape[1]), gains.dtype)], 1)
    gates = np.zeros((P, KB + 1, 8), we.dtype)
    gates[:, 0:KB, :] = we[:, 3072:3080].reshape(KB, P, 8).transpose(1, 0, 2)
    gates[0:4, KB, 0] = e_b_igate[0]
    gates[0:4, KB, 1] = e_b_fgate[0]
    inv = np.stack([1.0 / np.minimum(np.arange(1, T + 1), w) for w in POOL_WINDOWS]).astype(np.float32)
    return {
        "xT": a(x[0].T.reshape(KB, P, T).transpose(1, 0, 2)),
        "dense0": a(dense0), "dense1": a(dense1), "u0": a(table(f_u[0])), "u1": a(table(f_u[1])),
        "v_tab": a(f_v), "keys": a(f_sub_keys.transpose(0, 4, 1, 2, 3).reshape(2, P, 2048)),
        "gains": a(gains), "gates_in": gates,
        "w_pool": a(e_w_pool[0].reshape(4, 2, P, POOL_GROUP).transpose(2, 0, 1, 3).reshape(P, 2048)),
        "inv_count": a(np.broadcast_to(inv.reshape(1, 1024), (P, 1024))),
        "w_glow": a(wo[:, 6144:6160].reshape(KB, P, G_RANK).transpose(1, 0, 2).reshape(P, KB * G_RANK)),
        "w_gate": a(o_w_gate[0]),
    }


def kernel(**inputs):
    import concourse.bacc as bacc
    from concourse.bass_utils import run_bass_kernel_spmd as run
    arrays = lay_out(**{k: np.asarray(v) for k, v in inputs.items()})
    nc = bacc.Bacc("TRN2", target_bir_lowering=False, num_devices=1)
    args = [nc.dram_tensor(f"in_{n}", arrays[n].shape, F32, kind="ExternalInput").ap() for n in INPUTS]
    out = nc.dram_tensor("out_0", (P, KB, T), F32, kind="ExternalOutput").ap()
    decoder_kernel(nc, *args, out)
    r = run(nc, [{f"in_{n}": arrays[n] for n in INPUTS}], core_ids=[0])
    got = np.asarray(r.results[0]["out_0"])
    return np.ascontiguousarray(got.transpose(2, 1, 0).reshape(1, T, D))
```
